# Optimizing a Trainium2 kernel written in Bass

```python
import jax, jax.numpy as jnp
from jax import lax
import numpy as np

D_MODEL = 1024
BATCH = 1
SEQ = 256
DEPTH = 2

EPS = 1e-6
GLA_HEADS = 4
GLA_DK = 128
GLA_DV = 256
GLA_GATE_RANK = 16
GLA_GATE_TAU = 16.0
GLA_CHUNK = 64
GLA_PROJ = GLA_HEADS * (2 * GLA_DK + 2 * GLA_DV) + GLA_GATE_RANK
SWA_HEADS = 16
SWA_KV_HEADS = 4
SWA_GROUP = SWA_HEADS // SWA_KV_HEADS
SWA_HEAD_DIM = 64
SWA_WINDOW = 128
SWA_BLOCK = 128
ROT_DIM = SWA_HEAD_DIM // 4
ROPE_THETA = 500000.0
PEER_HEADS = 8
PEER_N_KEYS = 128
PEER_EXPERTS = PEER_N_KEYS * PEER_N_KEYS
PEER_TOPK = 16
PEER_QDIM = 256
PEER_BLOCK = 128


def rmsnorm(x, g):
    x32 = x.astype(jnp.float32)
    y = x32 * lax.rsqrt(jnp.mean(x32 * x32, axis=-1, keepdims=True) + EPS)
    return (y * g.astype(jnp.float32)).astype(x.dtype)

def modulate(x, g, shift, scale):
    return rmsnorm(x, g) * (1.0 + scale[:, None, :]) + shift[:, None, :]

def rope_tables(positions):
    inv = ROPE_THETA ** (-jnp.arange(0, ROT_DIM, 2, dtype=jnp.float32) / ROT_DIM)
    ang = positions.astype(jnp.float32)[..., None] * inv
    return jnp.cos(ang), jnp.sin(ang)

def apply_partial_rope(x, cos, sin):
    half = ROT_DIM // 2
    xr = x[..., :ROT_DIM].astype(jnp.float32)
    x1, x2 = xr[..., :half], xr[..., half:]
    c = cos[:, :, None, :]
    s = sin[:, :, None, :]
    rot = jnp.concatenate([x1 * c - x2 * s, x2 * c + x1 * s], axis=-1).astype(x.dtype)
    return jnp.concatenate([rot, x[..., ROT_DIM:]], axis=-1)

def gla_mixer(h, w_in, w_g2, b_g2, norm_g, w_out):
    bsz, s_len, _ = h.shape
    H, dk, dv, C = GLA_HEADS, GLA_DK, GLA_DV, GLA_CHUNK
    n_c = s_len // C
    proj = h @ w_in
    q, k, v, og, gl = jnp.split(proj, [H * dk, 2 * H * dk, 2 * H * dk + H * dv, 2 * H * dk + 2 * H * dv], axis=-1)
    log_a = jax.nn.log_sigmoid((gl @ w_g2 + b_g2).astype(jnp.float32)) / GLA_GATE_TAU
    shp = (bsz, n_c, C, H, dk)
    q = q.reshape(shp).astype(jnp.float32) * (dk ** -0.5)
    k = k.reshape(shp).astype(jnp.float32)
    v = v.reshape(bsz, n_c, C, H, dv).astype(jnp.float32)
    b = jnp.cumsum(log_a.reshape(shp), axis=2)
    b_last = b[:, :, -1:]
    q_t = q * jnp.exp(b)
    k_t = k * jnp.exp(-b)
    k_dec = k * jnp.exp(b_last - b)
    scores = jnp.einsum('bnchd,bnmhd->bnhcm', q_t, k_t)
    tri = jnp.tril(jnp.ones((C, C), dtype=bool))
    scores = jnp.where(tri, scores, 0.0)
    o_intra = jnp.einsum('bnhcm,bnmhe->bnche', scores, v)
    dec = jnp.exp(b_last[:, :, 0])

    def step(state, inp):
        q_n, k_n, v_n, d_n = inp
        o_n = jnp.einsum('bchd,bhde->bche', q_n, state)
        state = d_n[..., None] * state + jnp.einsum('bchd,bche->bhde', k_n, v_n)
        return state, o_n

    xs = (jnp.moveaxis(q_t, 1, 0), jnp.moveaxis(k_dec, 1, 0), jnp.moveaxis(v, 1, 0), jnp.moveaxis(dec, 1, 0))
    _, o_inter = lax.scan(step, jnp.zeros((bsz, H, dk, dv), jnp.float32), xs)
    o = (o_intra + jnp.moveaxis(o_inter, 0, 1)).reshape(bsz, s_len, H, dv)
    o = rmsnorm(o, norm_g) * jax.nn.silu(og.reshape(bsz, s_len, H, dv).astype(jnp.float32))
    return (o.reshape(bsz, s_len, H * dv) @ w_out).astype(h.dtype)

def shared_kv(h, kv_w, cos, sin):
    bsz, s_len, _ = h.shape
    kv = h @ kv_w
    k, v = jnp.split(kv, 2, axis=-1)
    k = apply_partial_rope(k.reshape(bsz, s_len, SWA_KV_HEADS, SWA_HEAD_DIM), cos, sin)
    v = v.reshape(bsz, s_len, SWA_KV_HEADS, SWA_HEAD_DIM)
    return k, v

def swa_sink_attention(h, w_q, sinks, w_out, k, v, cos, sin):
    bsz, s_len, _ = h.shape
    P = SWA_BLOCK
    n_b = s_len // P
    q = apply_partial_rope((h @ w_q).reshape(bsz, s_len, SWA_HEADS, SWA_HEAD_DIM), cos, sin)
    q = q.reshape(bsz, n_b, P, SWA_KV_HEADS, SWA_GROUP, SWA_HEAD_DIM)

    def band(t):
        prev = jnp.pad(t, ((0, 0), (P, 0), (0, 0), (0, 0)))[:, :s_len]
        shp = (bsz, n_b, P, SWA_KV_HEADS, SWA_HEAD_DIM)
        return jnp.concatenate([prev.reshape(shp), t.reshape(shp)], axis=2)

    k_band, v_band = band(k), band(v)
    s = jnp.einsum('bnqkgd,bnmkd->bnkgqm', q, k_band).astype(jnp.float32) * (SWA_HEAD_DIM ** -0.5)
    qi = jnp.arange(P)[:, None]
    mi = jnp.arange(2 * P)[None, :]
    rel = qi + P - mi
    in_window = (rel >= 0) & (rel < SWA_WINDOW)
    key_pos = jnp.arange(n_b)[:, None, None] * P - P + mi[None]
    mask = in_window[None] & (key_pos >= 0)
    s = jnp.where(mask[None, :, None, None], s, -jnp.inf)
    sink = sinks.astype(jnp.float32).reshape(SWA_KV_HEADS, SWA_GROUP)[None, None, :, :, None, None]
    m = jnp.maximum(jnp.max(s, axis=-1, keepdims=True), sink)
    p = jnp.exp(s - m)
    probs = p / (jnp.sum(p, axis=-1, keepdims=True) + jnp.exp(sink - m))
    o = jnp.einsum('bnkgqm,bnmkd->bnqkgd', probs, v_band.astype(jnp.float32))
    return (o.reshape(bsz, s_len, SWA_HEADS * SWA_HEAD_DIM) @ w_out).astype(h.dtype)

def peer(h, w_q, subkeys, u_tab, v_tab):
    bsz, s_len, d = h.shape
    half = PEER_QDIM // 2
    tokens = h.reshape(-1, PEER_BLOCK, d)

    def block(xb):
        q = (xb @ w_q).reshape(PEER_BLOCK, PEER_HEADS, PEER_QDIM)
        s1 = jnp.einsum('phd,nd->phn', q[..., :half], subkeys[0])
        s2 = jnp.einsum('phd,nd->phn', q[..., half:], subkeys[1])
        v1, i1 = lax.top_k(s1, PEER_TOPK)
        v2, i2 = lax.top_k(s2, PEER_TOPK)
        cand = (v1[..., :, None] + v2[..., None, :]).reshape(PEER_BLOCK, PEER_HEADS, PEER_TOPK * PEER_TOPK)
        cs, ci = lax.top_k(cand, PEER_TOPK)
        e = (jnp.take_along_axis(i1, ci // PEER_TOPK, axis=-1) * PEER_N_KEYS
             + jnp.take_along_axis(i2, ci % PEER_TOPK, axis=-1))
        g = jax.nn.softmax(cs.astype(jnp.float32), axis=-1)
        u = u_tab[e]
        a = jax.nn.gelu(jnp.einsum('pd,phkd->phk', xb, u).astype(jnp.float32), approximate=False)
        return jnp.einsum('phk,phkd->pd', g * a, v_tab[e].astype(jnp.float32)).astype(xb.dtype)

    return lax.map(block, tokens).reshape(bsz, s_len, d)

def first_inputs(seed: int = 0) -> dict:
    key = jax.random.key(seed)
    ks = jax.random.split(key, 24)
    n_a = DEPTH // 2
    n_b = DEPTH - n_a
    D = D_MODEL
    f32 = jnp.float32

    def nrm(k, shape, scale):
        return jax.random.normal(k, shape, f32) * scale

    positions = (jax.random.randint(ks[2], (BATCH, 1), 0, 4096, dtype=jnp.int32)
                 + jnp.arange(SEQ, dtype=jnp.int32)[None, :])
    return {
        "x": nrm(ks[0], (BATCH, SEQ, D), 1.0),
        "c": nrm(ks[1], (BATCH, D), 1.0),
        "positions": positions,
        "mod_w": nrm(ks[3], (DEPTH, D, 6 * D), 0.5 * D ** -0.5),
        "mod_b": nrm(ks[4], (DEPTH, 6 * D), 0.02),
        "norm_g": 1.0 + nrm(ks[5], (DEPTH, 2, D), 0.02),
        "gla_w_in": nrm(ks[6], (n_a, D, GLA_PROJ), D ** -0.5),
        "gla_w_g2": nrm(ks[7], (n_a, GLA_GATE_RANK, GLA_HEADS * GLA_DK), GLA_GATE_RANK ** -0.5),
        "gla_b_g2": nrm(ks[8], (n_a, GLA_HEADS * GLA_DK), 0.1),
        "gla_norm_g": 1.0 + nrm(ks[9], (n_a, GLA_DV), 0.02),
        "gla_w_out": nrm(ks[10], (n_a, GLA_HEADS * GLA_DV, D), (GLA_HEADS * GLA_DV) ** -0.5),
        "kv_mod_w": nrm(ks[11], (D, 2 * D), 0.5 * D ** -0.5),
        "kv_mod_b": nrm(ks[12], (2 * D,), 0.02),
        "kv_norm_g": 1.0 + nrm(ks[13], (D,), 0.02),
        "kv_w": nrm(ks[14], (D, 2 * SWA_KV_HEADS * SWA_HEAD_DIM), D ** -0.5),
        "swa_w_q": nrm(ks[15], (n_b, D, SWA_HEADS * SWA_HEAD_DIM), D ** -0.5),
        "swa_sinks": nrm(ks[16], (n_b, SWA_HEADS), 0.5),
        "swa_w_out": nrm(ks[17], (n_b, SWA_HEADS * SWA_HEAD_DIM, D), (SWA_HEADS * SWA_HEAD_DIM) ** -0.5),
        "peer_w_q": nrm(ks[18], (DEPTH, D, PEER_HEADS * PEER_QDIM), D ** -0.5),
        "peer_subkeys": nrm(ks[19], (DEPTH, 2, PEER_N_KEYS, PEER_QDIM // 2), (PEER_QDIM // 2) ** -0.5),
        "peer_u": nrm(ks[20], (DEPTH, PEER_EXPERTS, D), D ** -0.5),
        "peer_v": nrm(ks[21], (DEPTH, PEER_EXPERTS, D), PEER_HEADS ** -0.5),
        "final_norm_g": 1.0 + nrm(ks[22], (D,), 0.02),
    }

def first_block(x, c, positions, mod_w, mod_b, norm_g, gla_w_in, gla_w_g2, gla_b_g2, gla_norm_g,
              gla_w_out, kv_mod_w, kv_mod_b, kv_norm_g, kv_w, swa_w_q, swa_sinks, swa_w_out,
              peer_w_q, peer_subkeys, peer_u, peer_v, final_norm_g):
    n_a = DEPTH // 2
    cos, sin = rope_tables(positions)
    c_act = jax.nn.silu(c)
    k_sh, v_sh = None, None
    for l in range(DEPTH):
        mod = c_act @ mod_w[l] + mod_b[l]
        sh1, sc1, g1, sh2, sc2, g2 = jnp.split(mod, 6, axis=-1)
        h = modulate(x, norm_g[l, 0], sh1, sc1)
        if l < n_a:
            y = gla_mixer(h, gla_w_in[l], gla_w_g2[l], gla_b_g2[l], gla_norm_g[l], gla_w_out[l])
        else:
            j = l - n_a
            y = swa_sink_attention(h, swa_w_q[j], swa_sinks[j], swa_w_out[j], k_sh, v_sh, cos, sin)
        x = x + (g1[:, None, :] * y).astype(x.dtype)
        h = modulate(x, norm_g[l, 1], sh2, sc2)
        y = peer(h, peer_w_q[l], peer_subkeys[l], peer_u[l], peer_v[l])
        x = x + (g2[:, None, :] * y).astype(x.dtype)
        if l == n_a - 1:
            kv_mod = c_act @ kv_mod_w + kv_mod_b
            kv_shift, kv_scale = jnp.split(kv_mod, 2, axis=-1)
            k_sh, v_sh = shared_kv(modulate(x, kv_norm_g, kv_shift, kv_scale), kv_w, cos, sin)
    return rmsnorm(x, final_norm_g)


DEPTH_2 = 1

RET_HEADS = 4
RET_DK = 256
RET_DV = 256
RET_CHUNK = 128
MLA_HEADS = 8
MLA_NOPE = 128
MLA_ROPE = 64
MLA_V = 128
MLA_Q_LORA = 384
MLA_KV_LORA = 256
ATTN_BLOCK = 128
ROPE_THETA_2 = 10000.0
N_GROUPS = 4
EXPERTS_PER_GROUP = 8
TOP_K = 2
D_EXPERT = 256

RET_QK_W = RET_HEADS * RET_DK
RET_V_W = RET_HEADS * RET_DV
MLA_V_W = MLA_HEADS * MLA_V
SPLITS = [RET_QK_W, RET_QK_W, RET_V_W, RET_V_W, MLA_Q_LORA, MLA_KV_LORA, MLA_ROPE, D_MODEL, D_MODEL]
IN_W = sum(SPLITS)


def rmsnorm_2(x, g):
    xf = x.astype(jnp.float32)
    y = xf * lax.rsqrt(jnp.mean(xf * xf, axis=-1, keepdims=True) + EPS)
    return (y * g.astype(jnp.float32)).astype(x.dtype)

def modulate_2(x, shift, scale):
    return x * (1.0 + scale) + shift

def rope_tables_2(pos, dim):
    inv = ROPE_THETA_2 ** (-jnp.arange(0, dim, 2, dtype=jnp.float32) / dim)
    ang = pos[:, None] * inv[None, :]
    return jnp.cos(ang), jnp.sin(ang)

def apply_rope(x, cos, sin):
    x1, x2 = jnp.split(x.astype(jnp.float32), 2, axis=-1)
    cos = cos[None, :, None, :]
    sin = sin[None, :, None, :]
    return jnp.concatenate([x1 * cos - x2 * sin, x2 * cos + x1 * sin], axis=-1).astype(x.dtype)

def retention(q, k, v):
    b, s, h, dk = q.shape
    dv = v.shape[-1]
    c = RET_CHUNK
    n = s // c
    log_gamma = jnp.log1p(-jnp.exp2(-5.0 - jnp.arange(h, dtype=jnp.float32)))
    idx = jnp.arange(c, dtype=jnp.float32)
    rel = idx[:, None] - idx[None, :]
    decay_in = jnp.where(rel[None] >= 0, jnp.exp(log_gamma[:, None, None] * jnp.maximum(rel, 0.0)[None]), 0.0)
    xi = jnp.exp(log_gamma[:, None] * (idx[None, :] + 1.0))
    zeta = jnp.exp(log_gamma[:, None] * (c - 1.0 - idx[None, :]))
    chunk_decay = jnp.exp(log_gamma * c)

    def to_chunks(t):
        return t.astype(jnp.float32).reshape(b, n, c, h, t.shape[-1]).transpose(1, 0, 2, 3, 4)

    qc = to_chunks(q)
    kc = to_chunks(k) * (dk ** -0.5)
    vc = to_chunks(v)

    def step(state, inp):
        qi, ki, vi = inp
        scores = jnp.einsum('bihd,bjhd->bhij', qi, ki) * decay_in[None]
        y = jnp.einsum('bhij,bjhe->bihe', scores, vi) + jnp.einsum('bihd,hi,bhde->bihe', qi, xi, state)
        state = state * chunk_decay[None, :, None, None] + jnp.einsum('bjhd,hj,bjhe->bhde', ki, zeta, vi)
        return state, y

    state0 = jnp.zeros((b, h, dk, dv), jnp.float32)
    _, ys = lax.scan(step, state0, (qc, kc, vc))
    return ys.transpose(1, 0, 2, 3, 4).reshape(b, s, h, dv)

def head_norm(y):
    mu = jnp.mean(y, axis=-1, keepdims=True)
    var = jnp.mean(jnp.square(y - mu), axis=-1, keepdims=True)
    return (y - mu) * lax.rsqrt(var + EPS)

def mla(c_q, c_kv, k_pe, q_norm, kv_norm, w_uq, w_ukv, cos, sin):
    b, s, _ = c_q.shape
    q = (rmsnorm_2(c_q, q_norm) @ w_uq).reshape(b, s, MLA_HEADS, MLA_NOPE + MLA_ROPE)
    q_nope, q_pe = q[..., :MLA_NOPE], q[..., MLA_NOPE:]
    q_pe = apply_rope(q_pe, cos, sin)
    kv = (rmsnorm_2(c_kv, kv_norm) @ w_ukv).reshape(b, s, MLA_HEADS, MLA_NOPE + MLA_V)
    k_nope, v = kv[..., :MLA_NOPE], kv[..., MLA_NOPE:]
    k_pe = apply_rope(k_pe[:, :, None, :], cos, sin)[:, :, 0, :]
    scale = (MLA_NOPE + MLA_ROPE) ** -0.5
    outs = []
    for blk in range(s // ATTN_BLOCK):
        lo = blk * ATTN_BLOCK
        hi = lo + ATTN_BLOCK
        scores = (jnp.einsum('bqhd,bkhd->bhqk', q_nope[:, lo:hi], k_nope[:, :hi])
                  + jnp.einsum('bqhr,bkr->bhqk', q_pe[:, lo:hi], k_pe[:, :hi])).astype(jnp.float32) * scale
        mask = (lo + jnp.arange(ATTN_BLOCK))[:, None] >= jnp.arange(hi)[None, :]
        p = jax.nn.softmax(jnp.where(mask, scores, -jnp.inf), axis=-1).astype(v.dtype)
        outs.append(jnp.einsum('bhqk,bkhd->bqhd', p, v[:, :hi]))
    return jnp.concatenate(outs, axis=1).reshape(b, s, MLA_V_W)

def token_mixer(u, w_in, w_ret_o, q_norm, kv_norm, w_uq, w_ukv, w_mla_o, w_out, ret_rope, mla_rope):
    b, s, _ = u.shape
    proj = u @ w_in
    offs = np.cumsum(SPLITS)[:-1].tolist()
    rq, rk, rv, rg, c_q, c_kv, k_pe, gate_ret, gate_mla = jnp.split(proj, offs, axis=-1)
    rq = apply_rope(rq.reshape(b, s, RET_HEADS, RET_DK), *ret_rope)
    rk = apply_rope(rk.reshape(b, s, RET_HEADS, RET_DK), *ret_rope)
    rv = rv.reshape(b, s, RET_HEADS, RET_DV)
    y_ret = head_norm(retention(rq, rk, rv)).reshape(b, s, RET_V_W).astype(u.dtype)
    y_ret = (jax.nn.silu(rg) * y_ret) @ w_ret_o
    y_mla = mla(c_q, c_kv, k_pe, q_norm, kv_norm, w_uq, w_ukv, *mla_rope) @ w_mla_o
    merged = jax.nn.sigmoid(gate_ret) * y_ret + jax.nn.sigmoid(gate_mla) * y_mla
    return merged @ w_out

def hier_moe(u, w_grp, b_grp, w_exp, b_exp, w1, w3, w2):
    b, s, d = u.shape
    t = u.reshape(-1, d)
    n_tok = t.shape[0]
    grp_logits = (t @ w_grp).astype(jnp.float32) + b_grp.astype(jnp.float32)
    grp_prob = jax.nn.softmax(grp_logits, axis=-1)
    _, g_sel = lax.top_k(grp_logits, 1)
    p_grp = jnp.take_along_axis(grp_prob, g_sel, axis=-1)
    exp_logits = ((t @ w_exp).astype(jnp.float32) + b_exp.astype(jnp.float32)).reshape(n_tok, N_GROUPS, EXPERTS_PER_GROUP)
    in_grp = jnp.take_along_axis(exp_logits, g_sel[:, :, None], axis=1)[:, 0]
    top_val, top_idx = lax.top_k(in_grp, TOP_K)
    top_w = jax.nn.softmax(top_val, axis=-1) * p_grp
    exp_w = jnp.sum(jax.nn.one_hot(top_idx, EXPERTS_PER_GROUP, dtype=jnp.float32) * top_w[..., None], axis=1)
    gate = jax.nn.one_hot(g_sel[:, 0], N_GROUPS, dtype=jnp.float32)[:, :, None] * exp_w[:, None, :]
    out = jnp.zeros_like(t)
    for gi in range(N_GROUPS):
        hid = jax.nn.silu(jnp.einsum('td,edf->tef', t, w1[gi])) * jnp.einsum('td,edf->tef', t, w3[gi])
        hid = hid * gate[:, gi, :, None].astype(hid.dtype)
        out = out + jnp.einsum('tef,efd->td', hid, w2[gi])
    return out.reshape(b, s, d)

def second_inputs(seed: int = 0) -> dict:
    key = jax.random.key(seed)
    ks = jax.random.split(key, 24)
    L = DEPTH_2
    G, E, F = N_GROUPS, EXPERTS_PER_GROUP, D_EXPERT

    def nrm(k, shape, fan_in, scale=1.0):
        return jax.random.normal(k, shape, jnp.float32) * (scale * fan_in ** -0.5)

    def gain(k, shape):
        return 1.0 + 0.02 * jax.random.normal(k, shape, jnp.float32)

    return {
        "x": jax.random.normal(ks[0], (BATCH, SEQ, D_MODEL), jnp.float32),
        "c": jax.random.normal(ks[1], (BATCH, D_MODEL), jnp.float32),
        "w_ada": nrm(ks[2], (L, D_MODEL, 6 * D_MODEL), D_MODEL, 0.5),
        "b_ada": 0.02 * jax.random.normal(ks[3], (L, 6 * D_MODEL), jnp.float32),
        "norm1": gain(ks[4], (L, D_MODEL)),
        "norm2": gain(ks[5], (L, D_MODEL)),
        "w_in": nrm(ks[6], (L, D_MODEL, IN_W), D_MODEL),
        "w_ret_o": nrm(ks[7], (L, RET_V_W, D_MODEL), RET_V_W),
        "q_norm": gain(ks[8], (L, MLA_Q_LORA)),
        "kv_norm": gain(ks[9], (L, MLA_KV_LORA)),
        "w_uq": nrm(ks[10], (L, MLA_Q_LORA, MLA_HEADS * (MLA_NOPE + MLA_ROPE)), MLA_Q_LORA),
        "w_ukv": nrm(ks[11], (L, MLA_KV_LORA, MLA_HEADS * (MLA_NOPE + MLA_V)), MLA_KV_LORA),
        "w_mla_o": nrm(ks[12], (L, MLA_V_W, D_MODEL), MLA_V_W),
        "w_out": nrm(ks[13], (L, D_MODEL, D_MODEL), D_MODEL),
        "w_grp": nrm(ks[14], (L, D_MODEL, G), D_MODEL),
        "b_grp": 0.01 * jax.random.normal(ks[15], (L, G), jnp.float32),
        "w_exp": nrm(ks[16], (L, D_MODEL, G * E), D_MODEL),
        "b_exp": 0.01 * jax.random.normal(ks[17], (L, G * E), jnp.float32),
        "w1": nrm(ks[18], (L, G, E, D_MODEL, F), D_MODEL),
        "w3": nrm(ks[19], (L, G, E, D_MODEL, F), D_MODEL),
        "w2": nrm(ks[20], (L, G, E, F, D_MODEL), F),
        "final_norm": gain(ks[21], (D_MODEL,)),
    }

def second_block(x, c, w_ada, b_ada, norm1, norm2, w_in, w_ret_o, q_norm, kv_norm, w_uq, w_ukv, w_mla_o, w_out,
              w_grp, b_grp, w_exp, b_exp, w1, w3, w2, final_norm):
    s = x.shape[1]
    pos = jnp.arange(s, dtype=jnp.float32)
    ret_rope = rope_tables_2(pos, RET_DK)
    mla_rope = rope_tables_2(pos, MLA_ROPE)
    c_act = jax.nn.silu(c)
    h = x
    for l in range(DEPTH_2):
        mod = (c_act @ w_ada[l] + b_ada[l])[:, None, :]
        sh1, sc1, g1, sh2, sc2, g2 = jnp.split(mod, 6, axis=-1)
        u = modulate_2(rmsnorm_2(h, norm1[l]), sh1, sc1)
        h = h + g1 * token_mixer(u, w_in[l], w_ret_o[l], q_norm[l], kv_norm[l], w_uq[l], w_ukv[l],
                                 w_mla_o[l], w_out[l], ret_rope, mla_rope)
        u = modulate_2(rmsnorm_2(h, norm2[l]), sh2, sc2)
        h = h + g2 * hier_moe(u, w_grp[l], b_grp[l], w_exp[l], b_exp[l], w1[l], w3[l], w2[l])
    return rmsnorm_2(h, final_norm)


def setup_inputs(seed=0):
    out = dict(first_inputs(seed))
    for name, value in second_inputs(seed + 1).items():
        if name != "x":
            out[name + "_2"] = value
    return out


def reference(
    x, c, positions, mod_w, mod_b, norm_g, gla_w_in, gla_w_g2, gla_b_g2, gla_norm_g, gla_w_out,
    kv_mod_w, kv_mod_b, kv_norm_g, kv_w, swa_w_q, swa_sinks, swa_w_out, peer_w_q, peer_subkeys,
    peer_u, peer_v, final_norm_g, c_2, w_ada_2, b_ada_2, norm1_2, norm2_2, w_in_2, w_ret_o_2,
    q_norm_2, kv_norm_2, w_uq_2, w_ukv_2, w_mla_o_2, w_out_2, w_grp_2, b_grp_2, w_exp_2,
    b_exp_2, w1_2, w3_2, w2_2, final_norm_2,
):
    x = first_block(
        x, c, positions, mod_w, mod_b, norm_g, gla_w_in, gla_w_g2, gla_b_g2, gla_norm_g,
        gla_w_out, kv_mod_w, kv_mod_b, kv_norm_g, kv_w, swa_w_q, swa_sinks, swa_w_out, peer_w_q,
        peer_subkeys, peer_u, peer_v, final_norm_g,
    )
    return second_block(
        x, c_2, w_ada_2, b_ada_2, norm1_2, norm2_2, w_in_2, w_ret_o_2, q_norm_2, kv_norm_2,
        w_uq_2, w_ukv_2, w_mla_o_2, w_out_2, w_grp_2, b_grp_2, w_exp_2, b_exp_2, w1_2, w3_2,
        w2_2, final_norm_2,
    )


_drawn_inputs = setup_inputs


def setup_inputs(seed=0):
    import zlib

    import numpy as np

    out = dict(_drawn_inputs(seed))
    spreads = {}
    factors = {'norm_g': 3.077,
     'gla_b_g2': 3.75,
     'gla_norm_g': 5.56,
     'kv_mod_b': 4.792,
     'kv_norm_g': 8.0,
     'swa_sinks': 6.986,
     'norm1_2': 7.397,
     'norm2_2': 4.484,
     'q_norm_2': 8.0,
     'kv_norm_2': 8.0,
     'b_grp_2': 8.0,
     'b_exp_2': 6.089,
     'final_norm_2': 2.844}
    for name, (base, spread) in spreads.items():
        noise = np.random.default_rng([zlib.crc32(name.encode()), seed]).standard_normal(out[name].shape)
        drawn = base * np.exp(spread * noise) if base else spread * noise
        out[name] = __import__('jax').numpy.asarray(drawn.astype(out[name].dtype))
    for name, factor in factors.items():
        out[name] = (out[name] * factor).astype(out[name].dtype)
    return out
```

```python
from contextlib import ExitStack

import numpy as np
import concourse.bass as bass
from concourse import mybir

F32 = mybir.dt.float32
I32 = mybir.dt.int32
U32 = mybir.dt.uint32
ALU = mybir.AluOpType
ACT = mybir.ActivationFunctionType
AX = mybir.AxisListType

P = 128
D = 1024
T = 256
DC = D // P
TT = T // P
EPS = 1e-6
GH, GDV, GC = 4, 256, 64
NCH = T // GC
RANK = 16
SH, SKV, SHD = 16, 4, 64
PH, NK, TOPK = 8, 128, 16
RH = 4
MH = 8
QL, KVL = 384, 256
NG, EG = 4, 8
NE = NG * EG
NEG = -1.0e30
LOW = -3.0e38
RING = 8
CH = 1024

STREAM = [
    ("mod", 160),
    ("gla_gl", 1), ("gla_q", 4), ("gla_k", 4), ("gla_v", 8), ("gla_og", 8), ("gla_out", 8),
    ("peer0_q", 16), ("peer0_uv", 2 * NK),
    ("kv_k", 4), ("kv_v", 4), ("swa_q", 8), ("swa_out", 8),
    ("peer1_q", 16), ("peer1_uv", 2 * NK),
    ("ret_q", 8), ("ret_k", 8), ("ret_v", 8), ("ret_g", 8), ("mla_cq", 3), ("mla_ckv", 2), ("mla_kpe", 1),
    ("gate_r", 8), ("gate_m", 8), ("ret_o", 8), ("mla_uq", 6), ("mla_uk", 2), ("mla_uv", 2), ("mla_o", 8),
    ("mix_out", 8),
    ("router", 1), ("moe", 6 * NE),
]
N_SLOTS = sum(n for _, n in STREAM)

VECS = [("mod_b", 160), ("ng0a", 8), ("ng0b", 8), ("ng1a", 8), ("ng1b", 8), ("kvg", 8), ("fing", 8), ("n1", 8),
        ("n2", 8), ("fin2", 8), ("gla_b", 4), ("gla_ng", 2), ("qn", 3), ("kvn", 2), ("c", 8), ("c2", 8),
        ("sinks", SH), ("rb", NG + NE)]
CONSTS = [("ident", 128), ("ones", 128), ("iota", 128), ("gmask", 128), ("smask", 384), ("perm_s", 128),
          ("scan", 256), ("cols", 8)]
CONSTS2 = [("perm_m", 128), ("mmask", 384), ("mcos", 256), ("msin", 256), ("rcos", 256), ("rsin", 256),
           ("decay", RH * 384)]


def offsets(table):
    at, out = 0, {}
    for name, n in table:
        out[name] = (at, at + n)
        at += n
    return out, at


VO, NV = offsets(VECS)
CO, NCST = offsets(CONSTS)
C2O, NC2 = offsets(CONSTS2)
SO, _ = offsets(STREAM)

TAU = 16.0
LN2 = 0.6931471805599453
LN2_HI = 0.693359375
LN2_LO = LN2 - LN2_HI
TWO_PI = 6.283185307179586
C1 = 6.28125
C2 = float(np.float32(np.floor((TWO_PI - C1) * 2.0 ** 20) / 2.0 ** 20))
C3 = float(np.float32(TWO_PI - C1 - C2))
PI_IN = 3.1415925


def shape_constants():
    f = np.float32
    c = {}
    r = np.arange(P)
    c["ident"] = np.eye(P)
    c["ones"] = np.ones((P, P))
    c["iota"] = np.tile(r, (P, 1))
    c["gmask"] = (r[:, None] // GC == r[None] // GC) & (r[:, None] <= r[None])
    diag = np.where(r[:, None] >= r[None], 0.0, NEG)
    c["smask"] = np.concatenate([diag, np.where(r[None] > r[:, None], 0.0, NEG), diag], 1)
    m = np.zeros((P, P))
    for i in range(P):
        k = i % SHD
        if k < 16:
            m[(i + 8 if k < 8 else i - 8), i] = 1
    c["perm_s"] = m
    c["scan"] = np.tile(np.arange(T) % GC != 0, (P, 1))
    k = r % SHD
    inv = np.where(k < 16, f(500000.0) ** (-(2 * (k % 8)).astype(f) / f(16)), 0).astype(f)
    cols = np.zeros((P, 8))
    cols[:, 0] = inv
    cols[:, 1] = np.where(k < 8, -1, np.where(k < 16, 1, 0))
    cols[:, 2] = r < 64
    cols[:, 3] = r >= 64
    cols[:, 4] = 1.0
    c["cols"] = cols
    m = np.zeros((P, P))
    for i in range(P):
        m[(i + 32 if i % 64 < 32 else i - 32), i] = 1
    c["perm_m"] = m
    c["mmask"] = np.concatenate([diag, np.zeros((P, P)), diag], 1)
    pos = np.arange(T, dtype=f)

    def rope(dim):
        inv = f(10000.0) ** (-np.arange(0, dim, 2, dtype=f) / f(dim))
        ang = (pos[:, None] * inv[None]).astype(f)
        return np.cos(ang).astype(f).T, np.sin(ang).astype(f).T

    mc, ms = rope(64)
    c["mcos"] = np.tile(mc, (4, 1))
    c["msin"] = np.tile(np.concatenate([-ms, ms]), (2, 1))
    c["rcos"], c["rsin"] = rope(256)
    lg = np.log1p(-np.exp2(-5.0 - np.arange(RH)))
    t = np.arange(T)
    dec = []
    for h in range(RH):
        for jb, lo in ((0, 0), (1, P)):
            rel = t[None, lo:] - (jb * P + r)[:, None]
            dec.append(np.where(rel >= 0, np.exp(lg[h] * np.maximum(rel, 0)), 0.0))
    c["decay"] = np.concatenate(dec, 1)
    cat = lambda tab: np.ascontiguousarray(np.concatenate([np.asarray(c[n], f) for n, _ in tab], 1))
    return cat(CONSTS), cat(CONSTS2)


def block_program(nc, stream, vecs, consts, consts2, xin, pos, wg2, subk, out):
    ctx = ExitStack()
    with ctx:
        def sb(name, shape, dt=F32):
            return ctx.enter_context(nc.sbuf_tensor(name, shape, dt))

        ring = [sb(f"ring{i}", [P, CH]) for i in range(RING)]
        xT = sb("xT", [P, DC, T])
        hT = sb("hT", [P, DC, T])
        modv = sb("modv", [P, 160])
        gain = sb("gain", [P, 7, 8])
        vec = sb("vec", [P, NV])
        cst = sb("cst", [P, NCST])
        wg2s = sb("wg2s", [RANK, 4 * P])
        subks = sb("subks", [P, 4, NK])
        rope_c = sb("rope_c", [P, T])
        rope_s = sb("rope_s", [P, T])
        cact = sb("cact", [P, 16])
        rs = sb("rs", [P, T])
        route = sb("route", [P, 3, T])
        hot = sb("hot", [P, 8, 2, P])
        act_u = sb("act_u", [P, 2, T])
        act_g = sb("act_g", [P, 4, T])
        ARENA = NK * T
        N_LOADS = 6
        arena = sb("arena", [P, ARENA])
        bank = [ctx.enter_context(nc.psum_tensor(f"bank{i}", [P, 512], F32)) for i in range(8)]

        def V(name):
            return vec[:, VO[name][0]:VO[name][1]]

        def C(name):
            return cst[:, CO[name][0]:CO[name][1]]

        ident, ones, iota = C("ident"), C("ones"), C("iota")
        one_col = C("cols")[:, 4:5]

        class Place:
            def __init__(self, at=0):
                self.at = at

            def __call__(self, n):
                a = arena[:, self.at:self.at + n]
                self.at += n
                assert self.at <= ARENA, self.at
                return a

        sems = {}

        def sem(name):
            if name not in sems:
                sems[name] = ctx.enter_context(nc.semaphore(name))
            return sems[name]

        counts = {}

        def signal(name):
            counts[name] = counts.get(name, 0) + 1
            return sem(name)

        def signalled(name):
            return counts[name]

        SQUARES = ["0a", "0b", "kv", "1a", "1b", "mid", "2a", "cq", "ckv", "2b", "out"]
        ROOTS = ["0a", "g", "0b", "kv", "1a", "1b", "mid", "2a", "r", "cq", "ckv", "2b", "out"]
        RESULTS = ["0a", "0b", "kv", "1a", "1b", "mid", "2a", "2b", "out"]

        def results(u):
            return DC * (RESULTS.index(u) + 1)

        landed = [sem(f"landed{i}") for i in range(RING)]
        ring_free = sem("ring_free")
        full = [sem(f"bank_full{i}") for i in range(4)]
        free = [sem(f"bank_free{i}") for i in range(4)]

        tile_no = {}

        def open_tile(name):
            n = tile_no[name] = len(tile_no)
            return bank[n % 4]

        def tile_of(name):
            return bank[tile_no[name] % 4]

        def full_sem(name):
            return full[tile_no[name] % 4]

        def filled(name):
            return tile_no[name] // 4 + 1

        def free_sem(name):
            return free[tile_no[name] % 4]

        def freed(name):
            return tile_no[name] // 4 + 2

        block = ctx.enter_context(nc.Block())

        @block.sync
        def _(sp):
            rounds = N_SLOTS // RING
            with sp.Fori(0, rounds) as r:
                for s in range(RING):
                    sp.wait_ge(ring_free, r * RING + (s + 1))
                    sp.dma_start(ring[s][:, :], stream[r * RING + s]).then_inc(landed[s], 16)
            for s in range(N_SLOTS - rounds * RING):
                sp.wait_ge(ring_free, rounds * RING + s + 1)
                sp.dma_start(ring[s][:, :], stream[rounds * RING + s]).then_inc(landed[s], 16)
            sp.wait_ge(sem("norm_result"), results("out"))
            sp.dma_start(out.rearrange("c p t -> p c t"), hT[:, :, :]).then_inc(sem("stored"), 16)
            sp.wait_ge(sem("stored"), 16)

        def slot(name, k):
            return ring[(SO[name][0] + k) % RING]

        def landed_sem(name, k):
            return landed[(SO[name][0] + k) % RING]

        def landed_at(name, k):
            return 16 * ((SO[name][0] + k) // RING + 1)

        def norm_pe(pe, u, src, n=DC):
            pe.wait_ge(sem("norm_squares"), SQUARES.index(u) + 1)
            t = open_tile(f"n{u}_ss")
            pe.wait_ge(free_sem(f"n{u}_ss"), freed(f"n{u}_ss") - 1)
            for k in range(n):
                mm = pe.matmul(t[:, 0:T], ones, src[:, k, :], start=(k == 0), stop=(k == n - 1))
            mm.then_inc(full_sem(f"n{u}_ss"), 1)

        def project(pe, name, k, src, tile, n=DC):
            w = slot(name, k)
            pe.wait_ge(landed_sem(name, k), landed_at(name, k))
            t = open_tile(tile)
            pe.wait_ge(free_sem(tile), freed(tile) - 1)
            for q in range(n):
                mm = pe.matmul(t[:, 0:T], w[:, q * P:(q + 1) * P], src[:, q, :], start=(q == 0), stop=(q == n - 1))
                if q == 0:
                    mm.then_inc(ring_free, 1)
            mm.then_inc(full_sem(tile), 1)

        def project_tokens(pe, name, src, tile, halves):
            for nh in range(halves):
                t = []
                for a in range(TT):
                    b = open_tile(f"{tile}{nh}{a}")
                    pe.wait_ge(free_sem(f"{tile}{nh}{a}"), freed(f"{tile}{nh}{a}") - 1)
                    t.append(b)
                for kp in range(4):
                    w = slot(name, nh * 4 + kp)
                    pe.wait_ge(landed_sem(name, nh * 4 + kp), landed_at(name, nh * 4 + kp))
                    for q in range(2):
                        for a in range(TT):
                            k = 2 * kp + q
                            mm = pe.matmul(t[a][:, :], src[:, k, a * P:(a + 1) * P], w[:, q * 512:(q + 1) * 512],
                                           start=(k == 0), stop=(k == DC - 1))
                            if q == 0 and a == 0:
                                mm.then_inc(ring_free, 1)
                            if k == DC - 1:
                                mm.then_inc(full_sem(f"{tile}{nh}{a}"), 1)

        def mod_pe(pe):
            pe.sem_inc(ring_free, RING - 1)
            for b in range(4):
                pe.sem_inc(free[b], 1)
            pe.wait_ge(sem("cact"), 1)
            t = open_tile("mod")
            pe.wait_ge(free_sem("mod"), freed("mod") - 1)
            for lo, n, col in ((0, 112, 0), (112, 48, 8)):
                with pe.Fori(0, n // RING) as it:
                    for s in range(RING):
                        pe.wait_ge(landed[s], it * 16 + 16 * (lo // RING + 1))
                        for q in range(DC):
                            mm = pe.matmul(t[:, bass.ds(it * RING + (lo + s), 1)], ring[s][:, q * P:(q + 1) * P],
                                           cact[:, col + q:col + q + 1], start=(q == 0), stop=(q == DC - 1))
                            if q == 0:
                                mm.then_inc(ring_free, 1)
                    mm.then_inc(sem("mod_cols"), 1)
            pe.wait_ge(sem("mod_cols"), 160 // RING)
            pe.sem_inc(full[tile_no["mod"] % 4], 1)

        def gla_pe(pe):
            pe.wait_ge(sem("norm_result"), results("0a"))
            project(pe, "gla_gl", 0, hT, "g_gl")
            for h in range(GH):
                project(pe, "gla_q", h, hT, f"g_q{h}")
            pe.wait_ge(free_sem("g_gl"), freed("g_gl"))
            for h in range(GH):
                t = open_tile(f"g_z{h}")
                pe.wait_ge(free_sem(f"g_z{h}"), freed(f"g_z{h}") - 1)
                pe.matmul(t[:, 0:T], wg2s[:, h * P:(h + 1) * P], G.gl[0:RANK, :], start=True, stop=True).then_inc(full_sem(f"g_z{h}"), 1)
            for h in range(GH):
                project(pe, "gla_k", h, hT, f"g_k{h}")
            project_tokens(pe, "gla_v", hT, "g_v", 2)
            for c in range(8):
                project(pe, "gla_og", c, hT, f"g_og{c}")
            pe.wait_ge(sem("g_kd"), 1)
            for h in range(GH):
                t = open_tile(f"g_kt{h}")
                pe.wait_ge(free_sem(f"g_kt{h}"), freed(f"g_kt{h}") - 1)
                for b in range(TT):
                    mm = pe.transpose(t[:, b * P:(b + 1) * P], G.kd[:, h, b * P:(b + 1) * P], ident)
                mm.then_inc(full_sem(f"g_kt{h}"), 1)
            pe.wait_ge(sem("g_kq"), 2)
            for h in range(GH):
                t = open_tile(f"g_s{h}")
                pe.wait_ge(free_sem(f"g_s{h}"), freed(f"g_s{h}") - 1)
                for b in range(TT):
                    s = slice(b * P, (b + 1) * P)
                    mm = pe.matmul(t[:, s], G.k[:, h, s], G.q[:, h, s], start=True, stop=True)
                mm.then_inc(full_sem(f"g_s{h}"), 1)
            for n in range(NCH):
                b, cs = n // 2, slice(n * GC, (n + 1) * GC)
                for h in range(GH):
                    if n == 0:
                        pe.wait_ge(free_sem(f"g_s{h}"), freed(f"g_s{h}"))
                    else:
                        pe.wait_ge(sem("g_state"), GH * (n - 1) + h + 1)
                    for e in range(2):
                        vs = slice(h * GDV + e * P, h * GDV + (e + 1) * P)
                        o = bank[4 + h][:, e * T + n * GC:e * T + (n + 1) * GC]
                        mm = pe.matmul(o, G.v[:, b, vs], G.sm[:, h, cs], start=True, stop=(n == 0))
                        if n:
                            mm = pe.matmul(o, G.st[:, h, n % 2, e * P:(e + 1) * P], G.q[:, h, cs],
                                           start=False, stop=True)
                    if n == NCH - 1:
                        mm.then_inc(sem("g_o"), 1)
                for h in range(GH if n < NCH - 1 else 0):
                    if n == 0:
                        pe.wait_ge(free_sem(f"g_kt{h}"), freed(f"g_kt{h}"))
                    ps = slice((n % 2) * GC, (n % 2 + 1) * GC)
                    t = open_tile(f"g_u{n}{h}")
                    pe.wait_ge(free_sem(f"g_u{n}{h}"), freed(f"g_u{n}{h}") - 1)
                    pe.matmul(t[:, 0:GDV], G.kt[ps, h, b, :], G.v[ps, b, h * GDV:(h + 1) * GDV],
                                         start=True, stop=True).then_inc(full_sem(f"g_u{n}{h}"), 1)
            for h in range(GH):
                pe.wait_ge(sem("g_sq"), h + 1)
                t = open_tile(f"g_ss{h}")
                pe.wait_ge(free_sem(f"g_ss{h}"), freed(f"g_ss{h}") - 1)
                for e in range(2):
                    mm = pe.matmul(t[:, 0:T], ones, G.sq[:, h % 2, e, :], start=(e == 0), stop=(e == 1))
                mm.then_inc(full_sem(f"g_ss{h}"), 1)
            pe.wait_ge(sem("g_y"), 1)
            for c in range(DC):
                project(pe, "gla_out", c, G.o, f"g_out{c}")

        def peer_pe(pe, l):
            n = f"p{l}"
            pe.wait_ge(sem("norm_result"), results(f"{l}b"))
            for j in range(16):
                project(pe, f"peer{l}_q", j, hT, f"{n}_q{j}")
            for a in range(TT):
                for h in range(PH):
                    pe.wait_ge(free_sem(f"{n}_q{2 * h + 1}"), freed(f"{n}_q{2 * h + 1}"))
                    if h == 0:
                        pe.wait_ge(free_sem(f"{n}_q15"), freed(f"{n}_q15"))
                    t = open_tile(f"{n}_s{a}{h}")
                    pe.wait_ge(free_sem(f"{n}_s{a}{h}"), freed(f"{n}_s{a}{h}") - 1)
                    for half in range(2):
                        mm = pe.matmul(t[:, half * NK:(half + 1) * NK], R.q[:, 2 * h + half, a * P:(a + 1) * P],
                                       subks[:, 2 * l + half, :], start=True, stop=True)
                    mm.then_inc(full_sem(f"{n}_s{a}{h}"), 1)
            for a in range(TT):
                pe.wait_ge(sem(f"{n}_picked"), a + 1)
                t = open_tile(f"{n}_rt{a}")
                pe.wait_ge(free_sem(f"{n}_rt{a}"), freed(f"{n}_rt{a}") - 1)
                for k in range(3):
                    mm = pe.transpose(t[:, k * P:(k + 1) * P], R.pick[:, a, k, :], ident)
                mm.then_inc(full_sem(f"{n}_rt{a}"), 1)
            pe.sem_inc(sem(f"{n}_hot_free"), 8)
            pe.sem_inc(sem(f"{n}_table_free"), 2)
            with pe.Fori(0, T // 8) as it:
                for s in range(8):
                    if s % 4 == 0:
                        pe.wait_ge(sem(f"{n}_table_free"), it * 2 + (s // 4 + 1))
                    pe.wait_ge(sem(f"{n}_hot"), it * 8 + (s + 1))
                    pe.matmul(bank[4 + s // 4][:, (s % 4) * P:(s % 4 + 1) * P], hot[:, s, 0, :], hot[:, s, 1, :],
                              start=True, stop=True).then_inc(sem(f"{n}_hot_free"), 1)
            pe.wait_ge(sem(f"{n}_table_free"), 2 + T // 4)

            base = SO[f"peer{l}_uv"][0]

            def up(i, w, landing):
                pe.wait_ge(landed[w], landing)
                for q in range(DC):
                    mm = pe.matmul(bank[i % 4][:, 0:T], ring[w][:, q * P:(q + 1) * P], hT[:, q, :],
                                   start=(q == 0), stop=(q == DC - 1))
                    if q == 0:
                        mm.then_inc(ring_free, 1)
                mm.then_inc(sem(f"{n}_up"), 1)

            def down(i, w, landing, gated, start=False, stop=False):
                pe.wait_ge(landed[w], landing)
                pe.wait_ge(sem(f"{n}_gated"), gated)
                for a in range(TT):
                    for e in range(2):
                        mm = pe.matmul(bank[4 + 2 * a + e][:, :], act_g[:, i % 4, a * P:(a + 1) * P],
                                       ring[w][:, e * 512:(e + 1) * 512], start=start, stop=stop)
                        if a == 0 and e == 0:
                            mm.then_inc(ring_free, 1)
                return mm

            def at(k):
                c = base + k
                return c % RING, 16 * (c // RING + 1)

            up(0, *at(0))
            up(1, *at(1))
            down(0, *at(2), 1, start=True)
            with pe.Fori(0, 31) as it:
                for k in range(4):
                    w, t0 = at(3 + 2 * k)
                    up(2 + k, w, it * 16 + t0)
                    w, t0 = at(4 + 2 * k)
                    down(1 + k, w, it * 16 + t0, it * 4 + (2 + k))
            for i in (125, 126):
                up(i + 1, *at(2 * i + 1))
                down(i, *at(2 * i + 2), i + 1)
            down(127, *at(255), 128, stop=True).then_inc(sem(f"{n}_sum"), 1)
            back_pe(pe, n)

        def back_pe(pe, n):
            pe.wait_ge(sem(f"{n}_ysb"), 4)
            for c in range(DC):
                t = open_tile(f"{n}_y{c}")
                pe.wait_ge(free_sem(f"{n}_y{c}"), freed(f"{n}_y{c}") - 1)
                for a in range(TT):
                    mm = pe.transpose(t[:, a * P:(a + 1) * P], B.y[:, 2 * a + c // 4, (c % 4) * P:(c % 4 + 1) * P],
                                      ident)
                mm.then_inc(full_sem(f"{n}_y{c}"), 1)

        def attention_pe(pe, n, heads, scores, vcols, vtok):
            for h in range(heads):
                t = open_tile(f"{n}_s{h}")
                pe.wait_ge(free_sem(f"{n}_s{h}"), freed(f"{n}_s{h}") - 1)
                mm = scores(h, t)
                mm.then_inc(full_sem(f"{n}_s{h}"), 1)
            for h in range(heads):
                pe.wait_ge(sem(f"{n}_p"), h + 1)
                t = open_tile(f"{n}_pt{h}")
                pe.wait_ge(free_sem(f"{n}_pt{h}"), freed(f"{n}_pt{h}") - 1)
                for k in range(3):
                    mm = pe.transpose(t[:, k * P:(k + 1) * P], A.p[:, h, k * P:(k + 1) * P], ident)
                mm.then_inc(full_sem(f"{n}_pt{h}"), 1)
                pe.wait_ge(free_sem(f"{n}_pt{h}"), freed(f"{n}_pt{h}"))
                t = open_tile(f"{n}_o{h}")
                pe.wait_ge(free_sem(f"{n}_o{h}"), freed(f"{n}_o{h}") - 1)
                pe.matmul(t[:, 0:P], vtok[:, 0, vcols(h)], A.pt[:, h % 2, 0:P], start=True, stop=True)
                pe.matmul(t[:, P:T], vtok[:, 0, vcols(h)], A.pt[:, h % 2, P:2 * P], start=True, stop=False)
                pe.matmul(t[:, P:T], vtok[:, 1, vcols(h)], A.pt[:, h % 2, 2 * P:3 * P],
                                     start=False, stop=True).then_inc(full_sem(f"{n}_o{h}"), 1)

        def swa_pe(pe):
            pe.wait_ge(sem("norm_result"), results("kv"))
            for k in range(4):
                project(pe, "kv_k", k, hT, f"kv_k{k}")
            project_tokens(pe, "kv_v", hT, "kv_v", 1)
            for k in range(4):
                pe.wait_ge(free_sem(f"kv_k{k}"), freed(f"kv_k{k}"))
                t = open_tile(f"kv_r{k}")
                pe.wait_ge(free_sem(f"kv_r{k}"), freed(f"kv_r{k}") - 1)
                pe.matmul(t[:, 0:T], C("perm_s"), S.k[:, k, :], start=True, stop=True).then_inc(full_sem(f"kv_r{k}"), 1)
            norm_pe(pe, "1a", hT)
            pe.wait_ge(sem("norm_result"), results("1a"))
            for c in range(DC):
                project(pe, "swa_q", c, hT, f"w_q{c}")
            for c in range(DC):
                pe.wait_ge(free_sem(f"w_q{c}"), freed(f"w_q{c}"))
                t = open_tile(f"w_r{c}")
                pe.wait_ge(free_sem(f"w_r{c}"), freed(f"w_r{c}") - 1)
                pe.matmul(t[:, 0:T], C("perm_s"), S.q[:, c, :], start=True, stop=True).then_inc(full_sem(f"w_r{c}"), 1)

            def scores(h, t):
                c, rows = h // 2, slice((h % 2) * SHD, (h % 2 + 1) * SHD)
                k = h // (SH // SKV)
                if h == 0:
                    pe.wait_ge(sem("w_kr"), 4)
                if h % 2 == 0:
                    pe.wait_ge(sem("w_qr"), c + 1)
                pe.matmul(t[:, 0:P], S.q[rows, c, 0:P], S.k[rows, k, 0:P], start=True, stop=True)
                return pe.matmul(t[:, P:3 * P], S.q[rows, c, P:T], S.k[rows, k, :], start=True, stop=True)

            attention_pe(pe, "w", SH, scores, lambda h: slice((h // 4) * P, (h // 4 + 1) * P), S.v)
            pe.wait_ge(free_sem("w_o14"), freed("w_o14"))
            pe.wait_ge(free_sem("w_o15"), freed("w_o15"))
            for c in range(DC):
                project(pe, "swa_out", c, A.o, f"w_out{c}")

        def mix_pe(pe):
            pe.wait_ge(sem("norm_result"), results("2a"))
            for name in ("q", "k"):
                for c in range(8):
                    project(pe, f"ret_{name}", c, hT, f"r_{name}{c}")
            project_tokens(pe, "ret_v", hT, "r_v", 2)
            for c in range(8):
                project(pe, "ret_g", c, hT, f"r_g{c}")
            for c in range(3):
                project(pe, "mla_cq", c, hT, f"m_cq{c}")
            for c in range(2):
                project(pe, "mla_ckv", c, hT, f"m_ckv{c}")
            project(pe, "mla_kpe", 0, hT, "m_kpe")
            for c in range(8):
                project(pe, "gate_r", c, hT, f"r_gate{c}")
            for c in range(8):
                project(pe, "gate_m", c, hT, f"m_gate{c}")
            pe.wait_ge(sem("r_rot"), 4)
            for h in range(RH):
                t = open_tile(f"r_s{h}")
                pe.wait_ge(free_sem(f"r_s{h}"), freed(f"r_s{h}") - 1)
                for jb, cols, qs in ((0, slice(0, T), slice(0, T)), (1, slice(T, T + P), slice(P, T))):
                    for q in range(2):
                        mm = pe.matmul(t[:, cols], M.k[:, 2 * h + q, jb * P:(jb + 1) * P], M.q[:, 2 * h + q, qs],
                                       start=(q == 0), stop=(q == 1))
                mm.then_inc(full_sem(f"r_s{h}"), 1)
            for h in range(RH):
                pe.wait_ge(free_sem(f"r_s{h}"), freed(f"r_s{h}"))
                t = open_tile(f"r_y{h}")
                pe.wait_ge(free_sem(f"r_y{h}"), freed(f"r_y{h}") - 1)
                for e in range(2):
                    vs = slice(h * 256 + e * P, h * 256 + (e + 1) * P)
                    o = e * T
                    pe.matmul(t[:, o:o + P], M.v[:, 0, vs], M.s[:, h, 0:P], start=True, stop=True)
                    pe.matmul(t[:, o + P:o + T], M.v[:, 0, vs], M.s[:, h, P:T], start=True, stop=False)
                    mm = pe.matmul(t[:, o + P:o + T], M.v[:, 1, vs], M.s[:, h, T:T + P], start=False, stop=True)
                mm.then_inc(full_sem(f"r_y{h}"), 1)
            for h in range(RH):
                pe.wait_ge(free_sem(f"r_y{h}"), freed(f"r_y{h}"))
                t = open_tile(f"r_mean{h}")
                pe.wait_ge(free_sem(f"r_mean{h}"), freed(f"r_mean{h}") - 1)
                for e in range(2):
                    mm = pe.matmul(t[:, 0:T], ones, M.y[:, 2 * h + e, :], start=(e == 0), stop=(e == 1))
                mm.then_inc(full_sem(f"r_mean{h}"), 1)
            for h in range(RH):
                pe.wait_ge(sem("r_sq"), h + 1)
                t = open_tile(f"r_var{h}")
                pe.wait_ge(free_sem(f"r_var{h}"), freed(f"r_var{h}") - 1)
                for e in range(2):
                    mm = pe.matmul(t[:, 0:T], ones, M.sq[:, 2 * h + e, :], start=(e == 0), stop=(e == 1))
                mm.then_inc(full_sem(f"r_var{h}"), 1)
            norm_pe(pe, "cq", M.sqc, 3)
            norm_pe(pe, "ckv", M.sqk, 2)
            pe.wait_ge(sem("r_yn"), 1)
            for c in range(DC):
                project(pe, "ret_o", c, M.y, f"r_o{c}")
            pe.wait_ge(sem("m_cqn"), 3)
            for k in range(6):
                w = slot("mla_uq", k)
                pe.wait_ge(landed_sem("mla_uq", k), landed_at("mla_uq", k))
                for j in range(2):
                    i = 2 * k + j
                    t = open_tile(f"m_q{i}")
                    pe.wait_ge(free_sem(f"m_q{i}"), freed(f"m_q{i}") - 1)
                    for q in range(3):
                        mm = pe.matmul(t[:, 0:T], w[:, (3 * j + q) * P:(3 * j + q + 1) * P], M.cq[:, q, :],
                                       start=(q == 0), stop=(q == 2))
                        if j == 0 and q == 0:
                            mm.then_inc(ring_free, 1)
                    mm.then_inc(full_sem(f"m_q{i}"), 1)
            pe.wait_ge(sem("m_ckvn"), 2)
            for k in range(2):
                w = slot("mla_uk", k)
                pe.wait_ge(landed_sem("mla_uk", k), landed_at("mla_uk", k))
                for j in range(4):
                    t = open_tile(f"m_k{4 * k + j}")
                    pe.wait_ge(free_sem(f"m_k{4 * k + j}"), freed(f"m_k{4 * k + j}") - 1)
                    for q in range(2):
                        mm = pe.matmul(t[:, 0:T], w[:, (2 * j + q) * P:(2 * j + q + 1) * P], M.ckv[:, q, :],
                                       start=(q == 0), stop=(q == 1))
                        if j == 0 and q == 0:
                            mm.then_inc(ring_free, 1)
                    mm.then_inc(full_sem(f"m_k{4 * k + j}"), 1)
            for nh in range(2):
                w = slot("mla_uv", nh)
                pe.wait_ge(landed_sem("mla_uv", nh), landed_at("mla_uv", nh))
                for a in range(TT):
                    t = open_tile(f"m_v{nh}{a}")
                    pe.wait_ge(free_sem(f"m_v{nh}{a}"), freed(f"m_v{nh}{a}") - 1)
                    for q in range(2):
                        mm = pe.matmul(t[:, :], M.ckv[:, q, a * P:(a + 1) * P], w[:, q * 512:(q + 1) * 512],
                                       start=(q == 0), stop=(q == 1))
                        if a == 0 and q == 0:
                            mm.then_inc(ring_free, 1)
                    mm.then_inc(full_sem(f"m_v{nh}{a}"), 1)
            for c in range(5):
                pe.wait_ge(free_sem(f"m_q{8 + c}" if c < 4 else "m_kpe"), freed(f"m_q{8 + c}" if c < 4 else "m_kpe"))
                t = open_tile(f"m_r{c}")
                pe.wait_ge(free_sem(f"m_r{c}"), freed(f"m_r{c}") - 1)
                pe.matmul(t[:, 0:T], M.perm, M.qp[:, c, :] if c < 4 else M.kp[:, 0, :], start=True, stop=True).then_inc(full_sem(f"m_r{c}"), 1)

            def scores(h, t):
                if h == 0:
                    pe.wait_ge(free_sem("m_v11"), freed("m_v11"))
                    pe.wait_ge(sem("m_rot"), 6)
                for o, qs, n in ((0, slice(0, P), P), (P, slice(P, T), T)):
                    pe.matmul(t[:, o:o + n], M.qn[:, h, qs], M.kn[:, h, 0:n], start=True, stop=False)
                    mm = pe.matmul(t[:, o:o + n], M.qp[:, h // 2, qs], M.kp[:, 1 + h % 2, 0:n], start=False, stop=True)
                return mm

            attention_pe(pe, "m", MH, scores, lambda h: slice(h * P, (h + 1) * P), M.vm)
            pe.wait_ge(free_sem("m_o7"), freed("m_o7"))
            pe.wait_ge(free_sem("m_o6"), freed("m_o6"))
            for c in range(DC):
                project(pe, "mla_o", c, A.o, f"m_out{c}")
            pe.wait_ge(sem("merged"), 1)
            for c in range(DC):
                project(pe, "mix_out", c, M.mg, f"mix{c}")

        def moe_pe(pe):
            pe.wait_ge(sem("norm_result"), results("2b"))
            w = slot("router", 0)
            pe.wait_ge(landed_sem("router", 0), landed_at("router", 0))
            t = []
            for a in range(TT):
                b = open_tile(f"e_l{a}")
                pe.wait_ge(free_sem(f"e_l{a}"), freed(f"e_l{a}") - 1)
                t.append(b)
            for a in range(TT):
                for q in range(DC):
                    mm = pe.matmul(t[a][:, 0:NG + NE], hT[:, q, a * P:(a + 1) * P], w[:, q * P:q * P + NG + NE],
                                   start=(q == 0), stop=(q == DC - 1))
                    if a == 0 and q == 0:
                        mm.then_inc(ring_free, 1)
                mm.then_inc(full_sem(f"e_l{a}"), 1)
            pe.wait_ge(sem("e_gate"), 1)
            t = open_tile("e_gt")
            pe.wait_ge(free_sem("e_gt"), freed("e_gt") - 1)
            for a in range(TT):
                mm = pe.transpose(t[0:NE, a * P:(a + 1) * P], E.gate[:, a, :], ident)
            mm.then_inc(full_sem("e_gt"), 1)
            pe.wait_ge(free_sem("e_gt"), freed("e_gt"))
            for e in range(NE // 2):
                t = open_tile(f"e_b{e}")
                pe.wait_ge(free_sem(f"e_b{e}"), freed(f"e_b{e}") - 1)
                for k in range(2):
                    mm = pe.matmul(t[:, k * T:(k + 1) * T], cst[0:NE, 2 * e + k:2 * e + k + 1].broadcast_to([NE, P]),
                                   E.gt[0:NE, :], start=True, stop=True)
                mm.then_inc(full_sem(f"e_b{e}"), 1)
            for e in range(NE // 2 - 4, NE // 2):
                pe.wait_ge(free_sem(f"e_b{e}"), freed(f"e_b{e}"))
            base = SO["moe"][0]

            def at(k):
                c = base + k
                return c % RING, 16 * (c // RING + 1)

            def up(par, k, step):
                for m in range(2):
                    for f in range(2):
                        w, t0 = at(k + 2 * m + f)
                        pe.wait_ge(landed[w], step(t0))
                        for q in range(DC):
                            mm = pe.matmul(bank[2 * par + m][:, f * T:(f + 1) * T], ring[w][:, q * P:(q + 1) * P],
                                           hT[:, q, :], start=(q == 0), stop=(q == DC - 1))
                            if q == 0:
                                mm.then_inc(ring_free, 1)
                mm.then_inc(sem("e_up"), 1)

            def down(par, k, step, hidden, start=False, stop=False):
                pe.wait_ge(sem("e_hid"), hidden)
                for f in range(2):
                    w, t0 = at(k + f)
                    pe.wait_ge(landed[w], step(t0))
                    for a in range(TT):
                        for e in range(2):
                            mm = pe.matmul(bank[4 + 2 * a + e][:, :], E.hid[:, par, f, a * P:(a + 1) * P],
                                           ring[w][:, e * 512:(e + 1) * 512], start=(start and f == 0),
                                           stop=(stop and f == 1))
                            if a == 0 and e == 0:
                                mm.then_inc(ring_free, 1)
                return mm

            same = lambda t0: t0
            up(0, 0, same)
            up(1, 4, same)
            down(0, 8, same, 1, start=True)
            with pe.Fori(0, 7) as it:
                for j in range(4):
                    k = 10 + 6 * j
                    step = lambda t0: it * 48 + t0
                    up(j % 2, k, step)
                    down((1 + j) % 2, k + 4, step, it * 4 + (2 + j))
            for e in (29, 30):
                up((e + 1) % 2, 10 + 6 * (e - 1), same)
                down(e % 2, 14 + 6 * (e - 1), same, e + 1)
            down(1, 6 * NE - 2, same, NE, stop=True).then_inc(sem("e_sum"), 1)
            back_pe(pe, "e")

        mean = act_g

        class Bag:
            pass

        G, R, A, S, M, E, B, G2 = (Bag() for _ in range(8))
        G2.r2 = act_u[:, 0, :]
        ph = Place()
        G.gl = ph(T)
        G.q = ph(GH * T).rearrange("p (h t) -> p h t", h=GH)
        G.k = ph(GH * T).rearrange("p (h t) -> p h t", h=GH)
        G.kd = ph(GH * T).rearrange("p (h t) -> p h t", h=GH)
        G.z = ph(GH * T).rearrange("p (h t) -> p h t", h=GH)
        G.b = ph(GH * T).rearrange("p (h t) -> p h t", h=GH)
        G.e = ph(GH * T).rearrange("p (h t) -> p h t", h=GH)
        G.e2 = ph(GH * T).rearrange("p (h t) -> p h t", h=GH)
        G.dec = ph(GH * NCH).rearrange("p (h n) -> p h n", h=GH)
        G.v = ph(2 * D).rearrange("p (a n) -> p a n", a=2)
        G.kt = ph(GH * T).rearrange("p (h b k) -> p h b k", h=GH, b=2)
        G.sm = ph(GH * T).rearrange("p (h t) -> p h t", h=GH)
        G.st = ph(GH * 2 * GDV).rearrange("p (h s e) -> p h s e", h=GH, s=2)
        G.sq = ph(4 * T).rearrange("p (h e t) -> p h e t", h=2, e=2)
        G.r = ph(GH * T).rearrange("p (h t) -> p h t", h=GH)
        G.og = ph(8 * T).rearrange("p (c t) -> p c t", c=8)
        G.o = ph(8 * T).rearrange("p (c t) -> p c t", c=8)

        ph = Place()
        R.q = ph(16 * T).rearrange("p (j t) -> p j t", j=16)
        R.s = ph(TT * 16 * NK).rearrange("p (a g n) -> p a g n", a=2, g=16)
        R.s2 = ph(16 * NK).rearrange("p (g n) -> p g n", g=16)
        R.v = ph(TT * 256).rearrange("p (a g k) -> p a g k", a=2, g=16)
        R.ix = ph(TT * 256).rearrange("p (a g k) -> p a g k", a=2, g=16)
        R.ixf = ph(TT * 256).rearrange("p (a g k) -> p a g k", a=2, g=16)
        R.cand = ph(PH * 256).rearrange("p (h c) -> p h c", h=PH)
        R.cand2 = ph(PH * 256).rearrange("p (h c) -> p h c", h=PH)
        R.cs = ph(128).rearrange("p (h k) -> p h k", h=PH)
        R.ci = ph(128).rearrange("p (h k) -> p h k", h=PH)
        R.ca = ph(128)
        R.cb = ph(128)
        R.caf = ph(128)
        R.cbf = ph(128)
        R.sum = ph(16)
        R.pick = ph(TT * 3 * 128).rearrange("p (a k n) -> p a k n", a=2, k=3)
        W = arena[:, 0:NK * T].rearrange("p (i t) -> p i t", i=NK)
        B.y = arena[:, 0:4 * 512].rearrange("p (a n) -> p a n", a=4)

        ph = Place()
        A.p = ph(SH * 384).rearrange("p (h k) -> p h k", h=SH)
        A.pt = ph(2 * 384).rearrange("p (s k) -> p s k", s=2)
        A.m = ph(2 * SH).rearrange("p (b h) -> p b h", b=2)
        A.l = ph(2 * SH).rearrange("p (b h) -> p b h", b=2)
        A.x = ph(2 * SH).rearrange("p (b h) -> p b h", b=2)
        A.o = ph(8 * T).rearrange("p (c t) -> p c t", c=8)
        mark = ph.at
        S.k = ph(4 * T).rearrange("p (c t) -> p c t", c=4)
        S.v = ph(TT * 512).rearrange("p (a n) -> p a n", a=2)
        S.q = ph(8 * T).rearrange("p (c t) -> p c t", c=8)
        S.tmp = ph(T)

        ph = Place(mark)
        M.cst = ph(NC2)
        M.perm = M.cst[:, C2O["perm_m"][0]:C2O["perm_m"][1]]
        M.q = ph(8 * T).rearrange("p (c t) -> p c t", c=8)
        M.k = ph(8 * T).rearrange("p (c t) -> p c t", c=8)
        M.v = ph(TT * D).rearrange("p (a n) -> p a n", a=2)
        M.g = ph(8 * T).rearrange("p (c t) -> p c t", c=8)
        M.gr = ph(8 * T).rearrange("p (c t) -> p c t", c=8)
        M.gm = ph(8 * T).rearrange("p (c t) -> p c t", c=8)
        M.cq = ph(3 * T).rearrange("p (c t) -> p c t", c=3)
        M.ckv = ph(2 * T).rearrange("p (c t) -> p c t", c=2)
        M.kp = ph(3 * T).rearrange("p (c t) -> p c t", c=3)
        M.sqc = ph(3 * T).rearrange("p (c t) -> p c t", c=3)
        M.sqk = ph(2 * T).rearrange("p (c t) -> p c t", c=2)
        M.s = ph(RH * 384).rearrange("p (h t) -> p h t", h=RH)
        M.y = A.p[:, 0:6, :].rearrange("p h k -> p (h k)")[:, 0:8 * T].rearrange("p (c t) -> p c t", c=8)
        M.sq = A.p[:, 6:12, :].rearrange("p h k -> p (h k)")[:, 0:8 * T].rearrange("p (c t) -> p c t", c=8)
        M.r = ph(RH * T).rearrange("p (h t) -> p h t", h=RH)
        M.t = A.p[:, 10:16, :].rearrange("p h k -> p (h k)")[:, 0:8 * T].rearrange("p (c t) -> p c t", c=8)
        M.qn, M.kn, M.vm = M.q, M.k, M.v
        M.qp = M.s[:, 0:3, :].rearrange("p h t -> p (h t)")[:, 0:4 * T].rearrange("p (c t) -> p c t", c=4)
        M.mg = M.g

        ph = Place(2048)
        E.l = ph(TT * (NG + NE)).rearrange("p (a n) -> p a n", a=2)
        E.g8 = ph(TT * 8).rearrange("p (a n) -> p a n", a=2)
        E.m8 = ph(TT * 8).rearrange("p (a n) -> p a n", a=2)
        E.i8 = ph(TT * 8).rearrange("p (a n) -> p a n", a=2)
        E.if8 = ph(TT * 8).rearrange("p (a n) -> p a n", a=2)
        E.oh = ph(TT * NG).rearrange("p (a n) -> p a n", a=2)
        E.x8 = ph(TT * 8).rearrange("p (a n) -> p a n", a=2)
        E.w = ph(TT * 8).rearrange("p (a n) -> p a n", a=2)
        E.tmp = ph(TT * NE).rearrange("p (a n) -> p a n", a=2)
        E.ew = ph(TT * 8).rearrange("p (a n) -> p a n", a=2)
        E.ew2 = ph(TT * 8).rearrange("p (a n) -> p a n", a=2)
        E.gate = ph(TT * NE).rearrange("p (a n) -> p a n", a=2)
        E.gt = ph(T)
        E.gb = ph(NE * T).rearrange("p (e t) -> p e t", e=NE)
        E.sa = ph(2 * 512).rearrange("p (s n) -> p s n", s=2)
        E.hp = ph(2 * 512).rearrange("p (s n) -> p s n", s=2)
        E.hid = ph(2 * 512).rearrange("p (s f t) -> p s f t", s=2, f=2)

        @block.tensor
        def _(pe):
            pe.wait_ge(sem("loaded"), 16 * N_LOADS)
            mod_pe(pe)
            norm_pe(pe, "0a", hT)
            gla_pe(pe)
            norm_pe(pe, "0b", hT)
            peer_pe(pe, 0)
            norm_pe(pe, "kv", hT)
            swa_pe(pe)
            norm_pe(pe, "1b", hT)
            peer_pe(pe, 1)
            norm_pe(pe, "mid", hT)
            norm_pe(pe, "2a", hT)
            mix_pe(pe)
            norm_pe(pe, "2b", hT)
            moe_pe(pe)
            norm_pe(pe, "out", hT)

        def norm_act(act, u):
            act.activation(hT[:, :, :], xT[:, :, :], ACT.Square).then_inc(signal("norm_squares"), 1)
            act.wait_ge(sem("norm_squares"), signalled("norm_squares"))
            root_act(act, u, rs[:, :])

        def root_act(act, u, r):
            act.wait_ge(sem("norm_mean"), ROOTS.index(u) + 1)
            act.activation(r, r, ACT.Sqrt).then_inc(signal("norm_root"), 1)
            act.wait_ge(sem("norm_root"), signalled("norm_root"))

        def copy_act(act, dst, name, src=None, func=ACT.Copy):
            act.wait_ge(full_sem(name), filled(name))
            t = tile_of(name)
            act.activation(dst, t[:, 0:T] if src is None else src(t), func).then_inc(free_sem(name), 1)
            act.wait_ge(free_sem(name), freed(name))

        def mod_act(act):
            act.activation(cact[:, 0:8], V("c"), ACT.Sigmoid).then_inc(signal("csig"), 1)
            act.wait_ge(sem("csig"), signalled("csig"))
            act.activation(cact[:, 8:16], V("c2"), ACT.Sigmoid).then_inc(signal("csig"), 1)
            act.wait_ge(sem("csig"), signalled("csig"))
            act.wait_ge(sem("rope_args"), 1)
            act.activation(rope_c[:, :], rope_c[:, :], ACT.Sin).then_inc(signal("rope_sin"), 1)
            act.wait_ge(sem("rope_sin"), signalled("rope_sin"))
            act.activation(rope_s[:, :], rope_s[:, :], ACT.Sin).then_inc(signal("rope_sin"), 1)
            act.wait_ge(sem("rope_sin"), signalled("rope_sin"))

        def gla_act(act):
            copy_act(act, G.gl, "g_gl")
            for h in range(GH):
                copy_act(act, G.q[:, h, :], f"g_q{h}")
            for h in range(GH):
                copy_act(act, G.k[:, h, :], f"g_k{h}")
            for nh in range(2):
                for a in range(TT):
                    copy_act(act, G.v[:, a, nh * 512:(nh + 1) * 512], f"g_v{nh}{a}", lambda t: t[:, :])
            for c in range(8):
                copy_act(act, G.og[:, c, :], f"g_og{c}")
            act.wait_ge(sem("g_abs"), 1)
            act.activation(G.e, G.e, ACT.Sigmoid, scale=-1.0).then_inc(signal("g_act"), 1)
            act.wait_ge(sem("g_act"), signalled("g_act"))
            act.activation(G.e, G.e, ACT.Ln).then_inc(signal("g_ln"), 1)
            act.wait_ge(sem("g_ln"), signalled("g_ln"))
            act.activation(G.o, G.og, ACT.Sigmoid).then_inc(signal("g_sig"), 1)
            act.wait_ge(sem("g_sig"), signalled("g_sig"))
            for h in range(GH):
                copy_act(act, G.kt[:, h, :, :], f"g_kt{h}", lambda t: t[:, 0:T].rearrange("p (b k) -> p b k", b=2))
            for h in range(GH):
                act.wait_ge(sem("g_o"), h + 1)
                if h >= 2:
                    act.wait_ge(free_sem(f"g_ss{h - 2}"), freed(f"g_ss{h - 2}"))
                act.activation(G.sq[:, h % 2, :, :], bank[4 + h][:, :].rearrange("p (e t) -> p e t", e=2),
                                         ACT.Square).then_inc(signal("g_sq"), 1)
                act.wait_ge(sem("g_sq"), signalled("g_sq"))
            root_act(act, "g", G.r)

        def peer_act(act, l):
            n = f"p{l}"
            for j in range(16):
                copy_act(act, R.q[:, j, :], f"{n}_q{j}")
            for a in range(TT):
                for h in range(PH):
                    copy_act(act, R.s[:, a, 2 * h:2 * h + 2, :], f"{n}_s{a}{h}",
                             lambda t: t[:, 0:2 * NK].rearrange("p (g n) -> p g n", g=2))
            for a in range(TT):
                act.wait_ge(sem(f"{n}_cs"), a + 1)
                act.activation(R.cs, R.cs, ACT.Exp).then_inc(signal(f"{n}_ecs"), 1)
                act.wait_ge(sem(f"{n}_ecs"), signalled(f"{n}_ecs"))
            with act.Fori(0, T // 8) as it:
                for k in range(2):
                    act.wait_ge(sem(f"{n}_hot_free"), it * 8 + (8 + 4 * k + 4))
                    act.activation(W[:, :, bass.ds(it * 8 + 4 * k, 4)],
                                   bank[4 + k][:, :].rearrange("p (t i) -> p i t", t=4),
                                   ACT.Copy).then_inc(sem(f"{n}_table_free"), 1)
            with act.Fori(0, NK // 4) as it:
                for k in range(4):
                    act.wait_ge(sem(f"{n}_up"), it * 4 + (k + 1))
                    act.activation(act_u[:, k % 2, :], bank[k][:, 0:T], ACT.Gelu).then_inc(sem(f"{n}_gelu"), 1)
            back_act(act, n)

        def back_act(act, n):
            act.wait_ge(sem(f"{n}_sum"), 1)
            for a in range(4):
                act.activation(B.y[:, a, :], bank[4 + a][:, :], ACT.Copy).then_inc(signal(f"{n}_ysb"), 1)
                act.wait_ge(sem(f"{n}_ysb"), signalled(f"{n}_ysb"))

        def attention_act(act, n, heads):
            for h in range(heads):
                for b, cols in ((0, slice(0, P)), (1, slice(P, 3 * P))):
                    if h == 0 and b == 0:
                        act.wait_ge(sem(f"{n}_max"), 1)
                    ins = act.activation(A.p[:, h, cols], A.p[:, h, cols], ACT.Exp, bias=A.x[:, b, h:h + 1],
                                         accum_out=A.l[:, b, h:h + 1])
                ins.then_inc(signal(f"{n}_exp"), 1)
                act.wait_ge(sem(f"{n}_exp"), signalled(f"{n}_exp"))

        def attention_copies_act(act, n, heads):
            for h in range(heads):
                copy_act(act, A.pt[:, h % 2, :], f"{n}_pt{h}", lambda t: t[:, 0:384])

        def swa_act(act):
            for k in range(4):
                copy_act(act, S.k[:, k, :], f"kv_k{k}")
            for a in range(TT):
                copy_act(act, S.v[:, a, :], f"kv_v0{a}", lambda t: t[:, :])
            act.wait_ge(free_sem("kv_v01"), freed("kv_v01"))
            norm_act(act, "1a")
            for c in range(DC):
                copy_act(act, S.q[:, c, :], f"w_q{c}")
            act.wait_ge(sem("w_max"), 1)
            act.activation(A.m, A.m, ACT.Exp).then_inc(signal("w_sink"), 1)
            act.wait_ge(sem("w_sink"), signalled("w_sink"))
            attention_act(act, "w", SH)
            attention_copies_act(act, "w", SH)

        def mix_act(act):
            for c in range(8):
                copy_act(act, M.q[:, c, :], f"r_q{c}")
            for c in range(8):
                copy_act(act, M.k[:, c, :], f"r_k{c}")
            for nh in range(2):
                for a in range(TT):
                    copy_act(act, M.v[:, a, nh * 512:(nh + 1) * 512], f"r_v{nh}{a}", lambda t: t[:, :])
            for c in range(8):
                copy_act(act, M.g[:, c, :], f"r_g{c}", func=ACT.Silu)
            for c in range(3):
                copy_act(act, M.cq[:, c, :], f"m_cq{c}")
            for c in range(2):
                copy_act(act, M.ckv[:, c, :], f"m_ckv{c}")
            copy_act(act, M.kp[:, 0, :], "m_kpe")
            act.activation(M.sqc, M.cq, ACT.Square).then_inc(signal("norm_squares"), 1)
            act.wait_ge(sem("norm_squares"), signalled("norm_squares"))
            act.activation(M.sqk, M.ckv, ACT.Square).then_inc(signal("norm_squares"), 1)
            act.wait_ge(sem("norm_squares"), signalled("norm_squares"))
            for c in range(8):
                copy_act(act, M.gr[:, c, :], f"r_gate{c}", func=ACT.Sigmoid)
            for c in range(8):
                copy_act(act, M.gm[:, c, :], f"m_gate{c}", func=ACT.Sigmoid)
            for h in range(RH):
                copy_act(act, M.y[:, 2 * h:2 * h + 2, :], f"r_y{h}", lambda t: t[:, :].rearrange("p (e t) -> p e t", e=2))
            for h in range(RH):
                act.wait_ge(sem("r_cent"), h + 1)
                act.activation(M.sq[:, 2 * h:2 * h + 2, :], M.y[:, 2 * h:2 * h + 2, :], ACT.Square).then_inc(signal("r_sq"), 1)
                act.wait_ge(sem("r_sq"), signalled("r_sq"))
            root_act(act, "r", M.r)
            root_act(act, "cq", rs[:, :])
            root_act(act, "ckv", G2.r2)
            for i in range(12):
                copy_act(act, M.qn[:, i, :] if i < 8 else M.qp[:, i - 8, :], f"m_q{i}")
            for i in range(8):
                copy_act(act, M.kn[:, i, :], f"m_k{i}")
            for nh in range(2):
                for a in range(TT):
                    copy_act(act, M.vm[:, a, nh * 512:(nh + 1) * 512], f"m_v{nh}{a}", lambda t: t[:, :])
            attention_act(act, "m", MH)
            attention_copies_act(act, "m", MH)

        def moe_act(act):
            act.wait_ge(sem("e_gx"), 1)
            act.activation(E.x8, E.x8, ACT.Exp).then_inc(signal("e_gexp"), 1)
            act.wait_ge(sem("e_gexp"), signalled("e_gexp"))
            act.wait_ge(sem("e_vx"), 1)
            act.activation(E.w[:, :, 0:1], E.w[:, :, 0:1], ACT.Exp).then_inc(signal("e_vexp"), 1)
            act.wait_ge(sem("e_vexp"), signalled("e_vexp"))
            copy_act(act, E.gt[0:NE, :], "e_gt", lambda t: t[0:NE, 0:T])
            for e in range(NE // 2):
                copy_act(act, E.gb[:, 2 * e:2 * e + 2, :], f"e_b{e}", lambda t: t[:, :].rearrange("p (e t) -> p e t", e=2))
            with act.Fori(0, NE // 2) as it:
                for s in range(2):
                    act.wait_ge(sem("e_up"), it * 2 + (s + 1))
                    act.activation(E.sa[:, s, :], bank[2 * s][:, :], ACT.Silu).then_inc(sem("e_silu"), 1)
            back_act(act, "e")

        @block.scalar
        def _(act):
            for dst, src in ((vec[:, :], vecs), (cst[:, :], consts), (xT[:, :, :], xin.rearrange("c p t -> p c t")),
                             (G.z.rearrange("p h t -> p (h t)")[:, 0:T].bitcast(I32), pos), (wg2s[:, :], wg2),
                             (subks[:, :, :], subk)):
                act.dma_start(dst, src).then_inc(sem("loaded"), 16)
            act.wait_ge(sem("loaded"), 16 * N_LOADS)
            mod_act(act)
            norm_act(act, "0a")
            gla_act(act)
            act.wait_ge(free_sem("g_out7"), freed("g_out7"))
            norm_act(act, "0b")
            peer_act(act, 0)
            act.wait_ge(free_sem("p0_y7"), freed("p0_y7"))
            norm_act(act, "kv")
            swa_act(act)
            act.wait_ge(free_sem("w_out7"), freed("w_out7"))
            norm_act(act, "1b")
            peer_act(act, 1)
            act.wait_ge(free_sem("p1_y7"), freed("p1_y7"))
            act.dma_start(M.cst, consts2).then_inc(sem("loaded2"), 16)
            act.wait_ge(free_sem("p1_y7"), freed("p1_y7"))
            norm_act(act, "mid")
            act.wait_ge(sem("norm_result"), results("mid"))
            norm_act(act, "2a")
            mix_act(act)
            act.wait_ge(free_sem("mix7"), freed("mix7"))
            norm_act(act, "2b")
            moe_act(act)
            act.wait_ge(free_sem("e_y7"), freed("e_y7"))
            norm_act(act, "out")

        def inv_root_dve(dve, u, r, tiles, width):
            for i, (tile, part) in enumerate(tiles):
                dve.wait_ge(full_sem(tile), filled(tile))
                t = tile_of(tile)
                dve.tensor_scalar(part, t[:, 0:T], 1.0 / width, EPS, ALU.mult, ALU.add).then_inc(free_sem(tile), 1)
                dve.wait_ge(free_sem(tile), freed(tile))
                dve.tensor_copy(mean[:, i, :], part).then_inc(signal("dve_step"), 1)
                dve.wait_ge(sem("dve_step"), signalled("dve_step"))
            dve.sem_inc(sem("norm_mean"), 1)
            dve.wait_ge(sem("norm_root"), ROOTS.index(u) + 1)
            dve.reciprocal(r, r).then_inc(signal("dve_step"), 1)
            dve.wait_ge(sem("dve_step"), signalled("dve_step"))
            m = mean[:, 0, :] if len(tiles) == 1 else mean[:, 0:len(tiles), :]
            dve.tensor_tensor(m, m, r, ALU.mult).then_inc(signal("dve_step"), 1)
            dve.wait_ge(sem("dve_step"), signalled("dve_step"))
            dve.tensor_tensor(m, m, r, ALU.mult).then_inc(signal("dve_step"), 1)
            dve.wait_ge(sem("dve_step"), signalled("dve_step"))
            dve.tensor_scalar(m, m, -0.5, 1.5, ALU.mult, ALU.add).then_inc(signal("dve_step"), 1)
            dve.wait_ge(sem("dve_step"), signalled("dve_step"))
            dve.tensor_tensor(r, r, m, ALU.mult).then_inc(signal("dve_step"), 1)
            dve.wait_ge(sem("dve_step"), signalled("dve_step"))

        def norm_dve(dve, u, gains, shifts, dst=None):
            inv_root_dve(dve, u, rs[:, :], [(f"n{u}_ss", rs[:, :])], D)
            dst = hT if dst is None else dst
            dve.tensor_tensor(dst[:, :, :], xT[:, :, :], rs[:, :].unsqueeze(1).broadcast_to([P, DC, T]),
                                         ALU.mult).then_inc(signal("dve_step"), 1)
            dve.wait_ge(sem("dve_step"), signalled("dve_step"))
            for c in range(DC):
                if shifts is None:
                    ins = dve.tensor_scalar(dst[:, c, :], dst[:, c, :], gains[:, c:c + 1], None, ALU.mult)
                else:
                    ins = dve.tensor_scalar(dst[:, c, :], dst[:, c, :], gains[:, c:c + 1], shifts[:, c:c + 1],
                                            ALU.mult, ALU.add)
                ins.then_inc(signal("norm_result"), 1)
                dve.wait_ge(sem("norm_result"), signalled("norm_result"))

        def update_dve(dve, tile, gate):
            for c in range(DC):
                dve.wait_ge(full_sem(f"{tile}{c}"), filled(f"{tile}{c}"))
                t = tile_of(f"{tile}{c}")
                dve.scalar_tensor_tensor(xT[:, c, :], t[:, 0:T], gate[:, c:c + 1], xT[:, c, :],
                                                      ALU.mult, ALU.add).then_inc(free_sem(f"{tile}{c}"), 1)
                dve.wait_ge(free_sem(f"{tile}{c}"), freed(f"{tile}{c}"))

        def wrap(dve, r, tmp):
            for op, lim, step in ((ALU.is_gt, PI_IN, -TWO_PI), (ALU.is_lt, -PI_IN, TWO_PI)):
                dve.tensor_scalar(tmp, r, lim, step, op, ALU.mult).then_inc(signal("dve_step"), 1)
                dve.wait_ge(sem("dve_step"), signalled("dve_step"))
                dve.tensor_tensor(r, r, tmp, ALU.add).then_inc(signal("dve_step"), 1)
                dve.wait_ge(sem("dve_step"), signalled("dve_step"))
            dve.tensor_scalar(r, r, PI_IN, -PI_IN, ALU.min, ALU.max).then_inc(signal("dve_step"), 1)
            dve.wait_ge(sem("dve_step"), signalled("dve_step"))

        def mod_dve(dve):
            dve.wait_ge(sem("csig"), 2)
            dve.tensor_tensor(cact[:, :], cact[:, :], vec[:, VO["c"][0]:VO["c2"][1]], ALU.mult).then_inc(signal("cact"), 1)
            dve.wait_ge(sem("cact"), signalled("cact"))
            ang, k, kf = G.b[:, 0, :], G.b[:, 1, :], G.b[:, 2, :]
            posi = G.z.rearrange("p h t -> p (h t)")[:, 0:T].bitcast(I32)
            inv, sign = C("cols")[:, 0:1], C("cols")[:, 1:2]
            dve.tensor_copy(ang, posi).then_inc(signal("dve_step"), 1)
            dve.wait_ge(sem("dve_step"), signalled("dve_step"))
            dve.tensor_scalar(ang, ang, inv, None, ALU.mult).then_inc(signal("dve_step"), 1)
            dve.wait_ge(sem("dve_step"), signalled("dve_step"))
            dve.tensor_scalar(k.bitcast(I32), ang, 1.0 / TWO_PI, None, ALU.mult).then_inc(signal("dve_step"), 1)
            dve.wait_ge(sem("dve_step"), signalled("dve_step"))
            dve.tensor_copy(kf, k.bitcast(I32)).then_inc(signal("dve_step"), 1)
            dve.wait_ge(sem("dve_step"), signalled("dve_step"))
            for c in (C1, C2, C3):
                dve.scalar_tensor_tensor(ang, kf, -c, ang, ALU.mult, ALU.add).then_inc(signal("dve_step"), 1)
                dve.wait_ge(sem("dve_step"), signalled("dve_step"))
            wrap(dve, ang, kf)
            dve.tensor_scalar(rope_s[:, :], ang, 1.0, None, ALU.mult).then_inc(signal("dve_step"), 1)
            dve.wait_ge(sem("dve_step"), signalled("dve_step"))
            dve.tensor_scalar(rope_c[:, :], ang, TWO_PI / 4, None, ALU.add).then_inc(signal("dve_step"), 1)
            dve.wait_ge(sem("dve_step"), signalled("dve_step"))
            wrap(dve, rope_c[:, :], kf)
            dve.sem_inc(sem("rope_args"), 1)
            dve.wait_ge(sem("rope_sin"), 2)
            dve.tensor_scalar(rope_s[:, :], rope_s[:, :], sign, None, ALU.mult).then_inc(signal("dve_step"), 1)
            dve.wait_ge(sem("dve_step"), signalled("dve_step"))
            dve.wait_ge(full_sem("mod"), filled("mod"))
            t = tile_of("mod")
            dve.tensor_tensor(modv[:, :], t[:, 0:160], V("mod_b"), ALU.add).then_inc(free_sem("mod"), 1)
            dve.wait_ge(free_sem("mod"), freed("mod"))
            for i, (g, at) in enumerate((("ng0a", 8), ("ng0b", 32), ("ng1a", 56), ("ng1b", 80), ("kvg", 104),
                                         ("n1", 120), ("n2", 144))):
                dve.scalar_tensor_tensor(gain[:, i, :], modv[:, at:at + 8], 1.0, V(g), ALU.add, ALU.mult).then_inc(signal("dve_step"), 1)
                dve.wait_ge(sem("dve_step"), signalled("dve_step"))

        def mod(at):
            return modv[:, at:at + 8]

        def exp_dve(dve, dst, x, tmp, tmp2):
            k = tmp.bitcast(I32)
            dve.tensor_scalar(k, x, 1.0 / LN2, None, ALU.mult).then_inc(signal("dve_step"), 1)
            dve.wait_ge(sem("dve_step"), signalled("dve_step"))
            dve.tensor_copy(tmp2, k).then_inc(signal("dve_step"), 1)
            dve.wait_ge(sem("dve_step"), signalled("dve_step"))
            dve.scalar_tensor_tensor(x, tmp2, -LN2_HI, x, ALU.mult, ALU.add).then_inc(signal("dve_step"), 1)
            dve.wait_ge(sem("dve_step"), signalled("dve_step"))
            dve.scalar_tensor_tensor(x, tmp2, -LN2_LO, x, ALU.mult, ALU.add).then_inc(signal("dve_step"), 1)
            dve.wait_ge(sem("dve_step"), signalled("dve_step"))
            dve.tensor_scalar(k, tmp2, 127.0, None, ALU.add).then_inc(signal("dve_step"), 1)
            dve.wait_ge(sem("dve_step"), signalled("dve_step"))
            dve.tensor_scalar(k, k, 23, None, ALU.logical_shift_left).then_inc(signal("dve_step"), 1)
            dve.wait_ge(sem("dve_step"), signalled("dve_step"))
            c = [1.0]
            for i in range(1, 9):
                c.append(c[-1] / i)
            dve.tensor_scalar(dst, x, c[8], None, ALU.mult).then_inc(signal("dve_step"), 1)
            dve.wait_ge(sem("dve_step"), signalled("dve_step"))
            for i in range(7, 0, -1):
                dve.scalar_tensor_tensor(dst, dst, c[i], x, ALU.add, ALU.mult).then_inc(signal("dve_step"), 1)
                dve.wait_ge(sem("dve_step"), signalled("dve_step"))
            dve.scalar_tensor_tensor(dst, dst, 1.0, tmp, ALU.add, ALU.mult).then_inc(signal("dve_step"), 1)
            dve.wait_ge(sem("dve_step"), signalled("dve_step"))

        def gla_dve(dve):
            for h in range(GH):
                dve.wait_ge(full_sem(f"g_z{h}"), filled(f"g_z{h}"))
                t = tile_of(f"g_z{h}")
                dve.tensor_scalar(G.z[:, h, :], t[:, 0:T], V("gla_b")[:, h:h + 1], None, ALU.add).then_inc(free_sem(f"g_z{h}"), 1)
                dve.wait_ge(free_sem(f"g_z{h}"), freed(f"g_z{h}"))
            dve.scalar_tensor_tensor(G.e, G.z, -1.0, G.z, ALU.mult, ALU.min).then_inc(signal("g_abs"), 1)
            dve.wait_ge(sem("g_abs"), signalled("g_abs"))
            dve.wait_ge(sem("g_ln"), 1)
            dve.scalar_tensor_tensor(G.z, G.z, 0.0, G.e, ALU.min, ALU.add).then_inc(signal("dve_step"), 1)
            dve.wait_ge(sem("dve_step"), signalled("dve_step"))
            for h in range(GH):
                dve.tensor_tensor_scan(G.b[:, h, :], C("scan"), G.z[:, h, :], 0.0, ALU.mult, ALU.add).then_inc(signal("dve_step"), 1)
                dve.wait_ge(sem("dve_step"), signalled("dve_step"))
            dve.tensor_scalar(G.b, G.b, 1.0 / TAU, -87.0, ALU.mult, ALU.max).then_inc(signal("dve_step"), 1)
            dve.wait_ge(sem("dve_step"), signalled("dve_step"))
            exp_dve(dve, G.z, G.b, G.e, G.e2)
            dve.reciprocal(G.e, G.z).then_inc(signal("dve_step"), 1)
            dve.wait_ge(sem("dve_step"), signalled("dve_step"))
            dve.wait_ge(free_sem("g_k3"), freed("g_k3"))
            dve.tensor_tensor(G.k, G.k, G.e, ALU.mult).then_inc(signal("g_kq"), 1)
            dve.wait_ge(sem("g_kq"), signalled("g_kq"))
            k4 = G.k.rearrange("p h (n c) -> p (h n) c", c=GC)
            kd4 = G.kd.rearrange("p h (n c) -> p (h n) c", c=GC)
            z4 = G.z.rearrange("p h (n c) -> p (h n) c", c=GC)
            dve.tensor_copy(G.dec.rearrange("p h n -> p (h n)"), z4[:, :, GC - 1]).then_inc(signal("dve_step"), 1)
            dve.wait_ge(sem("dve_step"), signalled("dve_step"))
            dve.tensor_tensor(kd4, k4, z4[:, :, GC - 1:GC].broadcast_to([P, GH * NCH, GC]), ALU.mult).then_inc(signal("g_kd"), 1)
            dve.wait_ge(sem("g_kd"), signalled("g_kd"))
            dve.scalar_tensor_tensor(G.q, G.q, float(P) ** -0.5, G.z, ALU.mult, ALU.mult).then_inc(signal("g_kq"), 1)
            dve.wait_ge(sem("g_kq"), signalled("g_kq"))
            dve.wait_ge(sem("g_sig"), 1)
            dve.tensor_tensor(G.og, G.og, G.o, ALU.mult).then_inc(signal("dve_step"), 1)
            dve.wait_ge(sem("dve_step"), signalled("dve_step"))
            for h in range(GH):
                dve.wait_ge(full_sem(f"g_s{h}"), filled(f"g_s{h}"))
                t = tile_of(f"g_s{h}")
                dve.tensor_tensor(G.sm[:, h, :].rearrange("p (b t) -> p b t", b=2),
                                               t[:, 0:T].rearrange("p (b t) -> p b t", b=2),
                                               C("gmask").unsqueeze(1).broadcast_to([P, 2, P]), ALU.mult).then_inc(free_sem(f"g_s{h}"), 1)
                dve.wait_ge(free_sem(f"g_s{h}"), freed(f"g_s{h}"))
            for n in range(NCH - 1):
                for h in range(GH):
                    dve.wait_ge(full_sem(f"g_u{n}{h}"), filled(f"g_u{n}{h}"))
                    t = tile_of(f"g_u{n}{h}")
                    new = G.st[:, h, (n + 1) % 2, :]
                    if n == 0:
                        ins = dve.tensor_copy(new, t[:, 0:GDV])
                    else:
                        ins = dve.scalar_tensor_tensor(new, G.st[:, h, n % 2, :], G.dec[:, h, n:n + 1], t[:, 0:GDV],
                                                       ALU.mult, ALU.add)
                    ins.then_inc(free_sem(f"g_u{n}{h}"), 1)
                    dve.wait_ge(free_sem(f"g_u{n}{h}"), freed(f"g_u{n}{h}"))
                    dve.sem_inc(sem("g_state"), 1)
            inv_root_dve(dve, "g", G.r, [(f"g_ss{h}", G.r[:, h, :]) for h in range(GH)], GDV)
            for h in range(GH):
                for e in range(2):
                    dve.scalar_tensor_tensor(G.o[:, 2 * h + e, :], bank[4 + h][:, e * T:(e + 1) * T],
                                                        V("gla_ng")[:, e:e + 1], G.r[:, h, :], ALU.mult, ALU.mult).then_inc(signal("dve_step"), 1)
                    dve.wait_ge(sem("dve_step"), signalled("dve_step"))
            dve.tensor_tensor(G.o, G.o, G.og, ALU.mult).then_inc(signal("g_y"), 1)
            dve.wait_ge(sem("g_y"), signalled("g_y"))
            update_dve(dve, "g_out", mod(16))

        def peer_dve(dve, l):
            n = f"p{l}"
            iota16 = iota[:, 0:TOPK]
            for a in range(TT):
                v, ix, ixf = R.v[:, a], R.ix[:, a].bitcast(U32), R.ixf[:, a]
                for g in range(16):
                    if g % 2 == 0:
                        dve.wait_ge(free_sem(f"{n}_s{a}{g // 2}"), freed(f"{n}_s{a}{g // 2}"))
                    ins = dve.max(v[:, g, 0:8], R.s[:, a, g, :])
                ins.then_inc(signal("dve_step"), 1)
                dve.wait_ge(sem("dve_step"), signalled("dve_step"))
                for g in range(16):
                    dve.max_index(ix[:, g, 0:8], v[:, g, 0:8], R.s[:, a, g, :])
                    ins = dve.match_replace(R.s2[:, g, :], v[:, g, 0:8], R.s[:, a, g, :], LOW)
                ins.then_inc(signal("dve_step"), 1)
                dve.wait_ge(sem("dve_step"), signalled("dve_step"))
                for g in range(16):
                    ins = dve.max(v[:, g, 8:16], R.s2[:, g, :])
                ins.then_inc(signal("dve_step"), 1)
                dve.wait_ge(sem("dve_step"), signalled("dve_step"))
                for g in range(16):
                    ins = dve.max_index(ix[:, g, 8:16], v[:, g, 8:16], R.s2[:, g, :])
                ins.then_inc(signal("dve_step"), 1)
                dve.wait_ge(sem("dve_step"), signalled("dve_step"))
                dve.tensor_copy(ixf, ix).then_inc(signal("dve_step"), 1)
                dve.wait_ge(sem("dve_step"), signalled("dve_step"))
                v4 = v.rearrange("p (h f) k -> p h f k", f=2)
                i4 = ixf.rearrange("p (h f) k -> p h f k", f=2)
                c4 = R.cand.rearrange("p h (x y) -> p h x y", x=TOPK)
                dve.tensor_tensor(c4, v4[:, :, 0, :].unsqueeze(3).broadcast_to([P, PH, TOPK, TOPK]),
                                             v4[:, :, 1, :].unsqueeze(2).broadcast_to([P, PH, TOPK, TOPK]), ALU.add).then_inc(signal("dve_step"), 1)
                dve.wait_ge(sem("dve_step"), signalled("dve_step"))
                ci = R.ci.bitcast(U32)
                if a:
                    dve.wait_ge(sem(f"{n}_ecs"), a)
                for h in range(PH):
                    ins = dve.max(R.cs[:, h, 0:8], R.cand[:, h, :])
                ins.then_inc(signal("dve_step"), 1)
                dve.wait_ge(sem("dve_step"), signalled("dve_step"))
                for h in range(PH):
                    dve.max_index(ci[:, h, 0:8], R.cs[:, h, 0:8], R.cand[:, h, :])
                    ins = dve.match_replace(R.cand2[:, h, :], R.cs[:, h, 0:8], R.cand[:, h, :], LOW)
                ins.then_inc(signal("dve_step"), 1)
                dve.wait_ge(sem("dve_step"), signalled("dve_step"))
                for h in range(PH):
                    ins = dve.max(R.cs[:, h, 8:16], R.cand2[:, h, :])
                ins.then_inc(signal("dve_step"), 1)
                dve.wait_ge(sem("dve_step"), signalled("dve_step"))
                for h in range(PH):
                    ins = dve.max_index(ci[:, h, 8:16], R.cs[:, h, 8:16], R.cand2[:, h, :])
                ins.then_inc(signal("dve_step"), 1)
                dve.wait_ge(sem("dve_step"), signalled("dve_step"))
                dve.tensor_copy(R.sum[:, 0:8], R.cs[:, :, 0]).then_inc(signal("dve_step"), 1)
                dve.wait_ge(sem("dve_step"), signalled("dve_step"))
                dve.tensor_tensor(R.cs, R.cs, R.sum[:, 0:8].unsqueeze(2).broadcast_to([P, PH, TOPK]),
                                            ALU.subtract).then_inc(signal(f"{n}_cs"), 1)
                dve.wait_ge(sem(f"{n}_cs"), signalled(f"{n}_cs"))
                cif = R.ci.rearrange("p h k -> p (h k)").bitcast(U32)
                dve.tensor_scalar(R.ca.bitcast(U32), cif, 4, None, ALU.logical_shift_right).then_inc(signal("dve_step"), 1)
                dve.wait_ge(sem("dve_step"), signalled("dve_step"))
                dve.tensor_scalar(R.cb.bitcast(U32), cif, 15, None, ALU.bitwise_and).then_inc(signal("dve_step"), 1)
                dve.wait_ge(sem("dve_step"), signalled("dve_step"))
                dve.tensor_copy(R.caf, R.ca.bitcast(U32)).then_inc(signal("dve_step"), 1)
                dve.wait_ge(sem("dve_step"), signalled("dve_step"))
                dve.tensor_copy(R.cbf, R.cb.bitcast(U32)).then_inc(signal("dve_step"), 1)
                dve.wait_ge(sem("dve_step"), signalled("dve_step"))
                for f, (rank, wide) in enumerate(((R.caf, R.cand), (R.cbf, R.cand2))):
                    w3 = wide.rearrange("p h (k x) -> p (h k) x", x=TOPK)
                    w4 = wide.rearrange("p h (k x) -> p h k x", x=TOPK)
                    dve.tensor_tensor(w3, rank.unsqueeze(2).broadcast_to([P, P, TOPK]),
                                                 iota16.unsqueeze(1).broadcast_to([P, P, TOPK]), ALU.is_equal).then_inc(signal("dve_step"), 1)
                    dve.wait_ge(sem("dve_step"), signalled("dve_step"))
                    dve.tensor_tensor(w4, w4, i4[:, :, f, :].unsqueeze(2).broadcast_to(
                        [P, PH, TOPK, TOPK]), ALU.mult).then_inc(signal("dve_step"), 1)
                    dve.wait_ge(sem("dve_step"), signalled("dve_step"))
                    dve.tensor_reduce(R.pick[:, a, f, :], w3, AX.X, ALU.add).then_inc(signal("dve_step"), 1)
                    dve.wait_ge(sem("dve_step"), signalled("dve_step"))
                dve.wait_ge(sem(f"{n}_ecs"), a + 1)
                dve.tensor_reduce(R.sum[:, 0:8], R.cs, AX.X, ALU.add).then_inc(signal("dve_step"), 1)
                dve.wait_ge(sem("dve_step"), signalled("dve_step"))
                dve.reciprocal(R.sum[:, 8:16], R.sum[:, 0:8]).then_inc(signal("dve_step"), 1)
                dve.wait_ge(sem("dve_step"), signalled("dve_step"))
                dve.tensor_tensor(R.pick[:, a, 2, :].rearrange("p (h k) -> p h k", h=PH), R.cs,
                                            R.sum[:, 8:16].unsqueeze(2).broadcast_to([P, PH, TOPK]), ALU.mult).then_inc(signal(f"{n}_picked"), 1)
                dve.wait_ge(sem(f"{n}_picked"), signalled(f"{n}_picked"))
            for a in range(TT):
                dve.wait_ge(full_sem(f"{n}_rt{a}"), filled(f"{n}_rt{a}"))
                t = tile_of(f"{n}_rt{a}")
                dve.tensor_copy(route[:, :, a * P:(a + 1) * P],
                                             t[:, 0:384].rearrange("p (k t) -> p k t", k=3)).then_inc(free_sem(f"{n}_rt{a}"), 1)
                dve.wait_ge(free_sem(f"{n}_rt{a}"), freed(f"{n}_rt{a}"))
            with dve.Fori(0, T // 8) as it:
                for s in range(8):
                    dve.wait_ge(sem(f"{n}_hot_free"), it * 8 + (s + 1))
                    tok = bass.ds(it * 8 + s, 1)
                    dve.tensor_scalar(hot[:, s, 0, :], iota, route[:, 1, tok], None, ALU.is_equal)
                    dve.tensor_scalar(hot[:, s, 1, :], iota, route[:, 0, tok], route[:, 2, tok],
                                      ALU.is_equal, ALU.mult).then_inc(sem(f"{n}_hot"), 1)
            dve.wait_ge(sem(f"{n}_table_free"), 2 + T // 4)
            with dve.Fori(0, NK // 4) as it:
                for k in range(4):
                    dve.wait_ge(sem(f"{n}_gelu"), it * 4 + (k + 1))
                    dve.tensor_tensor(act_g[:, k, :], act_u[:, k % 2, :],
                                      W[:, bass.ds(it * 4 + k, 1), :].rearrange("p i t -> p (i t)"),
                                      ALU.mult).then_inc(sem(f"{n}_gated"), 1)
            update_dve(dve, f"{n}_y", mod(40 + 48 * l))

        def attention_dve(dve, n, heads, scale, mask, sinks, outp):
            for h in range(heads):
                dve.wait_ge(full_sem(f"{n}_s{h}"), filled(f"{n}_s{h}"))
                t = tile_of(f"{n}_s{h}")
                dve.scalar_tensor_tensor(A.p[:, h, :], t[:, 0:384], scale, mask, ALU.mult, ALU.add).then_inc(free_sem(f"{n}_s{h}"), 1)
                dve.wait_ge(free_sem(f"{n}_s{h}"), freed(f"{n}_s{h}"))
            dve.tensor_reduce(A.m[:, 0, 0:heads], A.p[:, 0:heads, 0:P], AX.X, ALU.max).then_inc(signal("dve_step"), 1)
            dve.wait_ge(sem("dve_step"), signalled("dve_step"))
            dve.tensor_reduce(A.m[:, 1, 0:heads], A.p[:, 0:heads, P:3 * P], AX.X, ALU.max).then_inc(signal("dve_step"), 1)
            dve.wait_ge(sem("dve_step"), signalled("dve_step"))
            if sinks is not None:
                sk = sinks.unsqueeze(1).broadcast_to([P, 2, heads])
                dve.tensor_tensor(A.m, A.m, sk, ALU.max).then_inc(signal("dve_step"), 1)
                dve.wait_ge(sem("dve_step"), signalled("dve_step"))
                dve.tensor_scalar(A.x, A.m, -1.0, None, ALU.mult).then_inc(signal("dve_step"), 1)
                dve.wait_ge(sem("dve_step"), signalled("dve_step"))
                dve.tensor_tensor(A.m, sk, A.m, ALU.subtract).then_inc(signal("dve_step"), 1)
                dve.wait_ge(sem("dve_step"), signalled("dve_step"))
            else:
                dve.tensor_scalar(A.x[:, :, 0:heads], A.m[:, :, 0:heads], -1.0, None, ALU.mult).then_inc(signal("dve_step"), 1)
                dve.wait_ge(sem("dve_step"), signalled("dve_step"))
            dve.sem_inc(sem(f"{n}_max"), 1)
            dve.wait_ge(sem(f"{n}_exp"), heads)
            if sinks is not None:
                dve.wait_ge(sem("w_sink"), 1)
                dve.tensor_tensor(A.l, A.l, A.m, ALU.add).then_inc(signal("dve_step"), 1)
                dve.wait_ge(sem("dve_step"), signalled("dve_step"))
            dve.reciprocal(A.l[:, :, 0:heads], A.l[:, :, 0:heads]).then_inc(signal("dve_step"), 1)
            dve.wait_ge(sem("dve_step"), signalled("dve_step"))
            for h in range(heads):
                for b, cols in ((0, slice(0, P)), (1, slice(P, 3 * P))):
                    ins = dve.tensor_scalar(A.p[:, h, cols], A.p[:, h, cols], A.l[:, b, h:h + 1], None, ALU.mult)
                ins.then_inc(signal(f"{n}_p"), 1)
                dve.wait_ge(sem(f"{n}_p"), signalled(f"{n}_p"))
            for h in range(heads):
                dve.wait_ge(full_sem(f"{n}_o{h}"), filled(f"{n}_o{h}"))
                t = tile_of(f"{n}_o{h}")
                outp(h, t).then_inc(free_sem(f"{n}_o{h}"), 1)
                dve.wait_ge(free_sem(f"{n}_o{h}"), freed(f"{n}_o{h}"))

        def rotate_dve(dve, x, tile, cos, sin, tmp, name):
            dve.wait_ge(full_sem(tile), filled(tile))
            t = tile_of(tile)
            dve.tensor_tensor(tmp, t[:, 0:T], sin, ALU.mult).then_inc(free_sem(tile), 1)
            dve.wait_ge(free_sem(tile), freed(tile))
            dve.tensor_tensor(x, x, cos, ALU.mult).then_inc(signal("dve_step"), 1)
            dve.wait_ge(sem("dve_step"), signalled("dve_step"))
            dve.tensor_tensor(x, x, tmp, ALU.add).then_inc(signal(name), 1)
            dve.wait_ge(sem(name), signalled(name))

        def swa_dve(dve):
            for k in range(4):
                rotate_dve(dve, S.k[:, k, :], f"kv_r{k}", rope_c[:, :], rope_s[:, :], S.tmp, "w_kr")
            norm_dve(dve, "1a", gain[:, 2, :], mod(48))
            for c in range(DC):
                rotate_dve(dve, S.q[:, c, :], f"w_r{c}", rope_c[:, :], rope_s[:, :], S.tmp, "w_qr")

            def outp(h, t):
                rows = slice((h % 2) * SHD, (h % 2 + 1) * SHD)
                return dve.tensor_copy(A.o[rows, h // 2, :], t[rows, 0:T])

            attention_dve(dve, "w", SH, SHD ** -0.5, C("smask"), V("sinks"), outp)
            update_dve(dve, "w_out", mod(48 + 16))

        def mix_dve(dve):
            dve.wait_ge(sem("loaded2"), 16)
            c2 = lambda name: M.cst[:, C2O[name][0]:C2O[name][1]]
            cosb = c2("rcos").unsqueeze(1).broadcast_to([P, RH, T])
            sinb = c2("rsin").unsqueeze(1).broadcast_to([P, RH, T])
            for name, x in (("q", M.q), ("k", M.k)):
                dve.wait_ge(free_sem(f"r_{name}6"), freed(f"r_{name}6"))
                dve.wait_ge(free_sem(f"r_{name}7"), freed(f"r_{name}7"))
                x4 = x.rearrange("p (h f) t -> p h f t", f=2)
                x1, x2 = x4[:, :, 0, :], x4[:, :, 1, :]
                t1, t2 = M.t[:, 0:4, :], M.t[:, 4:8, :]
                dve.tensor_tensor(t1, x2, sinb, ALU.mult).then_inc(signal("dve_step"), 1)
                dve.wait_ge(sem("dve_step"), signalled("dve_step"))
                dve.tensor_tensor(t2, x1, sinb, ALU.mult).then_inc(signal("dve_step"), 1)
                dve.wait_ge(sem("dve_step"), signalled("dve_step"))
                dve.tensor_tensor(x1, x1, cosb, ALU.mult).then_inc(signal("dve_step"), 1)
                dve.wait_ge(sem("dve_step"), signalled("dve_step"))
                dve.tensor_tensor(x2, x2, cosb, ALU.mult).then_inc(signal("dve_step"), 1)
                dve.wait_ge(sem("dve_step"), signalled("dve_step"))
                dve.tensor_tensor(x1, x1, t1, ALU.subtract).then_inc(signal("r_rot"), 1)
                dve.wait_ge(sem("r_rot"), signalled("r_rot"))
                dve.tensor_tensor(x2, x2, t2, ALU.add).then_inc(signal("r_rot"), 1)
                dve.wait_ge(sem("r_rot"), signalled("r_rot"))
            dec = c2("decay").rearrange("p (h t) -> p h t", h=RH)
            for h in range(RH):
                dve.wait_ge(full_sem(f"r_s{h}"), filled(f"r_s{h}"))
                t = tile_of(f"r_s{h}")
                dve.scalar_tensor_tensor(M.s[:, h, :], t[:, 0:384], 256.0 ** -0.5, dec[:, h, :],
                                                      ALU.mult, ALU.mult).then_inc(free_sem(f"r_s{h}"), 1)
                dve.wait_ge(free_sem(f"r_s{h}"), freed(f"r_s{h}"))
            for h in range(RH):
                dve.wait_ge(full_sem(f"r_mean{h}"), filled(f"r_mean{h}"))
                t = tile_of(f"r_mean{h}")
                y = M.y[:, 2 * h:2 * h + 2, :]
                dve.scalar_tensor_tensor(y, t[:, 0:T].unsqueeze(1).broadcast_to([P, 2, T]), -1.0 / 256, y,
                                                      ALU.mult, ALU.add).then_inc(free_sem(f"r_mean{h}"), 1)
                dve.wait_ge(free_sem(f"r_mean{h}"), freed(f"r_mean{h}"))
                dve.sem_inc(sem("r_cent"), 1)
            inv_root_dve(dve, "r", M.r, [(f"r_var{h}", M.r[:, h, :]) for h in range(RH)], 256)
            y4 = M.y.rearrange("p (h f) t -> p h f t", f=2)
            for f in range(2):
                dve.tensor_tensor(y4[:, :, f, :], y4[:, :, f, :], M.r, ALU.mult).then_inc(signal("dve_step"), 1)
                dve.wait_ge(sem("dve_step"), signalled("dve_step"))
            dve.wait_ge(free_sem("r_g7"), freed("r_g7"))
            dve.tensor_tensor(M.y, M.y, M.g, ALU.mult).then_inc(signal("r_yn"), 1)
            dve.wait_ge(sem("r_yn"), signalled("r_yn"))
            inv_root_dve(dve, "cq", rs[:, :], [("ncq_ss", rs[:, :])], QL)
            for c in range(3):
                dve.scalar_tensor_tensor(M.cq[:, c, :], M.cq[:, c, :], V("qn")[:, c:c + 1], rs[:, :],
                                                   ALU.mult, ALU.mult).then_inc(signal("m_cqn"), 1)
                dve.wait_ge(sem("m_cqn"), signalled("m_cqn"))
            inv_root_dve(dve, "ckv", G2.r2, [("nckv_ss", G2.r2)], KVL)
            for c in range(2):
                dve.scalar_tensor_tensor(M.ckv[:, c, :], M.ckv[:, c, :], V("kvn")[:, c:c + 1], G2.r2,
                                                   ALU.mult, ALU.mult).then_inc(signal("m_ckvn"), 1)
                dve.wait_ge(sem("m_ckvn"), signalled("m_ckvn"))
            for c in range(DC):
                dve.wait_ge(full_sem(f"r_o{c}"), filled(f"r_o{c}"))
                t = tile_of(f"r_o{c}")
                dve.tensor_tensor(M.gr[:, c, :], t[:, 0:T], M.gr[:, c, :], ALU.mult).then_inc(free_sem(f"r_o{c}"), 1)
                dve.wait_ge(free_sem(f"r_o{c}"), freed(f"r_o{c}"))
            for c in range(5):
                rotate_dve(dve, M.qp[:, c, :] if c < 4 else M.kp[:, 0, :], f"m_r{c}", c2("mcos"), c2("msin"),
                           M.t[:, 0, :], "m_rot0" if c == 4 else "m_rot")
            for f in range(2):
                dve.tensor_scalar(M.kp[:, 1 + f, :], M.kp[:, 0, :], C("cols")[:, 2 + f:3 + f], None,
                                            ALU.mult).then_inc(signal("m_rot"), 1)
                dve.wait_ge(sem("m_rot"), signalled("m_rot"))

            def outp(h, t):
                return dve.tensor_copy(A.o[:, h, :], t[:, 0:T])

            attention_dve(dve, "m", MH, float(192) ** -0.5, c2("mmask"), None, outp)
            for c in range(DC):
                dve.wait_ge(full_sem(f"m_out{c}"), filled(f"m_out{c}"))
                t = tile_of(f"m_out{c}")
                dve.tensor_tensor(M.gm[:, c, :], t[:, 0:T], M.gm[:, c, :], ALU.mult).then_inc(free_sem(f"m_out{c}"), 1)
                dve.wait_ge(free_sem(f"m_out{c}"), freed(f"m_out{c}"))
            dve.tensor_tensor(M.mg, M.gr, M.gm, ALU.add).then_inc(signal("merged"), 1)
            dve.wait_ge(sem("merged"), signalled("merged"))
            update_dve(dve, "mix", mod(112 + 16))

        def moe_dve(dve):
            dve.memset(E.g8, LOW).then_inc(signal("dve_step"), 1)
            dve.wait_ge(sem("dve_step"), signalled("dve_step"))
            for a in range(TT):
                dve.wait_ge(full_sem(f"e_l{a}"), filled(f"e_l{a}"))
                t = tile_of(f"e_l{a}")
                dve.tensor_tensor(E.l[:, a, :], t[:, 0:NG + NE], V("rb"), ALU.add).then_inc(free_sem(f"e_l{a}"), 1)
                dve.wait_ge(free_sem(f"e_l{a}"), freed(f"e_l{a}"))
            dve.tensor_copy(E.g8[:, :, 0:NG], E.l[:, :, 0:NG]).then_inc(signal("dve_step"), 1)
            dve.wait_ge(sem("dve_step"), signalled("dve_step"))
            i8 = E.i8.bitcast(U32)

            def top(src):
                for a in range(TT):
                    ins = dve.max(E.m8[:, a, :], src[:, a, :])
                ins.then_inc(signal("dve_step"), 1)
                dve.wait_ge(sem("dve_step"), signalled("dve_step"))
                for a in range(TT):
                    ins = dve.max_index(i8[:, a, :], E.m8[:, a, :], src[:, a, :])
                ins.then_inc(signal("dve_step"), 1)
                dve.wait_ge(sem("dve_step"), signalled("dve_step"))
                dve.tensor_copy(E.if8, i8).then_inc(signal("dve_step"), 1)
                dve.wait_ge(sem("dve_step"), signalled("dve_step"))

            def iota_b(k):
                return iota[:, 0:k].unsqueeze(1).broadcast_to([P, TT, k])

            def bc(ap, k):
                return ap.broadcast_to([P, TT, k])

            top(E.g8)
            dve.tensor_tensor(E.oh, bc(E.if8[:, :, 0:1], NG), iota_b(NG), ALU.is_equal).then_inc(signal("dve_step"), 1)
            dve.wait_ge(sem("dve_step"), signalled("dve_step"))
            dve.tensor_tensor(E.x8, E.g8, bc(E.m8[:, :, 0:1], 8), ALU.subtract).then_inc(signal("e_gx"), 1)
            dve.wait_ge(sem("e_gx"), signalled("e_gx"))
            t4 = E.tmp.rearrange("p a (g e) -> p a g e", g=NG)
            l4 = E.l[:, :, NG:NG + NE].rearrange("p a (g e) -> p a g e", g=NG)
            dve.tensor_tensor(t4, l4, E.oh.unsqueeze(3).broadcast_to([P, TT, NG, EG]), ALU.mult).then_inc(signal("dve_step"), 1)
            dve.wait_ge(sem("dve_step"), signalled("dve_step"))
            dve.tensor_reduce(E.g8, E.tmp.rearrange("p a (g e) -> p a e g", g=NG), AX.X, ALU.add).then_inc(signal("dve_step"), 1)
            dve.wait_ge(sem("dve_step"), signalled("dve_step"))
            top(E.g8)
            dve.tensor_tensor(E.w[:, :, 0:1], E.m8[:, :, 1:2], E.m8[:, :, 0:1], ALU.subtract).then_inc(signal("e_vx"), 1)
            dve.wait_ge(sem("e_vx"), signalled("e_vx"))
            dve.wait_ge(sem("e_gexp"), 1)
            dve.tensor_reduce(E.w[:, :, 1:2], E.x8[:, :, 0:NG], AX.X, ALU.add).then_inc(signal("dve_step"), 1)
            dve.wait_ge(sem("dve_step"), signalled("dve_step"))
            dve.wait_ge(sem("e_vexp"), 1)
            dve.scalar_tensor_tensor(E.w[:, :, 4:5], E.w[:, :, 0:1], 1.0, E.w[:, :, 1:2], ALU.add, ALU.mult).then_inc(signal("dve_step"), 1)
            dve.wait_ge(sem("dve_step"), signalled("dve_step"))
            dve.reciprocal(E.w[:, :, 2:3], E.w[:, :, 4:5]).then_inc(signal("dve_step"), 1)
            dve.wait_ge(sem("dve_step"), signalled("dve_step"))
            dve.tensor_tensor(E.w[:, :, 3:4], E.w[:, :, 0:1], E.w[:, :, 2:3], ALU.mult).then_inc(signal("dve_step"), 1)
            dve.wait_ge(sem("dve_step"), signalled("dve_step"))
            for k, dst in ((0, E.ew), (1, E.ew2)):
                dve.tensor_tensor(dst, bc(E.if8[:, :, k:k + 1], EG), iota_b(EG), ALU.is_equal).then_inc(signal("dve_step"), 1)
                dve.wait_ge(sem("dve_step"), signalled("dve_step"))
                dve.tensor_tensor(dst, dst, bc(E.w[:, :, 2 + k:3 + k], EG), ALU.mult).then_inc(signal("dve_step"), 1)
                dve.wait_ge(sem("dve_step"), signalled("dve_step"))
            dve.tensor_tensor(E.ew, E.ew, E.ew2, ALU.add).then_inc(signal("dve_step"), 1)
            dve.wait_ge(sem("dve_step"), signalled("dve_step"))
            dve.tensor_tensor(E.gate.rearrange("p a (g e) -> p a g e", g=NG),
                                        E.oh.unsqueeze(3).broadcast_to([P, TT, NG, EG]),
                                        E.ew.unsqueeze(2).broadcast_to([P, TT, NG, EG]), ALU.mult).then_inc(signal("e_gate"), 1)
            dve.wait_ge(sem("e_gate"), signalled("e_gate"))
            for e in range(NE // 2 - 4, NE // 2):
                dve.wait_ge(free_sem(f"e_b{e}"), freed(f"e_b{e}"))
            with dve.Fori(0, NE // 2) as it:
                for s in range(2):
                    dve.wait_ge(sem("e_silu"), it * 2 + (s + 1))
                    dve.tensor_tensor(E.hp[:, s, :], E.sa[:, s, :], bank[2 * s + 1][:, :], ALU.mult)\
                       .then_inc(sem("e_prod"), 1)
                    dve.wait_ge(sem("e_prod"), it * 2 + (s + 1))
                    dve.tensor_tensor(E.hid[:, s, :, :], E.hp[:, s, :].rearrange("p (f t) -> p f t", f=2),
                                      E.gb[:, bass.ds(it * 2 + s, 1), :].broadcast_to([P, 2, T]), ALU.mult)\
                       .then_inc(sem("e_hid"), 1)
            update_dve(dve, "e_y", mod(112 + 40))

        @block.vector
        def _(dve):
            dve.wait_ge(sem("loaded"), 16 * N_LOADS)
            mod_dve(dve)
            norm_dve(dve, "0a", gain[:, 0, :], mod(0))
            gla_dve(dve)
            norm_dve(dve, "0b", gain[:, 1, :], mod(24))
            peer_dve(dve, 0)
            norm_dve(dve, "kv", gain[:, 4, :], mod(96))
            swa_dve(dve)
            norm_dve(dve, "1b", gain[:, 3, :], mod(72))
            peer_dve(dve, 1)
            norm_dve(dve, "mid", V("fing"), None, xT)
            norm_dve(dve, "2a", gain[:, 5, :], mod(112))
            mix_dve(dve)
            norm_dve(dve, "2b", gain[:, 6, :], mod(136))
            moe_dve(dve)
            norm_dve(dve, "out", V("fin2"), None, None)


def slots_out_features(w, tiles=None):
    k, m = w.shape
    return w.reshape(k // P, P, m // P, P).transpose(2, 1, 0, 3).reshape(m // P, P, k)


def slots_tokens(w):
    k, m = w.shape
    return w.reshape(k // 256, 2, P, m // 512, 512).transpose(3, 0, 2, 1, 4).reshape(-1, P, CH)


def pad(a):
    out = np.zeros((a.shape[0], P, CH), np.float32)
    out[:, :, :a.shape[2]] = a
    return out


def layout(x):
    S = {}
    mods = [x["mod_w"][0], x["mod_w"][1], x["kv_mod_w"], x["w_ada_2"][0]]
    S["mod"] = np.concatenate([slots_out_features(w) for w in mods])
    w = x["gla_w_in"][0]
    gl = np.zeros((D, P), np.float32)
    gl[:, :RANK] = w[:, 3072:3088]
    S["gla_gl"] = slots_out_features(gl)
    S["gla_q"], S["gla_k"] = slots_out_features(w[:, 0:512]), slots_out_features(w[:, 512:1024])
    S["gla_v"], S["gla_og"] = slots_tokens(w[:, 1024:2048]), slots_out_features(w[:, 2048:3072])
    S["gla_out"] = slots_out_features(x["gla_w_out"][0])
    for l in range(2):
        S[f"peer{l}_q"] = slots_out_features(x["peer_w_q"][l])
        uv = np.empty((2 * NK, P, CH), np.float32)
        u = x["peer_u"][l].reshape(NK, P, DC, P).transpose(0, 3, 2, 1).reshape(NK, P, CH)
        v = x["peer_v"][l].reshape(NK, P, CH)
        uv[0], uv[1:-1:2], uv[2::2], uv[-1] = u[0], u[1:], v[:-1], v[-1]
        S[f"peer{l}_uv"] = uv
    w = x["kv_w"].reshape(D, 2, SKV, 1, SHD)
    w = np.broadcast_to(w, (D, 2, SKV, 2, SHD))
    S["kv_k"], S["kv_v"] = slots_out_features(w[:, 0].reshape(D, 512)), slots_tokens(w[:, 1].reshape(D, 512))
    S["swa_q"], S["swa_out"] = slots_out_features(x["swa_w_q"][0]), slots_out_features(x["swa_w_out"][0])
    w = x["w_in_2"][0]
    S["ret_q"], S["ret_k"] = slots_out_features(w[:, 0:1024]), slots_out_features(w[:, 1024:2048])
    S["ret_v"], S["ret_g"] = slots_tokens(w[:, 2048:3072]), slots_out_features(w[:, 3072:4096])
    S["mla_cq"], S["mla_ckv"] = slots_out_features(w[:, 4096:4480]), slots_out_features(w[:, 4480:4736])
    S["mla_kpe"] = slots_out_features(np.concatenate([w[:, 4736:4800]] * 2, 1))
    S["gate_r"], S["gate_m"] = slots_out_features(w[:, 4800:5824]), slots_out_features(w[:, 5824:6848])
    S["ret_o"], S["mla_o"] = slots_out_features(x["w_ret_o_2"][0]), slots_out_features(x["w_mla_o_2"][0])
    S["mix_out"] = slots_out_features(x["w_out_2"][0])
    w = x["w_uq_2"][0].reshape(QL, MH, 192)
    w = np.concatenate([w[:, :, :P].reshape(QL, -1), w[:, :, P:].reshape(QL, -1)], 1)
    S["mla_uq"] = pad(slots_out_features(w).reshape(6, 2, P, QL).transpose(0, 2, 1, 3).reshape(6, P, 2 * QL))
    w = x["w_ukv_2"][0].reshape(KVL, MH, 2, P)
    S["mla_uk"] = slots_out_features(w[:, :, 0].reshape(KVL, D)).reshape(2, 4, P, KVL).transpose(0, 2, 1, 3)\
        .reshape(2, P, CH)
    S["mla_uv"] = w[:, :, 1].reshape(2, P, 2, 512).transpose(2, 1, 0, 3).reshape(2, P, CH)
    r = np.zeros((D, P), np.float32)
    r[:, :NG], r[:, NG:NG + NE] = x["w_grp_2"][0], x["w_exp_2"][0]
    S["router"] = slots_out_features(r)
    w1 = x["w1_2"][0].reshape(NE, DC, P, 2, P).transpose(0, 3, 2, 1, 4).reshape(NE, 2, P, CH)
    w3 = x["w3_2"][0].reshape(NE, DC, P, 2, P).transpose(0, 3, 2, 1, 4).reshape(NE, 2, P, CH)
    w2 = x["w2_2"][0].reshape(NE, 2, P, CH)
    parts = [w1[0], w3[0]]
    for e in range(1, NE):
        parts += [w1[e], w3[e], w2[e - 1]]
    S["moe"] = np.concatenate(parts + [w2[NE - 1]])
    stream = np.empty((N_SLOTS, P, CH), np.float32)
    for name, n in STREAM:
        stream[SO[name][0]:SO[name][1]] = S.pop(name)

    def cols(*a):
        return np.concatenate([np.ascontiguousarray(v).reshape(-1, P).T for v in a], 1)

    rows = lambda v: np.broadcast_to(v.reshape(1, -1), (P, v.size))
    V = {"mod_b": cols(x["mod_b"], x["kv_mod_b"], x["b_ada_2"]), "ng0a": cols(x["norm_g"][0, 0]),
         "ng0b": cols(x["norm_g"][0, 1]), "ng1a": cols(x["norm_g"][1, 0]), "ng1b": cols(x["norm_g"][1, 1]),
         "kvg": cols(x["kv_norm_g"]), "fing": cols(x["final_norm_g"]), "n1": cols(x["norm1_2"]),
         "n2": cols(x["norm2_2"]), "fin2": cols(x["final_norm_2"]), "gla_b": cols(x["gla_b_g2"]),
         "gla_ng": cols(x["gla_norm_g"]), "qn": cols(x["q_norm_2"]), "kvn": cols(x["kv_norm_2"]),
         "c": cols(x["c"]), "c2": cols(x["c_2"]), "sinks": rows(x["swa_sinks"]),
         "rb": np.concatenate([rows(x["b_grp_2"]), rows(x["b_exp_2"])], 1)}
    consts, consts2 = shape_constants()
    return {
        "stream": stream,
        "vecs": np.ascontiguousarray(np.concatenate([V[n] for n, _ in VECS], 1)),
        "consts": consts, "consts2": consts2,
        "xin": np.ascontiguousarray(x["x"][0].T).reshape(DC, P, T),
        "pos": np.ascontiguousarray(np.broadcast_to(x["positions"].reshape(1, T), (P, T))),
        "wg2": np.ascontiguousarray(x["gla_w_g2"][0]),
        "subk": np.ascontiguousarray(x["peer_subkeys"].reshape(4, NK, P).transpose(2, 0, 1)),
    }


def kernel(**inputs):
    import concourse.bacc as bacc
    from concourse.bass_utils import run_bass_kernel_spmd

    arrays = layout({k: np.asarray(v) for k, v in inputs.items()})
    nc = bacc.Bacc("TRN2", target_bir_lowering=False, num_devices=1)
    args = [nc.dram_tensor(n, a.shape, mybir.dt.from_np(a.dtype), kind="ExternalInput").ap()
            for n, a in arrays.items()]
    out = nc.dram_tensor("out", (DC, P, T), F32, kind="ExternalOutput").ap()
    block_program(nc, *args, out)
    r = run_bass_kernel_spmd(nc, [arrays], core_ids=[0])
    y = r.results[0]["out"]
    return np.ascontiguousarray(y.reshape(1, D, T).transpose(0, 2, 1))
```

```python
from contextlib import ExitStack

import numpy as np
import concourse.bass as bass
from concourse import mybir

F32 = mybir.dt.float32
F32R = mybir.dt.float32r
I32 = mybir.dt.int32
U32 = mybir.dt.uint32
ALU = mybir.AluOpType
ACT = mybir.ActivationFunctionType
AX = mybir.AxisListType

P = 128
D = 1024
T = 256
DC = D // P
TT = T // P
EPS = 1e-6
GH, GDV, GC = 4, 256, 64
NCH = T // GC
RANK = 16
SH, SKV, SHD = 16, 4, 64
PH, NK, TOPK = 8, 128, 16
RH = 4
MH = 8
QL, KVL = 384, 256
NG, EG = 4, 8
NE = NG * EG
NEG = -1.0e30
LOW = -3.0e38
RING = 4
HALVES = 4
TURN = 16
CH = 1024

STREAM = [
    ("mod", 40),
    ("gla_gl", 1), ("gla_q", 4), ("gla_k", 4), ("gla_v", 8), ("gla_og", 8), ("gla_out", 8),
    ("peer0_q", 16), ("peer0_u", NK), ("peer0_v", 3 * NK // 2),
    ("kv_k", 4), ("kv_v", 4), ("swa_q", 8), ("swa_out", 8),
    ("peer1_q", 16), ("peer1_u", NK), ("peer1_v", 3 * NK // 2),
    ("ret_q", 8), ("ret_k", 8), ("ret_v", 8), ("ret_g", 8), ("mla_cq", 3), ("mla_ckv", 2), ("mla_kpe", 1),
    ("gate_r", 8), ("gate_m", 8), ("ret_o", 8), ("mla_uq", 6), ("mla_uk", 2), ("mla_uv", 2), ("mla_o", 8),
    ("mix_out", 8),
    ("router", 1), ("moe", 6 * NE),
]
N_SLOTS = sum(n for _, n in STREAM)

VECS = [("mod_b", 160), ("ng0a", 8), ("ng0b", 8), ("ng1a", 8), ("ng1b", 8), ("kvg", 8), ("fing", 8), ("n1", 8),
        ("n2", 8), ("fin2", 8), ("gla_b", 4), ("gla_ng", 2), ("qn", 3), ("kvn", 2), ("c", 8), ("c2", 8),
        ("sinks", SH), ("rb", NG + NE)]
CONSTS = [("ident", 128), ("ones", 128), ("iota", 128), ("cols", 8)]
CONSTS_G = [("gmask", 128), ("scan", 256)]
CONSTS_S = [("smask", 384), ("perm_s", 128)]
CONSTS2 = [("perm_m", 128), ("mmask", 384), ("mcos", 256), ("msin", 256), ("rcos", 256), ("rsin", 256),
           ("decay", RH * 384)]


def offsets(table):
    at, out = 0, {}
    for name, n in table:
        out[name] = (at, at + n)
        at += n
    return out, at


VO, NV = offsets(VECS)
CO, NCST = offsets(CONSTS)
CGO, NCG = offsets(CONSTS_G)
CSO, NCS = offsets(CONSTS_S)
C2O, NC2 = offsets(CONSTS2)
SO, _ = offsets(STREAM)

TAU = 16.0
LN2 = 0.6931471805599453
LN2_HI = 0.693359375
LN2_LO = LN2 - LN2_HI
TWO_PI = 6.283185307179586
C1 = 6.28125
C2 = float(np.float32(np.floor((TWO_PI - C1) * 2.0 ** 20) / 2.0 ** 20))
C3 = float(np.float32(TWO_PI - C1 - C2))
PI_IN = 3.1415925


def shape_constants():
    f = np.float32
    c = {}
    r = np.arange(P)
    c["ident"] = np.eye(P)
    c["ones"] = np.ones((P, P))
    c["iota"] = np.tile(r, (P, 1))
    c["gmask"] = (r[:, None] // GC == r[None] // GC) & (r[:, None] <= r[None])
    diag = np.where(r[:, None] >= r[None], 0.0, NEG)
    c["smask"] = np.concatenate([diag, np.where(r[None] > r[:, None], 0.0, NEG), diag], 1)
    m = np.zeros((P, P))
    for i in range(P):
        k = i % SHD
        if k < 16:
            m[(i + 8 if k < 8 else i - 8), i] = 1
    c["perm_s"] = m
    c["scan"] = np.tile(np.arange(T) % GC != 0, (P, 1))
    k = r % SHD
    inv = np.where(k < 16, f(500000.0) ** (-(2 * (k % 8)).astype(f) / f(16)), 0).astype(f)
    cols = np.zeros((P, 8))
    cols[:, 0] = inv
    cols[:, 1] = np.where(k < 8, -1, np.where(k < 16, 1, 0))
    cols[:, 2] = r < 64
    cols[:, 3] = r >= 64
    cols[:, 4] = 1.0
    c["cols"] = cols
    m = np.zeros((P, P))
    for i in range(P):
        m[(i + 32 if i % 64 < 32 else i - 32), i] = 1
    c["perm_m"] = m
    c["mmask"] = np.concatenate([diag, np.zeros((P, P)), diag], 1)
    pos = np.arange(T, dtype=f)

    def rope(dim):
        inv = f(10000.0) ** (-np.arange(0, dim, 2, dtype=f) / f(dim))
        ang = (pos[:, None] * inv[None]).astype(f)
        return np.cos(ang).astype(f).T, np.sin(ang).astype(f).T

    mc, ms = rope(64)
    c["mcos"] = np.tile(mc, (4, 1))
    c["msin"] = np.tile(np.concatenate([-ms, ms]), (2, 1))
    c["rcos"], c["rsin"] = rope(256)
    lg = np.log1p(-np.exp2(-5.0 - np.arange(RH)))
    t = np.arange(T)
    dec = []
    for h in range(RH):
        for jb, lo in ((0, 0), (1, P)):
            rel = t[None, lo:] - (jb * P + r)[:, None]
            dec.append(np.where(rel >= 0, np.exp(lg[h] * np.maximum(rel, 0)), 0.0))
    c["decay"] = np.concatenate(dec, 1)
    cat = lambda tab: np.ascontiguousarray(np.concatenate([np.asarray(c[n], f) for n, _ in tab], 1))
    return {"consts": cat(CONSTS), "consts_g": cat(CONSTS_G), "consts_s": cat(CONSTS_S), "consts2": cat(CONSTS2)}


def block_program(nc, stream, vecs, xin, pos, wg2, subk, consts, consts_g, consts_s, consts2, out):
    ctx = ExitStack()
    with ctx:
        def sb(name, shape, dt=F32):
            return ctx.enter_context(nc.sbuf_tensor(name, shape, dt))

        ring = [sb(f"ring{i}", [P, CH]) for i in range(RING)]
        xT = sb("xT", [P, DC, T])
        hT = sb("hT", [P, DC, T])
        modv = sb("modv", [P, 160])
        gain = sb("gain", [P, 7, 8])
        vec = sb("vec", [P, NV])
        cst = sb("cst", [P, NCST])
        rope_c = sb("rope_c", [P, T])
        rope_s = sb("rope_s", [P, T])
        cact = sb("cact", [P, 16])
        rs = sb("rs", [P, T])
        mean = sb("mean", [P, 4, T])
        route = mean[:, 0:3, :]
        h_parts = sb("h_parts", [P, 2, DC, T], F32R)
        w_parts = [sb(f"w_parts{i}", [P, 2, CH // 2], F32R) for i in range(HALVES)]
        hot1 = hT[:, :, :].rearrange("p s (k n) -> p (s k) n", k=2)
        hot2 = h_parts[:, 0, :, :].rearrange("p s (k n) -> p (s k) n", k=2)
        a_parts = sb("a_parts", [P, 2, 2, T], F32R)
        ARENA = NK * T
        N_LOADS = 6
        ROUTE_TILE = 72
        arena = sb("arena", [P, ARENA])
        bank = [ctx.enter_context(nc.psum_tensor(f"bank{i}", [P, 512], F32)) for i in range(8)]

        def V(name):
            return vec[:, VO[name][0]:VO[name][1]]

        def C(name):
            return cst[:, CO[name][0]:CO[name][1]]

        ident, ones, iota = C("ident"), C("ones"), C("iota")
        one_col = C("cols")[:, 4:5]

        class Place:
            def __init__(self, at=0):
                self.at = at

            def __call__(self, n):
                a = arena[:, self.at:self.at + n]
                self.at += n
                assert self.at <= ARENA, self.at
                return a

        sems = {}

        def sem(name):
            if name not in sems:
                sems[name] = ctx.enter_context(nc.semaphore(name))
            return sems[name]

        counts = {}

        def signal(name):
            counts[name] = counts.get(name, 0) + 1
            return sem(name)

        def signalled(name):
            return counts[name]

        SQUARES = ["0a", "0b", "kv", "1a", "1b", "mid", "2a", "cq", "ckv", "2b", "out"]
        ROOTS = ["0a", "g", "0b", "kv", "1a", "1b", "mid", "2a", "r", "cq", "ckv", "2b", "out"]
        RESULTS = ["0a", "0b", "kv", "1a", "1b", "mid", "2a", "2b", "out"]

        def results(u):
            return DC * (RESULTS.index(u) + 1)

        landed = [sem(f"landed{i}") for i in range(RING)]
        ring_free = sem("ring_free")
        full = [sem(f"bank_full{i}") for i in range(4)]
        free = [sem(f"bank_free{i}") for i in range(4)]

        tile_no = {}

        def open_tile(name):
            n = tile_no[name] = len(tile_no)
            return bank[n % 4]

        def tile_of(name):
            return bank[tile_no[name] % 4]

        def full_sem(name):
            return full[tile_no[name] % 4]

        def filled(name):
            return tile_no[name] // 4 + 1

        def free_sem(name):
            return free[tile_no[name] % 4]

        def freed(name):
            return tile_no[name] // 4 + 2

        block = ctx.enter_context(nc.Block())

        @block.sync
        def _(sp):
            rounds = N_SLOTS // RING
            with sp.Fori(0, rounds) as r:
                for s in range(RING):
                    sp.wait_ge(ring_free, r * RING + (s + 1))
                    sp.dma_start(ring[s][:, :], stream[r * RING + s]).then_inc(landed[s], 16)
            for s in range(N_SLOTS - rounds * RING):
                sp.wait_ge(ring_free, rounds * RING + s + 1)
                sp.dma_start(ring[s][:, :], stream[rounds * RING + s]).then_inc(landed[s], 16)
            sp.wait_ge(sem("norm_result"), results("out"))
            sp.dma_start(out.rearrange("c p t -> p c t"), hT[:, :, :]).then_inc(sem("stored"), 16)
            sp.wait_ge(sem("stored"), 16)

        def slot(name, k):
            return ring[(SO[name][0] + k) % RING]

        def landed_sem(name, k):
            return landed[(SO[name][0] + k) % RING]

        def landed_at(name, k):
            return 16 * ((SO[name][0] + k) // RING + 1)

        def norm_pe(pe, u, src, n=DC):
            pe.wait_ge(sem("norm_squares"), SQUARES.index(u) + 1)
            t = open_tile(f"n{u}_ss")
            pe.wait_ge(free_sem(f"n{u}_ss"), freed(f"n{u}_ss") - 1)
            for k in range(n):
                mm = pe.matmul(t[:, 0:T], ones, src[:, k, :], start=(k == 0), stop=(k == n - 1))
            mm.then_inc(full_sem(f"n{u}_ss"), 1)

        def project(pe, name, k, src, tile, n=DC):
            w = slot(name, k)
            pe.wait_ge(landed_sem(name, k), landed_at(name, k))
            t = open_tile(tile)
            pe.wait_ge(free_sem(tile), freed(tile) - 1)
            for q in range(n):
                mm = pe.matmul(t[:, 0:T], w[:, q * P:(q + 1) * P], src[:, q, :], start=(q == 0), stop=(q == n - 1))
                if q == 0 and name != "gla_gl":
                    mm.then_inc(ring_free, 1)
            mm.then_inc(full_sem(tile), 1)

        def project_tokens(pe, name, src, tile, halves):
            for nh in range(halves):
                t = []
                for a in range(TT):
                    b = open_tile(f"{tile}{nh}{a}")
                    pe.wait_ge(free_sem(f"{tile}{nh}{a}"), freed(f"{tile}{nh}{a}") - 1)
                    t.append(b)
                for kp in range(4):
                    w = slot(name, nh * 4 + kp)
                    pe.wait_ge(landed_sem(name, nh * 4 + kp), landed_at(name, nh * 4 + kp))
                    for q in range(2):
                        for a in range(TT):
                            k = 2 * kp + q
                            mm = pe.matmul(t[a][:, :], src[:, k, a * P:(a + 1) * P], w[:, q * 512:(q + 1) * 512],
                                           start=(k == 0), stop=(k == DC - 1))
                            if q == 0 and a == 0:
                                mm.then_inc(ring_free, 1)
                            if k == DC - 1:
                                mm.then_inc(full_sem(f"{tile}{nh}{a}"), 1)

        def column(pe, out_col, part, first=True, last=True):
            return pe.matmul(out_col, part, one_col, start=first, stop=last)

        def mod_pe(pe):
            pe.sem_inc(ring_free, RING)
            pe.sem_inc(sem("mod_col"), RING)
            for b in range(4):
                pe.sem_inc(free[b], 1)
            t = open_tile("mod")
            pe.wait_ge(free_sem("mod"), freed("mod") - 1)
            with pe.Fori(0, 40 // RING) as it:
                for s in range(RING):
                    pe.wait_ge(sem("mod_part"), it * RING + (s + 1))
                    for q in range(4):
                        mm = column(pe, t[:, bass.ds(it * RING + s, 1)], mod_prod[s][:, (3 - q) * P:(4 - q) * P], q == 0, q == 3)
                    mm.then_inc(sem("mod_col"), 1)
            column(pe, t[:, 511:512], mod_prod[RING - 1][:, 0:P]).then_inc(full_sem("mod"), 1)

        def gla_pe(pe):
            pe.wait_ge(sem("norm_result"), results("0a"))
            project(pe, "gla_gl", 0, hT, "g_gl")
            for h in range(GH):
                project(pe, "gla_q", h, hT, f"g_q{h}")
            pe.wait_ge(free_sem("g_gl"), freed("g_gl"))
            for h in range(GH):
                t = open_tile(f"g_z{h}")
                pe.wait_ge(free_sem(f"g_z{h}"), freed(f"g_z{h}") - 1)
                pe.matmul(t[:, 0:T], G.wg2[0:RANK, h * P:(h + 1) * P], G.gl[0:RANK, :], start=True, stop=True).then_inc(full_sem(f"g_z{h}"), 1)
            for h in range(GH):
                project(pe, "gla_k", h, hT, f"g_k{h}")
            project_tokens(pe, "gla_v", hT, "g_v", 2)
            for c in range(8):
                project(pe, "gla_og", c, hT, f"g_og{c}")
            pe.wait_ge(sem("g_kd"), 1)
            for h in range(GH):
                t = open_tile(f"g_kt{h}")
                pe.wait_ge(free_sem(f"g_kt{h}"), freed(f"g_kt{h}") - 1)
                for b in range(TT):
                    mm = pe.transpose(t[:, b * P:(b + 1) * P], G.kd[:, h, b * P:(b + 1) * P], ident)
                mm.then_inc(full_sem(f"g_kt{h}"), 1)
            pe.wait_ge(sem("g_kq"), 2)
            for h in range(GH):
                t = open_tile(f"g_s{h}")
                pe.wait_ge(free_sem(f"g_s{h}"), freed(f"g_s{h}") - 1)
                for b in range(TT):
                    s = slice(b * P, (b + 1) * P)
                    mm = pe.matmul(t[:, s], G.k[:, h, s], G.q[:, h, s], start=True, stop=True)
                mm.then_inc(full_sem(f"g_s{h}"), 1)
            for n in range(NCH):
                b, cs = n // 2, slice(n * GC, (n + 1) * GC)
                for h in range(GH):
                    if n == 0:
                        pe.wait_ge(free_sem(f"g_s{h}"), freed(f"g_s{h}"))
                    else:
                        pe.wait_ge(sem("g_state"), GH * (n - 1) + h + 1)
                    for e in range(2):
                        vs = slice(h * GDV + e * P, h * GDV + (e + 1) * P)
                        o = bank[4 + h][:, e * T + n * GC:e * T + (n + 1) * GC]
                        mm = pe.matmul(o, G.v[:, b, vs], G.sm[:, h, cs], start=True, stop=(n == 0))
                        if n:
                            mm = pe.matmul(o, G.st[:, h, n % 2, e * P:(e + 1) * P], G.q[:, h, cs],
                                           start=False, stop=True)
                    if n == NCH - 1:
                        mm.then_inc(sem("g_o"), 1)
                for h in range(GH if n < NCH - 1 else 0):
                    if n == 0:
                        pe.wait_ge(free_sem(f"g_kt{h}"), freed(f"g_kt{h}"))
                    ps = slice((n % 2) * GC, (n % 2 + 1) * GC)
                    t = open_tile(f"g_u{n}{h}")
                    pe.wait_ge(free_sem(f"g_u{n}{h}"), freed(f"g_u{n}{h}") - 1)
                    pe.matmul(t[:, 0:GDV], G.kt[ps, h, b, :], G.v[ps, b, h * GDV:(h + 1) * GDV],
                                         start=True, stop=True).then_inc(full_sem(f"g_u{n}{h}"), 1)
            for h in range(GH):
                pe.wait_ge(sem("g_sq"), h + 1)
                t = open_tile(f"g_ss{h}")
                pe.wait_ge(free_sem(f"g_ss{h}"), freed(f"g_ss{h}") - 1)
                for e in range(2):
                    mm = pe.matmul(t[:, 0:T], ones, G.sq[:, h % 2, e, :], start=(e == 0), stop=(e == 1))
                mm.then_inc(full_sem(f"g_ss{h}"), 1)
            pe.wait_ge(sem("g_y"), 1)
            for c in range(DC):
                project(pe, "gla_out", c, G.o, f"g_out{c}")

        def peer_pe(pe, l):
            n = f"p{l}"
            pe.wait_ge(sem("norm_result"), results(f"{l}b"))
            for j in range(16):
                project(pe, f"peer{l}_q", j, hT, f"{n}_q{j}")
            pe.wait_ge(sem(f"{n}_subk"), 16)
            for a in range(TT):
                for h in range(PH):
                    pe.wait_ge(free_sem(f"{n}_q{2 * h + 1}"), freed(f"{n}_q{2 * h + 1}"))
                    if h == 0:
                        pe.wait_ge(free_sem(f"{n}_q15"), freed(f"{n}_q15"))
                    t = open_tile(f"{n}_s{a}{h}")
                    pe.wait_ge(free_sem(f"{n}_s{a}{h}"), freed(f"{n}_s{a}{h}") - 1)
                    for half in range(2):
                        mm = pe.matmul(t[:, half * NK:(half + 1) * NK], R.q[:, 2 * h + half, a * P:(a + 1) * P],
                                       R.subk[:, half, :], start=True, stop=True)
                    mm.then_inc(full_sem(f"{n}_s{a}{h}"), 1)
            pe.sem_inc(sem(f"{n}_half_free"), HALVES)
            pe.wait_ge(sem(f"{n}_hparts"), 1)
            up_pe(pe, l, 0, ROUTE_TILE)
            pe.wait_ge(sem(f"{n}_gelu"), ROUTE_TILE)
            for a in range(TT):
                pe.wait_ge(sem(f"{n}_picked"), a + 1)
                t = open_tile(f"{n}_rt{a}")
                pe.wait_ge(free_sem(f"{n}_rt{a}"), freed(f"{n}_rt{a}") - 1)
                for k in range(3):
                    mm = pe.transpose(t[:, k * P:(k + 1) * P], R.pick[:, a, k, :], ident)
                mm.then_inc(full_sem(f"{n}_rt{a}"), 1)
            for a in range(TT):
                pe.wait_ge(free_sem(f"{n}_rt{a}"), freed(f"{n}_rt{a}"))
            up_pe(pe, l, ROUTE_TILE, NK)
            pe.sem_inc(sem(f"{n}_hot_free"), TURN)
            pe.sem_inc(sem(f"{n}_table_free"), TURN // 4)
            with pe.Fori(0, T // TURN) as it:
                for s in range(TURN):
                    if s % 4 == 0:
                        pe.wait_ge(sem(f"{n}_table_free"), it * (TURN // 4) + (s // 4 + 1))
                        pe.wait_ge(sem(f"{n}_hot2"), it * (TURN // 4) + (s // 4 + 1))
                    pe.wait_ge(sem(f"{n}_hot"), it * TURN + (s + 1))
                    pe.matmul(bank[4 + s // 4][:, (s % 4) * P:(s % 4 + 1) * P], hot2[:, s, :].bitcast(F32),
                              hot1[:, s, :], start=True, stop=True).then_inc(sem(f"{n}_hot_free"), 1)
            pe.wait_ge(sem(f"{n}_table_free"), TURN // 4 + T // 4)
            pe.wait_ge(sem(f"{n}_gelu"), NK)
            down_pe(pe, l)
            pe.wait_ge(sem(f"{n}_mods"), 1)
            back_pe(pe, n)

        def up_pe(pe, l, first, last):
            n, base = f"p{l}", SO[f"peer{l}_u"][0]
            with pe.Fori(first // 4, last // 4) as it:
                for k in range(4):
                    for j in range(2):
                        half = 2 * k + j
                        pe.wait_ge(sem(f"{n}_low"), it * 8 + (half + 1))
                        w = w_parts[half % HALVES]
                        for q in range(4):
                            ws = slice(q * P, (q + 1) * P)
                            for i, (wp, hp) in enumerate(((0, 0), (0, 1), (1, 0))):
                                mm = pe.matmul(bank[k][:, 0:T], w[:, wp, ws], h_parts[:, hp, 4 * j + q, :],
                                               start=(j == 0 and q == 0 and i == 0),
                                               stop=(j == 1 and q == 3 and i == 2))
                                if j == 0 and q == 0 and i == 0:
                                    mm.then_inc(ring_free, 1)
                        mm.then_inc(sem(f"{n}_half_free"), 1)

        def down_pe(pe, l):
            n = f"p{l}"
            for b in range(4, 8):
                pe.matmul(bank[b][:, 0:384], C("cols")[0:1, 5:6].broadcast_to([1, P]), cst[0:1, 0:384],
                          start=True, stop=False, skip_group_check=True)
                pe.matmul(bank[b][:, 384:512], C("cols")[0:1, 5:6].broadcast_to([1, P]), cst[0:1, 0:P],
                          start=False, stop=False, skip_group_check=True)
            with pe.Fori(0, NK // 8) as it:
                for k in range(8):
                    for e in range(2):
                        half = 2 * k + e
                        pe.wait_ge(sem(f"{n}_low"), it * 16 + (2 * NK + half + 1))
                        if e == 0:
                            pe.wait_ge(sem(f"{n}_gated"), it * 8 + (k + 1))
                        w = w_parts[half % HALVES]
                        for a in range(TT):
                            for i, (ap, wp) in enumerate(((0, 0), (0, 1), (1, 0))):
                                mm = pe.matmul(bank[4 + 2 * a + e][:, :], a_parts[:, k % 2, ap, a * P:(a + 1) * P],
                                               w[:, wp, :], start=False, stop=False, skip_group_check=True)
                                if e == 0 and a == 0 and i == 0:
                                    mm.then_inc(ring_free, 1)
                        mm.then_inc(sem(f"{n}_half_free"), 1)
                    if k % 2:
                        m = k // 2
                        pe.wait_ge(sem(f"{n}_part"), it * 4 + (m + 2))
                        column(pe, bank[0][:, bass.ds(it * 4 + m, 1)], hT[:, 4 + (m + 3) % 4, 0:P]).then_inc(ring_free, 1)
            pe.wait_ge(sem(f"{n}_part"), 2 + NK // 2)
            column(pe, bank[0][:, NK // 2:NK // 2 + 1], hT[:, 7, 0:P]).then_inc(sem(f"{n}_sum"), 1)

        def back_pe(pe, n):
            pe.wait_ge(sem(f"{n}_ysb"), 4)
            for c in range(DC):
                t = open_tile(f"{n}_y{c}")
                pe.wait_ge(free_sem(f"{n}_y{c}"), freed(f"{n}_y{c}") - 1)
                for a in range(TT):
                    mm = pe.transpose(t[:, a * P:(a + 1) * P], B.y[:, 2 * a + c // 4, (c % 4) * P:(c % 4 + 1) * P],
                                      ident)
                mm.then_inc(full_sem(f"{n}_y{c}"), 1)

        def attention_pe(pe, n, heads, scores, vcols, vtok):
            for h in range(heads):
                t = open_tile(f"{n}_s{h}")
                pe.wait_ge(free_sem(f"{n}_s{h}"), freed(f"{n}_s{h}") - 1)
                mm = scores(h, t)
                mm.then_inc(full_sem(f"{n}_s{h}"), 1)
            for h in range(heads):
                pe.wait_ge(sem(f"{n}_p"), h + 1)
                t = open_tile(f"{n}_pt{h}")
                pe.wait_ge(free_sem(f"{n}_pt{h}"), freed(f"{n}_pt{h}") - 1)
                for k in range(3):
                    mm = pe.transpose(t[:, k * P:(k + 1) * P], A.p[:, h, k * P:(k + 1) * P], ident)
                mm.then_inc(full_sem(f"{n}_pt{h}"), 1)
                pe.wait_ge(free_sem(f"{n}_pt{h}"), freed(f"{n}_pt{h}"))
                t = open_tile(f"{n}_o{h}")
                pe.wait_ge(free_sem(f"{n}_o{h}"), freed(f"{n}_o{h}") - 1)
                pe.matmul(t[:, 0:P], vtok[:, 0, vcols(h)], A.pt[:, h % 2, 0:P], start=True, stop=True)
                pe.matmul(t[:, P:T], vtok[:, 0, vcols(h)], A.pt[:, h % 2, P:2 * P], start=True, stop=False)
                pe.matmul(t[:, P:T], vtok[:, 1, vcols(h)], A.pt[:, h % 2, 2 * P:3 * P],
                                     start=False, stop=True).then_inc(full_sem(f"{n}_o{h}"), 1)

        def swa_pe(pe):
            pe.wait_ge(sem("norm_result"), results("kv"))
            pe.wait_ge(sem("loaded_s"), 16)
            for k in range(4):
                project(pe, "kv_k", k, hT, f"kv_k{k}")
            project_tokens(pe, "kv_v", hT, "kv_v", 1)
            for k in range(4):
                pe.wait_ge(free_sem(f"kv_k{k}"), freed(f"kv_k{k}"))
                t = open_tile(f"kv_r{k}")
                pe.wait_ge(free_sem(f"kv_r{k}"), freed(f"kv_r{k}") - 1)
                pe.matmul(t[:, 0:T], S.perm, S.k[:, k, :], start=True, stop=True).then_inc(full_sem(f"kv_r{k}"), 1)
            norm_pe(pe, "1a", hT)
            pe.wait_ge(sem("norm_result"), results("1a"))
            for c in range(DC):
                project(pe, "swa_q", c, hT, f"w_q{c}")
            for c in range(DC):
                pe.wait_ge(free_sem(f"w_q{c}"), freed(f"w_q{c}"))
                t = open_tile(f"w_r{c}")
                pe.wait_ge(free_sem(f"w_r{c}"), freed(f"w_r{c}") - 1)
                pe.matmul(t[:, 0:T], S.perm, S.q[:, c, :], start=True, stop=True).then_inc(full_sem(f"w_r{c}"), 1)

            def scores(h, t):
                c, rows = h // 2, slice((h % 2) * SHD, (h % 2 + 1) * SHD)
                k = h // (SH // SKV)
                if h == 0:
                    pe.wait_ge(sem("w_kr"), 4)
                if h % 2 == 0:
                    pe.wait_ge(sem("w_qr"), c + 1)
                pe.matmul(t[:, 0:P], S.q[rows, c, 0:P], S.k[rows, k, 0:P], start=True, stop=True)
                return pe.matmul(t[:, P:3 * P], S.q[rows, c, P:T], S.k[rows, k, :], start=True, stop=True)

            attention_pe(pe, "w", SH, scores, lambda h: slice((h // 4) * P, (h // 4 + 1) * P), S.v)
            pe.wait_ge(free_sem("w_o14"), freed("w_o14"))
            pe.wait_ge(free_sem("w_o15"), freed("w_o15"))
            for c in range(DC):
                project(pe, "swa_out", c, A.o, f"w_out{c}")

        def mix_pe(pe):
            pe.wait_ge(sem("norm_result"), results("2a"))
            for name in ("q", "k"):
                for c in range(8):
                    project(pe, f"ret_{name}", c, hT, f"r_{name}{c}")
            project_tokens(pe, "ret_v", hT, "r_v", 2)
            for c in range(8):
                project(pe, "ret_g", c, hT, f"r_g{c}")
            for c in range(3):
                project(pe, "mla_cq", c, hT, f"m_cq{c}")
            for c in range(2):
                project(pe, "mla_ckv", c, hT, f"m_ckv{c}")
            project(pe, "mla_kpe", 0, hT, "m_kpe")
            for c in range(8):
                project(pe, "gate_r", c, hT, f"r_gate{c}")
            for c in range(8):
                project(pe, "gate_m", c, hT, f"m_gate{c}")
            pe.wait_ge(sem("r_rot"), 4)
            for h in range(RH):
                t = open_tile(f"r_s{h}")
                pe.wait_ge(free_sem(f"r_s{h}"), freed(f"r_s{h}") - 1)
                for jb, cols, qs in ((0, slice(0, T), slice(0, T)), (1, slice(T, T + P), slice(P, T))):
                    for q in range(2):
                        mm = pe.matmul(t[:, cols], M.k[:, 2 * h + q, jb * P:(jb + 1) * P], M.q[:, 2 * h + q, qs],
                                       start=(q == 0), stop=(q == 1))
                mm.then_inc(full_sem(f"r_s{h}"), 1)
            for h in range(RH):
                pe.wait_ge(free_sem(f"r_s{h}"), freed(f"r_s{h}"))
                t = open_tile(f"r_y{h}")
                pe.wait_ge(free_sem(f"r_y{h}"), freed(f"r_y{h}") - 1)
                for e in range(2):
                    vs = slice(h * 256 + e * P, h * 256 + (e + 1) * P)
                    o = e * T
                    pe.matmul(t[:, o:o + P], M.v[:, 0, vs], M.s[:, h, 0:P], start=True, stop=True)
                    pe.matmul(t[:, o + P:o + T], M.v[:, 0, vs], M.s[:, h, P:T], start=True, stop=False)
                    mm = pe.matmul(t[:, o + P:o + T], M.v[:, 1, vs], M.s[:, h, T:T + P], start=False, stop=True)
                mm.then_inc(full_sem(f"r_y{h}"), 1)
            for h in range(RH):
                pe.wait_ge(free_sem(f"r_y{h}"), freed(f"r_y{h}"))
                t = open_tile(f"r_mean{h}")
                pe.wait_ge(free_sem(f"r_mean{h}"), freed(f"r_mean{h}") - 1)
                for e in range(2):
                    mm = pe.matmul(t[:, 0:T], ones, M.y[:, 2 * h + e, :], start=(e == 0), stop=(e == 1))
                mm.then_inc(full_sem(f"r_mean{h}"), 1)
            for h in range(RH):
                pe.wait_ge(sem("r_sq"), h + 1)
                t = open_tile(f"r_var{h}")
                pe.wait_ge(free_sem(f"r_var{h}"), freed(f"r_var{h}") - 1)
                for e in range(2):
                    mm = pe.matmul(t[:, 0:T], ones, M.sq[:, 2 * h + e, :], start=(e == 0), stop=(e == 1))
                mm.then_inc(full_sem(f"r_var{h}"), 1)
            norm_pe(pe, "cq", M.sqc, 3)
            norm_pe(pe, "ckv", M.sqk, 2)
            pe.wait_ge(sem("r_yn"), 1)
            for c in range(DC):
                project(pe, "ret_o", c, M.y, f"r_o{c}")
            pe.wait_ge(sem("m_cqn"), 3)
            for k in range(6):
                w = slot("mla_uq", k)
                pe.wait_ge(landed_sem("mla_uq", k), landed_at("mla_uq", k))
                for j in range(2):
                    i = 2 * k + j
                    t = open_tile(f"m_q{i}")
                    pe.wait_ge(free_sem(f"m_q{i}"), freed(f"m_q{i}") - 1)
                    for q in range(3):
                        mm = pe.matmul(t[:, 0:T], w[:, (3 * j + q) * P:(3 * j + q + 1) * P], M.cq[:, q, :],
                                       start=(q == 0), stop=(q == 2))
                        if j == 0 and q == 0:
                            mm.then_inc(ring_free, 1)
                    mm.then_inc(full_sem(f"m_q{i}"), 1)
            pe.wait_ge(sem("m_ckvn"), 2)
            for k in range(2):
                w = slot("mla_uk", k)
                pe.wait_ge(landed_sem("mla_uk", k), landed_at("mla_uk", k))
                for j in range(4):
                    t = open_tile(f"m_k{4 * k + j}")
                    pe.wait_ge(free_sem(f"m_k{4 * k + j}"), freed(f"m_k{4 * k + j}") - 1)
                    for q in range(2):
                        mm = pe.matmul(t[:, 0:T], w[:, (2 * j + q) * P:(2 * j + q + 1) * P], M.ckv[:, q, :],
                                       start=(q == 0), stop=(q == 1))
                        if j == 0 and q == 0:
                            mm.then_inc(ring_free, 1)
                    mm.then_inc(full_sem(f"m_k{4 * k + j}"), 1)
            for nh in range(2):
                w = slot("mla_uv", nh)
                pe.wait_ge(landed_sem("mla_uv", nh), landed_at("mla_uv", nh))
                for a in range(TT):
                    t = open_tile(f"m_v{nh}{a}")
                    pe.wait_ge(free_sem(f"m_v{nh}{a}"), freed(f"m_v{nh}{a}") - 1)
                    for q in range(2):
                        mm = pe.matmul(t[:, :], M.ckv[:, q, a * P:(a + 1) * P], w[:, q * 512:(q + 1) * 512],
                                       start=(q == 0), stop=(q == 1))
                        if a == 0 and q == 0:
                            mm.then_inc(ring_free, 1)
                    mm.then_inc(full_sem(f"m_v{nh}{a}"), 1)
            for c in range(5):
                pe.wait_ge(free_sem(f"m_q{8 + c}" if c < 4 else "m_kpe"), freed(f"m_q{8 + c}" if c < 4 else "m_kpe"))
                t = open_tile(f"m_r{c}")
                pe.wait_ge(free_sem(f"m_r{c}"), freed(f"m_r{c}") - 1)
                pe.matmul(t[:, 0:T], M.perm, M.qp[:, c, :] if c < 4 else M.kp[:, 0, :], start=True, stop=True).then_inc(full_sem(f"m_r{c}"), 1)

            def scores(h, t):
                if h == 0:
                    pe.wait_ge(free_sem("m_v11"), freed("m_v11"))
                    pe.wait_ge(sem("m_rot"), 6)
                for o, qs, n in ((0, slice(0, P), P), (P, slice(P, T), T)):
                    pe.matmul(t[:, o:o + n], M.qn[:, h, qs], M.kn[:, h, 0:n], start=True, stop=False)
                    mm = pe.matmul(t[:, o:o + n], M.qp[:, h // 2, qs], M.kp[:, 1 + h % 2, 0:n], start=False, stop=True)
                return mm

            attention_pe(pe, "m", MH, scores, lambda h: slice(h * P, (h + 1) * P), M.vm)
            pe.wait_ge(free_sem("m_o7"), freed("m_o7"))
            pe.wait_ge(free_sem("m_o6"), freed("m_o6"))
            for c in range(DC):
                project(pe, "mla_o", c, A.o, f"m_out{c}")
            pe.wait_ge(sem("merged"), 1)
            for c in range(DC):
                project(pe, "mix_out", c, M.mg, f"mix{c}")

        def moe_pe(pe):
            pe.wait_ge(sem("norm_result"), results("2b"))
            w = slot("router", 0)
            pe.wait_ge(landed_sem("router", 0), landed_at("router", 0))
            t = []
            for a in range(TT):
                b = open_tile(f"e_l{a}")
                pe.wait_ge(free_sem(f"e_l{a}"), freed(f"e_l{a}") - 1)
                t.append(b)
            for a in range(TT):
                for q in range(DC):
                    mm = pe.matmul(t[a][:, 0:NG + NE], hT[:, q, a * P:(a + 1) * P], w[:, q * P:q * P + NG + NE],
                                   start=(q == 0), stop=(q == DC - 1))
                    if a == 0 and q == 0:
                        mm.then_inc(ring_free, 1)
                mm.then_inc(full_sem(f"e_l{a}"), 1)
            pe.wait_ge(sem("e_gate"), 1)
            t = open_tile("e_gt")
            pe.wait_ge(free_sem("e_gt"), freed("e_gt") - 1)
            for a in range(TT):
                mm = pe.transpose(t[0:NE, a * P:(a + 1) * P], E.gate[:, a, :], ident)
            mm.then_inc(full_sem("e_gt"), 1)
            pe.wait_ge(free_sem("e_gt"), freed("e_gt"))
            for e in range(NE // 2):
                t = open_tile(f"e_b{e}")
                pe.wait_ge(free_sem(f"e_b{e}"), freed(f"e_b{e}") - 1)
                for k in range(2):
                    mm = pe.matmul(t[:, k * T:(k + 1) * T], cst[0:NE, 2 * e + k:2 * e + k + 1].broadcast_to([NE, P]),
                                   E.gt[0:NE, :], start=True, stop=True)
                mm.then_inc(full_sem(f"e_b{e}"), 1)
            for e in range(NE // 2 - 4, NE // 2):
                pe.wait_ge(free_sem(f"e_b{e}"), freed(f"e_b{e}"))
            pe.sem_inc(sem("e_half_free"), HALVES)
            pe.wait_ge(sem("e_hparts"), 1)

            def up(e_par, k, step):
                for m in range(2):
                    for f in range(2):
                        for j in range(2):
                            half = 2 * (k + 2 * m + f) + j
                            pe.wait_ge(sem("e_low"), step(half + 1))
                            w = w_parts[half % HALVES]
                            for q in range(4):
                                for i, (wp, hp) in enumerate(((0, 0), (0, 1), (1, 0))):
                                    mm = pe.matmul(bank[2 * e_par + m][:, f * T:(f + 1) * T],
                                                   w[:, wp, q * P:(q + 1) * P], h_parts[:, hp, 4 * j + q, :],
                                                   start=(j == 0 and q == 0 and i == 0),
                                                   stop=(j == 1 and q == 3 and i == 2))
                                    if j == 0 and q == 0 and i == 0:
                                        mm.then_inc(ring_free, 1)
                            mm.then_inc(sem("e_half_free"), 1)

            def down(k, step, hidden, start=False, stop=False):
                pe.wait_ge(sem("e_hlow"), hidden)
                for f in range(2):
                    for e in range(2):
                        half = 2 * (k + f) + e
                        pe.wait_ge(sem("e_low"), step(half + 1))
                        w = w_parts[half % HALVES]
                        for a in range(TT):
                            for i, (ap, wp) in enumerate(((0, 0), (0, 1), (1, 0))):
                                mm = pe.matmul(bank[4 + 2 * a + e][:, :], a_parts[:, ap, f, a * P:(a + 1) * P],
                                               w[:, wp, :], start=(start and f == 0 and i == 0),
                                               stop=(stop and f == 1 and i == 2))
                                if e == 0 and a == 0 and i == 0:
                                    mm.then_inc(ring_free, 1)
                        mm.then_inc(sem("e_sum" if stop and f == 1 and e == 1 else "e_half_free"), 1)

            same = lambda n: n
            up(0, 0, same)
            up(1, 4, same)
            down(8, same, 1, start=True)
            with pe.Fori(0, 7) as it:
                for j in range(4):
                    k = 10 + 6 * j
                    step = lambda n: it * 48 + n
                    up(j % 2, k, step)
                    down(k + 4, step, it * 4 + (2 + j))
            for e in (30, 31):
                up(e % 2, 6 * e - 2, same)
                down(6 * e + 2, same, e)
            down(6 * NE - 2, same, NE, stop=True)
            back_pe(pe, "e")

        class Bag:
            pass

        G, R, A, S, M, E, B, G2 = (Bag() for _ in range(8))
        G2.r2 = None
        ph = Place()
        G.gl = ph(T)
        G.wg2 = ph(4 * P)
        G.cst = ph(NCG)
        G.q = ph(GH * T).rearrange("p (h t) -> p h t", h=GH)
        G.k = ph(GH * T).rearrange("p (h t) -> p h t", h=GH)
        G.kd = ph(GH * T).rearrange("p (h t) -> p h t", h=GH)
        G.z = ph(GH * T).rearrange("p (h t) -> p h t", h=GH)
        G.b = ph(GH * T).rearrange("p (h t) -> p h t", h=GH)
        G.e = ph(GH * T).rearrange("p (h t) -> p h t", h=GH)
        G.e2 = ph(GH * T).rearrange("p (h t) -> p h t", h=GH)
        G.dec = ph(GH * NCH).rearrange("p (h n) -> p h n", h=GH)
        G.v = ph(2 * D).rearrange("p (a n) -> p a n", a=2)
        G.kt = ph(GH * T).rearrange("p (h b k) -> p h b k", h=GH, b=2)
        G.sm = ph(GH * T).rearrange("p (h t) -> p h t", h=GH)
        G.st = ph(GH * 2 * GDV).rearrange("p (h s e) -> p h s e", h=GH, s=2)
        G.sq = ph(4 * T).rearrange("p (h e t) -> p h e t", h=2, e=2)
        G.r = ph(GH * T).rearrange("p (h t) -> p h t", h=GH)
        G.og = ph(8 * T).rearrange("p (c t) -> p c t", c=8)
        G.o = ph(8 * T).rearrange("p (c t) -> p c t", c=8)

        mod_prod = [arena[:, ARENA - (i + 1) * CH:ARENA - i * CH] for i in range(RING)]

        ph = Place(ROUTE_TILE * T)
        R.subk = ph(2 * NK).rearrange("p (f n) -> p f n", f=2)
        R.q = ph(16 * T).rearrange("p (j t) -> p j t", j=16)
        R.s = ph(TT * 16 * NK).rearrange("p (a g n) -> p a g n", a=2, g=16)
        R.s2 = ph(16 * NK).rearrange("p (g n) -> p g n", g=16)
        R.v = ph(TT * 256).rearrange("p (a g k) -> p a g k", a=2, g=16)
        R.ix = ph(TT * 256).rearrange("p (a g k) -> p a g k", a=2, g=16)
        R.ixf = ph(TT * 256).rearrange("p (a g k) -> p a g k", a=2, g=16)
        R.cand = R.q[:, 0:8, :]
        R.cand2 = R.q[:, 8:16, :]
        R.cs = ph(128).rearrange("p (h k) -> p h k", h=PH)
        R.ci = ph(128).rearrange("p (h k) -> p h k", h=PH)
        R.ca = ph(128)
        R.cb = ph(128)
        R.caf = ph(128)
        R.cbf = ph(128)
        R.sum = ph(16)
        R.pick = ph(TT * 3 * 128).rearrange("p (a k n) -> p a k n", a=2, k=3)
        W = arena[:, 0:NK * T].rearrange("p (i t) -> p i t", i=NK)
        B.y = arena[:, 0:4 * 512].rearrange("p (a n) -> p a n", a=4)

        ph = Place()
        A.p = ph(SH * 384).rearrange("p (h k) -> p h k", h=SH)
        A.pt = ph(2 * 384).rearrange("p (s k) -> p s k", s=2)
        A.m = ph(2 * SH).rearrange("p (b h) -> p b h", b=2)
        A.l = ph(2 * SH).rearrange("p (b h) -> p b h", b=2)
        A.x = ph(2 * SH).rearrange("p (b h) -> p b h", b=2)
        A.o = ph(8 * T).rearrange("p (c t) -> p c t", c=8)
        mark = ph.at
        S.k = ph(4 * T).rearrange("p (c t) -> p c t", c=4)
        S.v = ph(TT * 512).rearrange("p (a n) -> p a n", a=2)
        S.q = ph(8 * T).rearrange("p (c t) -> p c t", c=8)
        S.tmp = ph(T)
        S.cst = ph(NCS)
        S.mask, S.perm = S.cst[:, 0:384], S.cst[:, 384:384 + P]

        ph = Place(mark)
        M.cst = ph(NC2)
        M.perm = M.cst[:, C2O["perm_m"][0]:C2O["perm_m"][1]]
        M.q = ph(8 * T).rearrange("p (c t) -> p c t", c=8)
        M.k = ph(8 * T).rearrange("p (c t) -> p c t", c=8)
        M.v = ph(TT * D).rearrange("p (a n) -> p a n", a=2)
        M.g = ph(8 * T).rearrange("p (c t) -> p c t", c=8)
        M.gr = ph(8 * T).rearrange("p (c t) -> p c t", c=8)
        M.gm = ph(8 * T).rearrange("p (c t) -> p c t", c=8)
        M.cq = ph(3 * T).rearrange("p (c t) -> p c t", c=3)
        M.ckv = ph(2 * T).rearrange("p (c t) -> p c t", c=2)
        M.kp = ph(3 * T).rearrange("p (c t) -> p c t", c=3)
        M.sqc = ph(3 * T).rearrange("p (c t) -> p c t", c=3)
        M.sqk = ph(2 * T).rearrange("p (c t) -> p c t", c=2)
        M.s = ph(RH * 384).rearrange("p (h t) -> p h t", h=RH)
        M.y = A.p[:, 0:6, :].rearrange("p h k -> p (h k)")[:, 0:8 * T].rearrange("p (c t) -> p c t", c=8)
        M.sq = A.p[:, 6:12, :].rearrange("p h k -> p (h k)")[:, 0:8 * T].rearrange("p (c t) -> p c t", c=8)
        G2.r2 = ph(T)
        M.r = ph(RH * T).rearrange("p (h t) -> p h t", h=RH)
        M.t = A.p[:, 10:16, :].rearrange("p h k -> p (h k)")[:, 0:8 * T].rearrange("p (c t) -> p c t", c=8)
        M.qn, M.kn, M.vm = M.q, M.k, M.v
        M.qp = M.s[:, 0:3, :].rearrange("p h t -> p (h t)")[:, 0:4 * T].rearrange("p (c t) -> p c t", c=4)
        M.mg = M.g

        ph = Place(2048)
        E.l = ph(TT * (NG + NE)).rearrange("p (a n) -> p a n", a=2)
        E.g8 = ph(TT * 8).rearrange("p (a n) -> p a n", a=2)
        E.m8 = ph(TT * 8).rearrange("p (a n) -> p a n", a=2)
        E.i8 = ph(TT * 8).rearrange("p (a n) -> p a n", a=2)
        E.if8 = ph(TT * 8).rearrange("p (a n) -> p a n", a=2)
        E.oh = ph(TT * NG).rearrange("p (a n) -> p a n", a=2)
        E.x8 = ph(TT * 8).rearrange("p (a n) -> p a n", a=2)
        E.w = ph(TT * 8).rearrange("p (a n) -> p a n", a=2)
        E.tmp = ph(TT * NE).rearrange("p (a n) -> p a n", a=2)
        E.ew = ph(TT * 8).rearrange("p (a n) -> p a n", a=2)
        E.ew2 = ph(TT * 8).rearrange("p (a n) -> p a n", a=2)
        E.gate = ph(TT * NE).rearrange("p (a n) -> p a n", a=2)
        E.gt = ph(T)
        E.gb = ph(NE * T).rearrange("p (e t) -> p e t", e=NE)
        E.sa = ph(2 * 512).rearrange("p (s n) -> p s n", s=2)
        E.hp = ph(2 * 512).rearrange("p (s n) -> p s n", s=2)
        E.hid = ph(2 * 512).rearrange("p (s f t) -> p s f t", s=2, f=2)

        @block.tensor
        def _(pe):
            pe.wait_ge(sem("loaded"), 16 * N_LOADS)
            mod_pe(pe)
            norm_pe(pe, "0a", hT)
            gla_pe(pe)
            norm_pe(pe, "0b", hT)
            peer_pe(pe, 0)
            norm_pe(pe, "kv", hT)
            swa_pe(pe)
            norm_pe(pe, "1b", hT)
            peer_pe(pe, 1)
            norm_pe(pe, "mid", hT)
            norm_pe(pe, "2a", hT)
            mix_pe(pe)
            norm_pe(pe, "2b", hT)
            moe_pe(pe)
            norm_pe(pe, "out", hT)

        def norm_act(act, u):
            act.activation(hT[:, :, :], xT[:, :, :], ACT.Square).then_inc(signal("norm_squares"), 1)
            act.wait_ge(sem("norm_squares"), signalled("norm_squares"))
            root_act(act, u, rs[:, :])

        def root_act(act, u, r):
            act.wait_ge(sem("norm_mean"), ROOTS.index(u) + 1)
            act.activation(r, r, ACT.Sqrt).then_inc(signal("norm_root"), 1)
            act.wait_ge(sem("norm_root"), signalled("norm_root"))

        def copy_act(act, dst, name, src=None, func=ACT.Copy):
            act.wait_ge(full_sem(name), filled(name))
            t = tile_of(name)
            act.activation(dst, t[:, 0:T] if src is None else src(t), func).then_inc(free_sem(name), 1)
            act.wait_ge(free_sem(name), freed(name))

        def mod_act(act):
            act.activation(cact[:, 0:8], V("c"), ACT.Sigmoid).then_inc(signal("csig"), 1)
            act.wait_ge(sem("csig"), signalled("csig"))
            act.activation(cact[:, 8:16], V("c2"), ACT.Sigmoid).then_inc(signal("csig"), 1)
            act.wait_ge(sem("csig"), signalled("csig"))

        def rope_act(act):
            act.wait_ge(sem("rope_args"), 1)
            act.activation(rope_c[:, :], rope_c[:, :], ACT.Sin).then_inc(signal("rope_sin"), 1)
            act.wait_ge(sem("rope_sin"), signalled("rope_sin"))
            act.activation(rope_s[:, :], rope_s[:, :], ACT.Sin).then_inc(signal("rope_sin"), 1)
            act.wait_ge(sem("rope_sin"), signalled("rope_sin"))

        def gla_act(act):
            copy_act(act, G.gl, "g_gl")
            for h in range(GH):
                copy_act(act, G.q[:, h, :], f"g_q{h}")
            for h in range(GH):
                copy_act(act, G.k[:, h, :], f"g_k{h}")
            for nh in range(2):
                for a in range(TT):
                    copy_act(act, G.v[:, a, nh * 512:(nh + 1) * 512], f"g_v{nh}{a}", lambda t: t[:, :])
            for c in range(8):
                copy_act(act, G.og[:, c, :], f"g_og{c}")
            act.wait_ge(sem("g_abs"), 1)
            act.activation(G.e, G.e, ACT.Sigmoid, scale=-1.0).then_inc(signal("g_act"), 1)
            act.wait_ge(sem("g_act"), signalled("g_act"))
            act.activation(G.e, G.e, ACT.Ln).then_inc(signal("g_ln"), 1)
            act.wait_ge(sem("g_ln"), signalled("g_ln"))
            act.activation(G.o, G.og, ACT.Sigmoid).then_inc(signal("g_sig"), 1)
            act.wait_ge(sem("g_sig"), signalled("g_sig"))
            for h in range(GH):
                copy_act(act, G.kt[:, h, :, :], f"g_kt{h}", lambda t: t[:, 0:T].rearrange("p (b k) -> p b k", b=2))
            for h in range(GH):
                act.wait_ge(sem("g_o"), h + 1)
                if h >= 2:
                    act.wait_ge(free_sem(f"g_ss{h - 2}"), freed(f"g_ss{h - 2}"))
                act.activation(G.sq[:, h % 2, :, :], bank[4 + h][:, :].rearrange("p (e t) -> p e t", e=2),
                                         ACT.Square).then_inc(signal("g_sq"), 1)
                act.wait_ge(sem("g_sq"), signalled("g_sq"))
            root_act(act, "g", G.r)

        def peer_act(act, l):
            n = f"p{l}"
            for j in range(16):
                copy_act(act, R.q[:, j, :], f"{n}_q{j}")
            for a in range(TT):
                for h in range(PH):
                    copy_act(act, R.s[:, a, 2 * h:2 * h + 2, :], f"{n}_s{a}{h}",
                             lambda t: t[:, 0:2 * NK].rearrange("p (g n) -> p g n", g=2))
            base = SO[f"peer{l}_u"][0]

            def high(i_k, count, landing, table):
                slot_ = (table + i_k) % RING
                act.wait_ge(landed[slot_], landing)
                for j in range(2):
                    half = 2 * i_k + j
                    act.wait_ge(sem(f"{n}_half_free"), count + (j + 1))
                    act.activation(w_parts[half % HALVES][:, 0, :], ring[slot_][:, j * 512:(j + 1) * 512],
                                   ACT.Copy).then_inc(sem(f"{n}_high"), 1)

            def gelu(i, k, count):
                act.wait_ge(sem(f"{n}_half_free"), HALVES + count)
                act.activation(W[:, i, :], bank[k][:, 0:T], ACT.Gelu).then_inc(sem(f"{n}_gelu"), 1)

            def tile_at(i):
                return 16 * ((base + i) // RING + 1)

            for i in range(2):
                high(i, 2 * i, tile_at(i), base)
            for part, (first, last) in enumerate(((0, ROUTE_TILE // 2), (ROUTE_TILE // 2, ROUTE_TILE), (ROUTE_TILE, NK - 4))):
                if part:
                    act.wait_ge(sem(f"{n}_cs"), part)
                    act.activation(R.cs, R.cs, ACT.Exp).then_inc(sem(f"{n}_ecs"), 1)
                if part == 2:
                    for a in range(TT):
                        act.wait_ge(free_sem(f"{n}_rt{a}"), freed(f"{n}_rt{a}"))
                with act.Fori(first // 4, last // 4) as it:
                    for k in range(4):
                        high((k + 2) % 4, it * 8 + 2 * (k + 2), it * 16 + tile_at(k + 2), base)
                        gelu(bass.ds(it * 4 + k, 1), k, it * 8 + 2 * (k + 1))
            for i in range(NK - 4, NK):
                if i + 2 < NK:
                    high((i + 2) % 4, 2 * (i + 2), tile_at(i + 2), base)
                gelu(slice(i, i + 1), i % 4, 2 * (i + 1))
            with act.Fori(0, T // TURN) as it:
                for k in range(TURN // 4):
                    act.wait_ge(sem(f"{n}_diff"), it * (TURN // 4) + (k + 1))
                    part = hot2[:, 4 * k:4 * k + 4, :]
                    act.activation(part, part.bitcast(F32), ACT.Abs).then_inc(sem(f"{n}_abs"), 1)
                    act.wait_ge(sem(f"{n}_abs"), it * (TURN // 4) + (k + 1))
                    act.activation(part, part.bitcast(F32), ACT.Relu, scale=-1.0, bias=one_col).then_inc(sem(f"{n}_hot2"), 1)
            base = SO[f"peer{l}_v"][0]
            with act.Fori(0, NK // 8) as it:
                for k in range(8):
                    c = base + k + k // 2
                    act.wait_ge(landed[c % RING], it * 48 + 16 * (c // RING + 1))
                    for j in range(2):
                        half = 2 * k + j
                        act.wait_ge(sem(f"{n}_half_free"), it * 16 + (2 * NK + half + 1))
                        act.activation(w_parts[half % HALVES][:, 0, :], ring[c % RING][:, j * 512:(j + 1) * 512],
                                       ACT.Copy).then_inc(sem(f"{n}_high"), 1)
                    if k == 0:
                        act.wait_ge(sem(f"{n}_table_free"), TURN // 4 + T // 4)
                    act.activation(a_parts[:, k % 2, 0, :], W[:, bass.ds(it * 8 + k, 1), :].rearrange("p i t -> p (i t)"),
                                   ACT.Copy).then_inc(sem(f"{n}_ahigh"), 1)
            back_act(act, n)

        def back_act(act, n):
            act.wait_ge(sem(f"{n}_sum"), 1)
            for a in range(4):
                act.activation(B.y[:, a, :], bank[4 + a][:, :], ACT.Copy).then_inc(signal(f"{n}_ysb"), 1)
                act.wait_ge(sem(f"{n}_ysb"), signalled(f"{n}_ysb"))

        def attention_act(act, n, heads):
            for h in range(heads):
                for b, cols in ((0, slice(0, P)), (1, slice(P, 3 * P))):
                    if h == 0 and b == 0:
                        act.wait_ge(sem(f"{n}_max"), 1)
                    ins = act.activation(A.p[:, h, cols], A.p[:, h, cols], ACT.Exp, bias=A.x[:, b, h:h + 1],
                                         accum_out=A.l[:, b, h:h + 1])
                ins.then_inc(signal(f"{n}_exp"), 1)
                act.wait_ge(sem(f"{n}_exp"), signalled(f"{n}_exp"))

        def attention_copies_act(act, n, heads):
            for h in range(heads):
                copy_act(act, A.pt[:, h % 2, :], f"{n}_pt{h}", lambda t: t[:, 0:384])

        def swa_act(act):
            for k in range(4):
                copy_act(act, S.k[:, k, :], f"kv_k{k}")
            for a in range(TT):
                copy_act(act, S.v[:, a, :], f"kv_v0{a}", lambda t: t[:, :])
            act.wait_ge(free_sem("kv_v01"), freed("kv_v01"))
            norm_act(act, "1a")
            for c in range(DC):
                copy_act(act, S.q[:, c, :], f"w_q{c}")
            act.wait_ge(sem("w_max"), 1)
            act.activation(A.m, A.m, ACT.Exp).then_inc(signal("w_sink"), 1)
            act.wait_ge(sem("w_sink"), signalled("w_sink"))
            attention_act(act, "w", SH)
            attention_copies_act(act, "w", SH)

        def mix_act(act):
            for c in range(8):
                copy_act(act, M.q[:, c, :], f"r_q{c}")
            for c in range(8):
                copy_act(act, M.k[:, c, :], f"r_k{c}")
            for nh in range(2):
                for a in range(TT):
                    copy_act(act, M.v[:, a, nh * 512:(nh + 1) * 512], f"r_v{nh}{a}", lambda t: t[:, :])
            for c in range(8):
                copy_act(act, M.g[:, c, :], f"r_g{c}", func=ACT.Silu)
            for c in range(3):
                copy_act(act, M.cq[:, c, :], f"m_cq{c}")
            for c in range(2):
                copy_act(act, M.ckv[:, c, :], f"m_ckv{c}")
            copy_act(act, M.kp[:, 0, :], "m_kpe")
            act.activation(M.sqc, M.cq, ACT.Square).then_inc(signal("norm_squares"), 1)
            act.wait_ge(sem("norm_squares"), signalled("norm_squares"))
            act.activation(M.sqk, M.ckv, ACT.Square).then_inc(signal("norm_squares"), 1)
            act.wait_ge(sem("norm_squares"), signalled("norm_squares"))
            for c in range(8):
                copy_act(act, M.gr[:, c, :], f"r_gate{c}", func=ACT.Sigmoid)
            for c in range(8):
                copy_act(act, M.gm[:, c, :], f"m_gate{c}", func=ACT.Sigmoid)
            for h in range(RH):
                copy_act(act, M.y[:, 2 * h:2 * h + 2, :], f"r_y{h}", lambda t: t[:, :].rearrange("p (e t) -> p e t", e=2))
            for h in range(RH):
                act.wait_ge(sem("r_cent"), h + 1)
                act.activation(M.sq[:, 2 * h:2 * h + 2, :], M.y[:, 2 * h:2 * h + 2, :], ACT.Square).then_inc(signal("r_sq"), 1)
                act.wait_ge(sem("r_sq"), signalled("r_sq"))
            root_act(act, "r", M.r)
            root_act(act, "cq", rs[:, :])
            root_act(act, "ckv", G2.r2)
            for i in range(12):
                copy_act(act, M.qn[:, i, :] if i < 8 else M.qp[:, i - 8, :], f"m_q{i}")
            for i in range(8):
                copy_act(act, M.kn[:, i, :], f"m_k{i}")
            for nh in range(2):
                for a in range(TT):
                    copy_act(act, M.vm[:, a, nh * 512:(nh + 1) * 512], f"m_v{nh}{a}", lambda t: t[:, :])
            attention_act(act, "m", MH)
            attention_copies_act(act, "m", MH)

        def moe_slot(k):
            c = SO["moe"][0] + k
            return c % RING, 16 * (c // RING + 1)

        def moe_act(act):
            act.wait_ge(sem("e_gx"), 1)
            act.activation(E.x8, E.x8, ACT.Exp).then_inc(signal("e_gexp"), 1)
            act.wait_ge(sem("e_gexp"), signalled("e_gexp"))
            act.wait_ge(sem("e_vx"), 1)
            act.activation(E.w[:, :, 0:1], E.w[:, :, 0:1], ACT.Exp).then_inc(signal("e_vexp"), 1)
            act.wait_ge(sem("e_vexp"), signalled("e_vexp"))
            copy_act(act, E.gt[0:NE, :], "e_gt", lambda t: t[0:NE, 0:T])
            for e in range(NE // 2):
                copy_act(act, E.gb[:, 2 * e:2 * e + 2, :], f"e_b{e}", lambda t: t[:, :].rearrange("p (e t) -> p e t", e=2))

            def highs(slots, step, land):
                for k in slots:
                    s, t0 = moe_slot(k)
                    act.wait_ge(landed[s], land(t0))
                    for j in range(2):
                        half = 2 * k + j
                        act.wait_ge(sem("e_half_free"), step(half + 1))
                        act.activation(w_parts[half % HALVES][:, 0, :], ring[s][:, j * 512:(j + 1) * 512],
                                       ACT.Copy).then_inc(sem("e_high"), 1)

            def silu(par, up_halves):
                act.wait_ge(sem("e_half_free"), up_halves)
                act.activation(E.sa[:, par, :], bank[2 * par][:, :], ACT.Silu).then_inc(sem("e_silu"), 1)

            def hidden_high(par, hidden):
                act.wait_ge(sem("e_hid"), hidden)
                act.activation(a_parts[:, 0, :, :], E.hid[:, par, :, :], ACT.Copy).then_inc(sem("e_hhigh"), 1)

            def expert(k, par, hidden, step, land):
                highs((k, k + 1), step, land)
                silu(par, step(2 * k + HALVES - (4 if k > 4 else 0)))
                highs((k + 2, k + 3), step, land)
                hidden_high(par, hidden)
                highs((k + 4, k + 5), step, land)

            same = lambda n: n
            highs(range(4), same, same)
            expert(4, 0, 1, same, same)
            with act.Fori(0, 7) as it:
                for j in range(4):
                    expert(10 + 6 * j, (1 + j) % 2, it * 4 + (2 + j), lambda n: it * 48 + n,
                           lambda n: it * (16 * 24 // RING) + n)
            for e in (30, 31):
                expert(6 * e - 2, (e - 1) % 2, e, same, same)
            silu(1, 2 * (6 * NE - 4) + HALVES)
            highs((6 * NE - 2, 6 * NE - 1), same, same)
            act.wait_ge(sem("e_half_free"), 2 * (6 * NE - 2) + HALVES)
            hidden_high(1, NE)
            back_act(act, "e")

        @block.scalar
        def _(act):
            for dst, src in ((vec[:, :], vecs), (cst[:, :], consts), (xT[:, :, :], xin.rearrange("c p t -> p c t")),
                             (G.z.rearrange("p h t -> p (h t)")[:, 0:T].bitcast(I32), pos), (G.wg2[0:RANK, :], wg2),
                             (G.cst, consts_g)):
                act.dma_start(dst, src).then_inc(sem("loaded"), 16)
            act.wait_ge(sem("loaded"), 16 * N_LOADS)
            mod_act(act)
            norm_act(act, "0a")
            rope_act(act)
            gla_act(act)
            act.wait_ge(free_sem("g_out7"), freed("g_out7"))
            norm_act(act, "0b")
            act.dma_start(R.subk, subk[:, 0:2, :]).then_inc(sem("p0_subk"), 16)
            peer_act(act, 0)
            act.wait_ge(free_sem("p0_y7"), freed("p0_y7"))
            act.dma_start(S.cst, consts_s).then_inc(sem("loaded_s"), 16)
            norm_act(act, "kv")
            swa_act(act)
            act.wait_ge(free_sem("w_out7"), freed("w_out7"))
            norm_act(act, "1b")
            act.dma_start(R.subk, subk[:, 2:4, :]).then_inc(sem("p1_subk"), 16)
            peer_act(act, 1)
            act.wait_ge(free_sem("p1_y7"), freed("p1_y7"))
            act.dma_start(M.cst, consts2).then_inc(sem("loaded2"), 16)
            act.wait_ge(free_sem("p1_y7"), freed("p1_y7"))
            norm_act(act, "mid")
            act.wait_ge(sem("norm_result"), results("mid"))
            norm_act(act, "2a")
            mix_act(act)
            act.wait_ge(free_sem("mix7"), freed("mix7"))
            norm_act(act, "2b")
            moe_act(act)
            act.wait_ge(free_sem("e_y7"), freed("e_y7"))
            norm_act(act, "out")

        def inv_root_dve(dve, u, r, tiles, width):
            for i, (tile, part) in enumerate(tiles):
                dve.wait_ge(full_sem(tile), filled(tile))
                t = tile_of(tile)
                dve.tensor_scalar(part, t[:, 0:T], 1.0 / width, EPS, ALU.mult, ALU.add).then_inc(free_sem(tile), 1)
                dve.wait_ge(free_sem(tile), freed(tile))
                dve.tensor_copy(mean[:, i, :], part).then_inc(signal("dve_step"), 1)
                dve.wait_ge(sem("dve_step"), signalled("dve_step"))
            dve.sem_inc(sem("norm_mean"), 1)
            dve.wait_ge(sem("norm_root"), ROOTS.index(u) + 1)
            dve.reciprocal(r, r).then_inc(signal("dve_step"), 1)
            dve.wait_ge(sem("dve_step"), signalled("dve_step"))
            m = mean[:, 0, :] if len(tiles) == 1 else mean[:, 0:len(tiles), :]
            dve.tensor_tensor(m, m, r, ALU.mult).then_inc(signal("dve_step"), 1)
            dve.wait_ge(sem("dve_step"), signalled("dve_step"))
            dve.tensor_tensor(m, m, r, ALU.mult).then_inc(signal("dve_step"), 1)
            dve.wait_ge(sem("dve_step"), signalled("dve_step"))
            dve.tensor_scalar(m, m, -0.5, 1.5, ALU.mult, ALU.add).then_inc(signal("dve_step"), 1)
            dve.wait_ge(sem("dve_step"), signalled("dve_step"))
            dve.tensor_tensor(r, r, m, ALU.mult).then_inc(signal("dve_step"), 1)
            dve.wait_ge(sem("dve_step"), signalled("dve_step"))

        def norm_dve(dve, u, gains, shifts, dst=None):
            inv_root_dve(dve, u, rs[:, :], [(f"n{u}_ss", rs[:, :])], D)
            dst = hT if dst is None else dst
            dve.tensor_tensor(dst[:, :, :], xT[:, :, :], rs[:, :].unsqueeze(1).broadcast_to([P, DC, T]),
                                         ALU.mult).then_inc(signal("dve_step"), 1)
            dve.wait_ge(sem("dve_step"), signalled("dve_step"))
            for c in range(DC):
                if shifts is None:
                    ins = dve.tensor_scalar(dst[:, c, :], dst[:, c, :], gains[:, c:c + 1], None, ALU.mult)
                else:
                    ins = dve.tensor_scalar(dst[:, c, :], dst[:, c, :], gains[:, c:c + 1], shifts[:, c:c + 1],
                                            ALU.mult, ALU.add)
                ins.then_inc(signal("norm_result"), 1)
                dve.wait_ge(sem("norm_result"), signalled("norm_result"))

        def parts_dve(dve, n):
            dve.tensor_copy(h_parts[:, 0, :, :], hT[:, :, :]).then_inc(signal("dve_step"), 1)
            dve.wait_ge(sem("dve_step"), signalled("dve_step"))
            dve.tensor_tensor(h_parts[:, 1, :, :], hT[:, :, :], h_parts[:, 0, :, :].bitcast(F32), ALU.subtract).then_inc(sem(f"{n}_hparts"), 1)

        def update_dve(dve, tile, gate):
            for c in range(DC):
                dve.wait_ge(full_sem(f"{tile}{c}"), filled(f"{tile}{c}"))
                t = tile_of(f"{tile}{c}")
                dve.scalar_tensor_tensor(xT[:, c, :], t[:, 0:T], gate[:, c:c + 1], xT[:, c, :],
                                                      ALU.mult, ALU.add).then_inc(free_sem(f"{tile}{c}"), 1)
                dve.wait_ge(free_sem(f"{tile}{c}"), freed(f"{tile}{c}"))

        def wrap(dve, r, tmp):
            for op, lim, step in ((ALU.is_gt, PI_IN, -TWO_PI), (ALU.is_lt, -PI_IN, TWO_PI)):
                dve.tensor_scalar(tmp, r, lim, step, op, ALU.mult).then_inc(signal("dve_step"), 1)
                dve.wait_ge(sem("dve_step"), signalled("dve_step"))
                dve.tensor_tensor(r, r, tmp, ALU.add).then_inc(signal("dve_step"), 1)
                dve.wait_ge(sem("dve_step"), signalled("dve_step"))
            dve.tensor_scalar(r, r, PI_IN, -PI_IN, ALU.min, ALU.max).then_inc(signal("dve_step"), 1)
            dve.wait_ge(sem("dve_step"), signalled("dve_step"))

        def mod_dve(dve):
            dve.wait_ge(sem("csig"), 2)
            dve.tensor_tensor(cact[:, :], cact[:, :], vec[:, VO["c"][0]:VO["c2"][1]], ALU.mult).then_inc(signal("cact"), 1)
            dve.wait_ge(sem("cact"), signalled("cact"))
            products_dve(dve)
            dve.wait_ge(full_sem("mod"), filled("mod"))
            t = tile_of("mod")
            dve.tensor_tensor(modv[:, 0:40], t[:, 0:40], V("mod_b")[:, 0:40], ALU.add).then_inc(free_sem("mod"), 1)
            dve.wait_ge(free_sem("mod"), freed("mod"))
            gains_dve(dve, ((0, "ng0a", 8), (1, "ng0b", 32)))

        def rope_dve(dve):
            ang, k, kf = G.b[:, 0, :], G.b[:, 1, :], G.b[:, 2, :]
            posi = G.z.rearrange("p h t -> p (h t)")[:, 0:T].bitcast(I32)
            inv, sign = C("cols")[:, 0:1], C("cols")[:, 1:2]
            dve.tensor_copy(ang, posi).then_inc(signal("dve_step"), 1)
            dve.wait_ge(sem("dve_step"), signalled("dve_step"))
            dve.tensor_scalar(ang, ang, inv, None, ALU.mult).then_inc(signal("dve_step"), 1)
            dve.wait_ge(sem("dve_step"), signalled("dve_step"))
            dve.tensor_scalar(k.bitcast(I32), ang, 1.0 / TWO_PI, None, ALU.mult).then_inc(signal("dve_step"), 1)
            dve.wait_ge(sem("dve_step"), signalled("dve_step"))
            dve.tensor_copy(kf, k.bitcast(I32)).then_inc(signal("dve_step"), 1)
            dve.wait_ge(sem("dve_step"), signalled("dve_step"))
            for c in (C1, C2, C3):
                dve.scalar_tensor_tensor(ang, kf, -c, ang, ALU.mult, ALU.add).then_inc(signal("dve_step"), 1)
                dve.wait_ge(sem("dve_step"), signalled("dve_step"))
            wrap(dve, ang, kf)
            dve.tensor_scalar(rope_s[:, :], ang, 1.0, None, ALU.mult).then_inc(signal("dve_step"), 1)
            dve.wait_ge(sem("dve_step"), signalled("dve_step"))
            dve.tensor_scalar(rope_c[:, :], ang, TWO_PI / 4, None, ALU.add).then_inc(signal("dve_step"), 1)
            dve.wait_ge(sem("dve_step"), signalled("dve_step"))
            wrap(dve, rope_c[:, :], kf)
            dve.sem_inc(sem("rope_args"), 1)
            dve.wait_ge(sem("rope_sin"), 2)
            dve.tensor_scalar(rope_s[:, :], rope_s[:, :], sign, None, ALU.mult).then_inc(signal("dve_step"), 1)
            dve.wait_ge(sem("dve_step"), signalled("dve_step"))

        def gains_dve(dve, which):
            for i, g, at in which:
                dve.scalar_tensor_tensor(gain[:, i, :], modv[:, at:at + 8], 1.0, V(g), ALU.add, ALU.mult).then_inc(signal("dve_step"), 1)
            dve.wait_ge(sem("dve_step"), signalled("dve_step"))

        def products_dve(dve):
            c_b = cact[:, 0:8].unsqueeze(2).broadcast_to([P, DC, P])
            with dve.Fori(0, 40 // RING) as it:
                for s in range(RING):
                    dve.wait_ge(landed[s], it * 16 + 16)
                    dve.wait_ge(sem("mod_col"), it * RING + (s + 1))
                    dve.tensor_tensor(mod_prod[s].rearrange("p (k n) -> p k n", k=DC),
                                      ring[s][:, :].rearrange("p (k n) -> p k n", k=DC), c_b,
                                      ALU.mult).then_inc(ring_free, 1)

        def mod(at):
            return modv[:, at:at + 8]

        def exp_dve(dve, dst, x, tmp, tmp2):
            k = tmp.bitcast(I32)
            dve.tensor_scalar(k, x, 1.0 / LN2, None, ALU.mult).then_inc(signal("dve_step"), 1)
            dve.wait_ge(sem("dve_step"), signalled("dve_step"))
            dve.tensor_copy(tmp2, k).then_inc(signal("dve_step"), 1)
            dve.wait_ge(sem("dve_step"), signalled("dve_step"))
            dve.scalar_tensor_tensor(x, tmp2, -LN2_HI, x, ALU.mult, ALU.add).then_inc(signal("dve_step"), 1)
            dve.wait_ge(sem("dve_step"), signalled("dve_step"))
            dve.scalar_tensor_tensor(x, tmp2, -LN2_LO, x, ALU.mult, ALU.add).then_inc(signal("dve_step"), 1)
            dve.wait_ge(sem("dve_step"), signalled("dve_step"))
            dve.tensor_scalar(k, tmp2, 127.0, None, ALU.add).then_inc(signal("dve_step"), 1)
            dve.wait_ge(sem("dve_step"), signalled("dve_step"))
            dve.tensor_scalar(k, k, 23, None, ALU.logical_shift_left).then_inc(signal("dve_step"), 1)
            dve.wait_ge(sem("dve_step"), signalled("dve_step"))
            c = [1.0]
            for i in range(1, 9):
                c.append(c[-1] / i)
            dve.tensor_scalar(dst, x, c[8], None, ALU.mult).then_inc(signal("dve_step"), 1)
            dve.wait_ge(sem("dve_step"), signalled("dve_step"))
            for i in range(7, 0, -1):
                dve.scalar_tensor_tensor(dst, dst, c[i], x, ALU.add, ALU.mult).then_inc(signal("dve_step"), 1)
                dve.wait_ge(sem("dve_step"), signalled("dve_step"))
            dve.scalar_tensor_tensor(dst, dst, 1.0, tmp, ALU.add, ALU.mult).then_inc(signal("dve_step"), 1)
            dve.wait_ge(sem("dve_step"), signalled("dve_step"))

        def gla_dve(dve):
            for h in range(GH):
                dve.wait_ge(full_sem(f"g_z{h}"), filled(f"g_z{h}"))
                t = tile_of(f"g_z{h}")
                dve.tensor_scalar(G.z[:, h, :], t[:, 0:T], V("gla_b")[:, h:h + 1], None, ALU.add).then_inc(free_sem(f"g_z{h}"), 1)
                dve.wait_ge(free_sem(f"g_z{h}"), freed(f"g_z{h}"))
            dve.scalar_tensor_tensor(G.e, G.z, -1.0, G.z, ALU.mult, ALU.min).then_inc(signal("g_abs"), 1)
            dve.wait_ge(sem("g_abs"), signalled("g_abs"))
            dve.wait_ge(sem("g_ln"), 1)
            dve.scalar_tensor_tensor(G.z, G.z, 0.0, G.e, ALU.min, ALU.add).then_inc(signal("dve_step"), 1)
            dve.wait_ge(sem("dve_step"), signalled("dve_step"))
            for h in range(GH):
                dve.tensor_tensor_scan(G.b[:, h, :], G.cst[:, P:P + T], G.z[:, h, :], 0.0, ALU.mult, ALU.add).then_inc(signal("dve_step"), 1)
                dve.wait_ge(sem("dve_step"), signalled("dve_step"))
            dve.tensor_scalar(G.b, G.b, 1.0 / TAU, -87.0, ALU.mult, ALU.max).then_inc(signal("dve_step"), 1)
            dve.wait_ge(sem("dve_step"), signalled("dve_step"))
            exp_dve(dve, G.z, G.b, G.e, G.e2)
            dve.reciprocal(G.e, G.z).then_inc(signal("dve_step"), 1)
            dve.wait_ge(sem("dve_step"), signalled("dve_step"))
            dve.wait_ge(free_sem("g_k3"), freed("g_k3"))
            dve.tensor_tensor(G.k, G.k, G.e, ALU.mult).then_inc(signal("g_kq"), 1)
            dve.wait_ge(sem("g_kq"), signalled("g_kq"))
            k4 = G.k.rearrange("p h (n c) -> p (h n) c", c=GC)
            kd4 = G.kd.rearrange("p h (n c) -> p (h n) c", c=GC)
            z4 = G.z.rearrange("p h (n c) -> p (h n) c", c=GC)
            dve.tensor_copy(G.dec.rearrange("p h n -> p (h n)"), z4[:, :, GC - 1]).then_inc(signal("dve_step"), 1)
            dve.wait_ge(sem("dve_step"), signalled("dve_step"))
            dve.tensor_tensor(kd4, k4, z4[:, :, GC - 1:GC].broadcast_to([P, GH * NCH, GC]), ALU.mult).then_inc(signal("g_kd"), 1)
            dve.wait_ge(sem("g_kd"), signalled("g_kd"))
            dve.scalar_tensor_tensor(G.q, G.q, float(P) ** -0.5, G.z, ALU.mult, ALU.mult).then_inc(signal("g_kq"), 1)
            dve.wait_ge(sem("g_kq"), signalled("g_kq"))
            dve.wait_ge(sem("g_sig"), 1)
            dve.tensor_tensor(G.og, G.og, G.o, ALU.mult).then_inc(signal("dve_step"), 1)
            dve.wait_ge(sem("dve_step"), signalled("dve_step"))
            for h in range(GH):
                dve.wait_ge(full_sem(f"g_s{h}"), filled(f"g_s{h}"))
                t = tile_of(f"g_s{h}")
                dve.tensor_tensor(G.sm[:, h, :].rearrange("p (b t) -> p b t", b=2),
                                               t[:, 0:T].rearrange("p (b t) -> p b t", b=2),
                                               G.cst[:, 0:P].unsqueeze(1).broadcast_to([P, 2, P]), ALU.mult).then_inc(free_sem(f"g_s{h}"), 1)
                dve.wait_ge(free_sem(f"g_s{h}"), freed(f"g_s{h}"))
            for n in range(NCH - 1):
                for h in range(GH):
                    dve.wait_ge(full_sem(f"g_u{n}{h}"), filled(f"g_u{n}{h}"))
                    t = tile_of(f"g_u{n}{h}")
                    new = G.st[:, h, (n + 1) % 2, :]
                    if n == 0:
                        ins = dve.tensor_copy(new, t[:, 0:GDV])
                    else:
                        ins = dve.scalar_tensor_tensor(new, G.st[:, h, n % 2, :], G.dec[:, h, n:n + 1], t[:, 0:GDV],
                                                       ALU.mult, ALU.add)
                    ins.then_inc(free_sem(f"g_u{n}{h}"), 1)
                    dve.wait_ge(free_sem(f"g_u{n}{h}"), freed(f"g_u{n}{h}"))
                    dve.sem_inc(sem("g_state"), 1)
            inv_root_dve(dve, "g", G.r, [(f"g_ss{h}", G.r[:, h, :]) for h in range(GH)], GDV)
            for h in range(GH):
                for e in range(2):
                    dve.scalar_tensor_tensor(G.o[:, 2 * h + e, :], bank[4 + h][:, e * T:(e + 1) * T],
                                                        V("gla_ng")[:, e:e + 1], G.r[:, h, :], ALU.mult, ALU.mult).then_inc(signal("dve_step"), 1)
                    dve.wait_ge(sem("dve_step"), signalled("dve_step"))
            dve.tensor_tensor(G.o, G.o, G.og, ALU.mult).then_inc(signal("g_y"), 1)
            dve.wait_ge(sem("g_y"), signalled("g_y"))
            update_dve(dve, "g_out", mod(16))

        def peer_dve(dve, l):
            n = f"p{l}"
            iota16 = iota[:, 0:TOPK]
            parts_dve(dve, n)
            for a in range(TT):
                v, ix, ixf = R.v[:, a], R.ix[:, a].bitcast(U32), R.ixf[:, a]
                for g in range(16):
                    if g % 2 == 0:
                        dve.wait_ge(free_sem(f"{n}_s{a}{g // 2}"), freed(f"{n}_s{a}{g // 2}"))
                    ins = dve.max(v[:, g, 0:8], R.s[:, a, g, :])
                ins.then_inc(signal("dve_step"), 1)
                dve.wait_ge(sem("dve_step"), signalled("dve_step"))
                for g in range(16):
                    dve.max_index(ix[:, g, 0:8], v[:, g, 0:8], R.s[:, a, g, :])
                    ins = dve.match_replace(R.s2[:, g, :], v[:, g, 0:8], R.s[:, a, g, :], LOW)
                ins.then_inc(signal("dve_step"), 1)
                dve.wait_ge(sem("dve_step"), signalled("dve_step"))
                for g in range(16):
                    ins = dve.max(v[:, g, 8:16], R.s2[:, g, :])
                ins.then_inc(signal("dve_step"), 1)
                dve.wait_ge(sem("dve_step"), signalled("dve_step"))
                for g in range(16):
                    ins = dve.max_index(ix[:, g, 8:16], v[:, g, 8:16], R.s2[:, g, :])
                ins.then_inc(signal("dve_step"), 1)
                dve.wait_ge(sem("dve_step"), signalled("dve_step"))
                dve.tensor_copy(ixf, ix).then_inc(signal("dve_step"), 1)
                dve.wait_ge(sem("dve_step"), signalled("dve_step"))
                if a == 0:
                    dve.wait_ge(free_sem(f"{n}_s{TT - 1}{PH - 1}"), freed(f"{n}_s{TT - 1}{PH - 1}"))
                v4 = v.rearrange("p (h f) k -> p h f k", f=2)
                i4 = ixf.rearrange("p (h f) k -> p h f k", f=2)
                c4 = R.cand.rearrange("p h (x y) -> p h x y", x=TOPK)
                dve.tensor_tensor(c4, v4[:, :, 0, :].unsqueeze(3).broadcast_to([P, PH, TOPK, TOPK]),
                                             v4[:, :, 1, :].unsqueeze(2).broadcast_to([P, PH, TOPK, TOPK]), ALU.add).then_inc(signal("dve_step"), 1)
                dve.wait_ge(sem("dve_step"), signalled("dve_step"))
                ci = R.ci.bitcast(U32)
                if a:
                    dve.wait_ge(sem(f"{n}_ecs"), a)
                for h in range(PH):
                    ins = dve.max(R.cs[:, h, 0:8], R.cand[:, h, :])
                ins.then_inc(signal("dve_step"), 1)
                dve.wait_ge(sem("dve_step"), signalled("dve_step"))
                for h in range(PH):
                    dve.max_index(ci[:, h, 0:8], R.cs[:, h, 0:8], R.cand[:, h, :])
                    ins = dve.match_replace(R.cand2[:, h, :], R.cs[:, h, 0:8], R.cand[:, h, :], LOW)
                ins.then_inc(signal("dve_step"), 1)
                dve.wait_ge(sem("dve_step"), signalled("dve_step"))
                for h in range(PH):
                    ins = dve.max(R.cs[:, h, 8:16], R.cand2[:, h, :])
                ins.then_inc(signal("dve_step"), 1)
                dve.wait_ge(sem("dve_step"), signalled("dve_step"))
                for h in range(PH):
                    ins = dve.max_index(ci[:, h, 8:16], R.cs[:, h, 8:16], R.cand2[:, h, :])
                ins.then_inc(signal("dve_step"), 1)
                dve.wait_ge(sem("dve_step"), signalled("dve_step"))
                dve.tensor_copy(R.sum[:, 0:8], R.cs[:, :, 0]).then_inc(signal("dve_step"), 1)
                dve.wait_ge(sem("dve_step"), signalled("dve_step"))
                dve.tensor_tensor(R.cs, R.cs, R.sum[:, 0:8].unsqueeze(2).broadcast_to([P, PH, TOPK]),
                                            ALU.subtract).then_inc(signal(f"{n}_cs"), 1)
                dve.wait_ge(sem(f"{n}_cs"), signalled(f"{n}_cs"))
                cif = R.ci.rearrange("p h k -> p (h k)").bitcast(U32)
                dve.tensor_scalar(R.ca.bitcast(U32), cif, 4, None, ALU.logical_shift_right).then_inc(signal("dve_step"), 1)
                dve.wait_ge(sem("dve_step"), signalled("dve_step"))
                dve.tensor_scalar(R.cb.bitcast(U32), cif, 15, None, ALU.bitwise_and).then_inc(signal("dve_step"), 1)
                dve.wait_ge(sem("dve_step"), signalled("dve_step"))
                dve.tensor_copy(R.caf, R.ca.bitcast(U32)).then_inc(signal("dve_step"), 1)
                dve.wait_ge(sem("dve_step"), signalled("dve_step"))
                dve.tensor_copy(R.cbf, R.cb.bitcast(U32)).then_inc(signal("dve_step"), 1)
                dve.wait_ge(sem("dve_step"), signalled("dve_step"))
                for f, (rank, wide) in enumerate(((R.caf, R.cand), (R.cbf, R.cand2))):
                    w3 = wide.rearrange("p h (k x) -> p (h k) x", x=TOPK)
                    w4 = wide.rearrange("p h (k x) -> p h k x", x=TOPK)
                    dve.tensor_tensor(w3, rank.unsqueeze(2).broadcast_to([P, P, TOPK]),
                                                 iota16.unsqueeze(1).broadcast_to([P, P, TOPK]), ALU.is_equal).then_inc(signal("dve_step"), 1)
                    dve.wait_ge(sem("dve_step"), signalled("dve_step"))
                    dve.tensor_tensor(w4, w4, i4[:, :, f, :].unsqueeze(2).broadcast_to(
                        [P, PH, TOPK, TOPK]), ALU.mult).then_inc(signal("dve_step"), 1)
                    dve.wait_ge(sem("dve_step"), signalled("dve_step"))
                    dve.tensor_reduce(R.pick[:, a, f, :], w3, AX.X, ALU.add).then_inc(signal("dve_step"), 1)
                    dve.wait_ge(sem("dve_step"), signalled("dve_step"))
                dve.wait_ge(sem(f"{n}_ecs"), a + 1)
                dve.tensor_reduce(R.sum[:, 0:8], R.cs, AX.X, ALU.add).then_inc(signal("dve_step"), 1)
                dve.wait_ge(sem("dve_step"), signalled("dve_step"))
                dve.reciprocal(R.sum[:, 8:16], R.sum[:, 0:8]).then_inc(signal("dve_step"), 1)
                dve.wait_ge(sem("dve_step"), signalled("dve_step"))
                dve.tensor_tensor(R.pick[:, a, 2, :].rearrange("p (h k) -> p h k", h=PH), R.cs,
                                            R.sum[:, 8:16].unsqueeze(2).broadcast_to([P, PH, TOPK]), ALU.mult).then_inc(signal(f"{n}_picked"), 1)
                dve.wait_ge(sem(f"{n}_picked"), signalled(f"{n}_picked"))
            for a in range(TT):
                dve.wait_ge(full_sem(f"{n}_rt{a}"), filled(f"{n}_rt{a}"))
                t = tile_of(f"{n}_rt{a}")
                dve.tensor_copy(route[:, :, a * P:(a + 1) * P],
                                             t[:, 0:384].rearrange("p (k t) -> p k t", k=3)).then_inc(free_sem(f"{n}_rt{a}"), 1)
                dve.wait_ge(free_sem(f"{n}_rt{a}"), freed(f"{n}_rt{a}"))
            dve.wait_ge(sem(f"{n}_gelu"), NK)

            def apply_tables(it, k):
                dve.wait_ge(sem(f"{n}_hot_free"), it * TURN + (TURN + 4 * k + 4))
                part = W[:, :, bass.ds(it * TURN + 4 * k, 4)]
                dve.tensor_tensor(part, part, bank[4 + k][:, :].rearrange("p (t i) -> p i t", t=4),
                                  ALU.mult).then_inc(sem(f"{n}_table_free"), 1)

            def one_hots(it, s):
                dve.wait_ge(sem(f"{n}_hot_free"), it * TURN + (s + 1))
                tok = bass.ds(it * TURN + s, 1)
                dve.tensor_scalar(hot1[:, s, :], iota, route[:, 0, tok], route[:, 2, tok],
                                  ALU.is_equal, ALU.mult).then_inc(sem(f"{n}_hot"), 1)

            for s in range(TURN):
                one_hots(0, s)
            with dve.Fori(0, T // TURN - 1) as it:
                for k in range(TURN // 4):
                    apply_tables(it, k)
                    for s in range(4 * k, 4 * k + 4):
                        one_hots(it + 1, s)
            for k in range(TURN // 4):
                apply_tables(T // TURN - 1, k)
            base = SO[f"peer{l}_v"][0]
            prods = hT[:, 0:4, :].rearrange("p c t -> p (c t)"), mean[:, :, :].rearrange("p c t -> p (c t)")
            for first, last, col in ((0, 16, 0),) if l == 0 else ((0, 2, 0), (2, 16, 8)):
                c_b = cact[:, col:col + 8].unsqueeze(2).broadcast_to([P, DC, P])
                with dve.Fori(first, last) as it:
                    for k in range(8):
                        c = base + k + k // 2
                        for j in range(2):
                            half = 2 * k + j
                            dve.wait_ge(sem(f"{n}_high"), it * 16 + (2 * NK + half + 1))
                            w = w_parts[half % HALVES]
                            dve.tensor_tensor(w[:, 1, :], ring[c % RING][:, j * 512:(j + 1) * 512],
                                              w[:, 0, :].bitcast(F32), ALU.subtract).then_inc(sem(f"{n}_low"), 1)
                        dve.wait_ge(sem(f"{n}_ahigh"), it * 8 + (k + 1))
                        dve.tensor_tensor(a_parts[:, k % 2, 1, :], W[:, bass.ds(it * 8 + k, 1), :].rearrange("p i t -> p (i t)"),
                                          a_parts[:, k % 2, 0, :].bitcast(F32), ALU.subtract).then_inc(sem(f"{n}_gated"), 1)
                        if k % 2:
                            m = k // 2
                            c += 1
                            dve.wait_ge(landed[c % RING], it * 48 + 16 * (c // RING + 1))
                            dve.wait_ge(sem(f"{n}_part"), it * 4 + (m + 1))
                            dve.tensor_tensor(prods[m % 2].rearrange("p (k n) -> p k n", k=DC),
                                              ring[c % RING][:, :].rearrange("p (k n) -> p k n", k=DC), c_b,
                                              ALU.mult).then_inc(sem(f"{n}_prod"), 1)
            dve.wait_ge(sem(f"{n}_sum"), 1)
            lo, hi = ((40, 104), (104, 160))[l]
            dve.tensor_tensor(modv[:, lo:hi], bank[0][:, 1:1 + hi - lo], V("mod_b")[:, lo:hi], ALU.add).then_inc(sem(f"{n}_mods"), 1)
            dve.wait_ge(sem(f"{n}_mods"), 1)
            gains_dve(dve, ((2, "ng1a", 72), (3, "ng1b", 96), (4, "kvg", 56)) if l == 0 else
                      ((5, "n1", 120), (6, "n2", 144)))
            update_dve(dve, f"{n}_y", mod(40 if l == 0 else 104))

        def attention_dve(dve, n, heads, scale, mask, sinks, outp):
            for h in range(heads):
                dve.wait_ge(full_sem(f"{n}_s{h}"), filled(f"{n}_s{h}"))
                t = tile_of(f"{n}_s{h}")
                dve.scalar_tensor_tensor(A.p[:, h, :], t[:, 0:384], scale, mask, ALU.mult, ALU.add).then_inc(free_sem(f"{n}_s{h}"), 1)
                dve.wait_ge(free_sem(f"{n}_s{h}"), freed(f"{n}_s{h}"))
            dve.tensor_reduce(A.m[:, 0, 0:heads], A.p[:, 0:heads, 0:P], AX.X, ALU.max).then_inc(signal("dve_step"), 1)
            dve.wait_ge(sem("dve_step"), signalled("dve_step"))
            dve.tensor_reduce(A.m[:, 1, 0:heads], A.p[:, 0:heads, P:3 * P], AX.X, ALU.max).then_inc(signal("dve_step"), 1)
            dve.wait_ge(sem("dve_step"), signalled("dve_step"))
            if sinks is not None:
                sk = sinks.unsqueeze(1).broadcast_to([P, 2, heads])
                dve.tensor_tensor(A.m, A.m, sk, ALU.max).then_inc(signal("dve_step"), 1)
                dve.wait_ge(sem("dve_step"), signalled("dve_step"))
                dve.tensor_scalar(A.x, A.m, -1.0, None, ALU.mult).then_inc(signal("dve_step"), 1)
                dve.wait_ge(sem("dve_step"), signalled("dve_step"))
                dve.tensor_tensor(A.m, sk, A.m, ALU.subtract).then_inc(signal("dve_step"), 1)
                dve.wait_ge(sem("dve_step"), signalled("dve_step"))
            else:
                dve.tensor_scalar(A.x[:, :, 0:heads], A.m[:, :, 0:heads], -1.0, None, ALU.mult).then_inc(signal("dve_step"), 1)
                dve.wait_ge(sem("dve_step"), signalled("dve_step"))
            dve.sem_inc(sem(f"{n}_max"), 1)
            dve.wait_ge(sem(f"{n}_exp"), heads)
            if sinks is not None:
                dve.wait_ge(sem("w_sink"), 1)
                dve.tensor_tensor(A.l, A.l, A.m, ALU.add).then_inc(signal("dve_step"), 1)
                dve.wait_ge(sem("dve_step"), signalled("dve_step"))
            dve.reciprocal(A.l[:, :, 0:heads], A.l[:, :, 0:heads]).then_inc(signal("dve_step"), 1)
            dve.wait_ge(sem("dve_step"), signalled("dve_step"))
            for h in range(heads):
                for b, cols in ((0, slice(0, P)), (1, slice(P, 3 * P))):
                    ins = dve.tensor_scalar(A.p[:, h, cols], A.p[:, h, cols], A.l[:, b, h:h + 1], None, ALU.mult)
                ins.then_inc(signal(f"{n}_p"), 1)
                dve.wait_ge(sem(f"{n}_p"), signalled(f"{n}_p"))
            for h in range(heads):
                dve.wait_ge(full_sem(f"{n}_o{h}"), filled(f"{n}_o{h}"))
                t = tile_of(f"{n}_o{h}")
                outp(h, t).then_inc(free_sem(f"{n}_o{h}"), 1)
                dve.wait_ge(free_sem(f"{n}_o{h}"), freed(f"{n}_o{h}"))

        def rotate_dve(dve, x, tile, cos, sin, tmp, name):
            dve.wait_ge(full_sem(tile), filled(tile))
            t = tile_of(tile)
            dve.tensor_tensor(tmp, t[:, 0:T], sin, ALU.mult).then_inc(free_sem(tile), 1)
            dve.wait_ge(free_sem(tile), freed(tile))
            dve.tensor_tensor(x, x, cos, ALU.mult).then_inc(signal("dve_step"), 1)
            dve.wait_ge(sem("dve_step"), signalled("dve_step"))
            dve.tensor_tensor(x, x, tmp, ALU.add).then_inc(signal(name), 1)
            dve.wait_ge(sem(name), signalled(name))

        def swa_dve(dve):
            for k in range(4):
                rotate_dve(dve, S.k[:, k, :], f"kv_r{k}", rope_c[:, :], rope_s[:, :], S.tmp, "w_kr")
            norm_dve(dve, "1a", gain[:, 2, :], mod(64))
            for c in range(DC):
                rotate_dve(dve, S.q[:, c, :], f"w_r{c}", rope_c[:, :], rope_s[:, :], S.tmp, "w_qr")

            def outp(h, t):
                rows = slice((h % 2) * SHD, (h % 2 + 1) * SHD)
                return dve.tensor_copy(A.o[rows, h // 2, :], t[rows, 0:T])

            dve.wait_ge(sem("loaded_s"), 16)
            attention_dve(dve, "w", SH, SHD ** -0.5, S.mask, V("sinks"), outp)
            update_dve(dve, "w_out", mod(64 + 16))

        def mix_dve(dve):
            dve.wait_ge(sem("loaded2"), 16)
            c2 = lambda name: M.cst[:, C2O[name][0]:C2O[name][1]]
            cosb = c2("rcos").unsqueeze(1).broadcast_to([P, RH, T])
            sinb = c2("rsin").unsqueeze(1).broadcast_to([P, RH, T])
            for name, x in (("q", M.q), ("k", M.k)):
                dve.wait_ge(free_sem(f"r_{name}6"), freed(f"r_{name}6"))
                dve.wait_ge(free_sem(f"r_{name}7"), freed(f"r_{name}7"))
                x4 = x.rearrange("p (h f) t -> p h f t", f=2)
                x1, x2 = x4[:, :, 0, :], x4[:, :, 1, :]
                t1, t2 = M.t[:, 0:4, :], M.t[:, 4:8, :]
                dve.tensor_tensor(t1, x2, sinb, ALU.mult).then_inc(signal("dve_step"), 1)
                dve.wait_ge(sem("dve_step"), signalled("dve_step"))
                dve.tensor_tensor(t2, x1, sinb, ALU.mult).then_inc(signal("dve_step"), 1)
                dve.wait_ge(sem("dve_step"), signalled("dve_step"))
                dve.tensor_tensor(x1, x1, cosb, ALU.mult).then_inc(signal("dve_step"), 1)
                dve.wait_ge(sem("dve_step"), signalled("dve_step"))
                dve.tensor_tensor(x2, x2, cosb, ALU.mult).then_inc(signal("dve_step"), 1)
                dve.wait_ge(sem("dve_step"), signalled("dve_step"))
                dve.tensor_tensor(x1, x1, t1, ALU.subtract).then_inc(signal("r_rot"), 1)
                dve.wait_ge(sem("r_rot"), signalled("r_rot"))
                dve.tensor_tensor(x2, x2, t2, ALU.add).then_inc(signal("r_rot"), 1)
                dve.wait_ge(sem("r_rot"), signalled("r_rot"))
            dec = c2("decay").rearrange("p (h t) -> p h t", h=RH)
            for h in range(RH):
                dve.wait_ge(full_sem(f"r_s{h}"), filled(f"r_s{h}"))
                t = tile_of(f"r_s{h}")
                dve.scalar_tensor_tensor(M.s[:, h, :], t[:, 0:384], 256.0 ** -0.5, dec[:, h, :],
                                                      ALU.mult, ALU.mult).then_inc(free_sem(f"r_s{h}"), 1)
                dve.wait_ge(free_sem(f"r_s{h}"), freed(f"r_s{h}"))
            for h in range(RH):
                dve.wait_ge(full_sem(f"r_mean{h}"), filled(f"r_mean{h}"))
                t = tile_of(f"r_mean{h}")
                y = M.y[:, 2 * h:2 * h + 2, :]
                dve.scalar_tensor_tensor(y, t[:, 0:T].unsqueeze(1).broadcast_to([P, 2, T]), -1.0 / 256, y,
                                                      ALU.mult, ALU.add).then_inc(free_sem(f"r_mean{h}"), 1)
                dve.wait_ge(free_sem(f"r_mean{h}"), freed(f"r_mean{h}"))
                dve.sem_inc(sem("r_cent"), 1)
            inv_root_dve(dve, "r", M.r, [(f"r_var{h}", M.r[:, h, :]) for h in range(RH)], 256)
            y4 = M.y.rearrange("p (h f) t -> p h f t", f=2)
            for f in range(2):
                dve.tensor_tensor(y4[:, :, f, :], y4[:, :, f, :], M.r, ALU.mult).then_inc(signal("dve_step"), 1)
                dve.wait_ge(sem("dve_step"), signalled("dve_step"))
            dve.wait_ge(free_sem("r_g7"), freed("r_g7"))
            dve.tensor_tensor(M.y, M.y, M.g, ALU.mult).then_inc(signal("r_yn"), 1)
            dve.wait_ge(sem("r_yn"), signalled("r_yn"))
            inv_root_dve(dve, "cq", rs[:, :], [("ncq_ss", rs[:, :])], QL)
            for c in range(3):
                dve.scalar_tensor_tensor(M.cq[:, c, :], M.cq[:, c, :], V("qn")[:, c:c + 1], rs[:, :],
                                                   ALU.mult, ALU.mult).then_inc(signal("m_cqn"), 1)
                dve.wait_ge(sem("m_cqn"), signalled("m_cqn"))
            inv_root_dve(dve, "ckv", G2.r2, [("nckv_ss", G2.r2)], KVL)
            for c in range(2):
                dve.scalar_tensor_tensor(M.ckv[:, c, :], M.ckv[:, c, :], V("kvn")[:, c:c + 1], G2.r2,
                                                   ALU.mult, ALU.mult).then_inc(signal("m_ckvn"), 1)
                dve.wait_ge(sem("m_ckvn"), signalled("m_ckvn"))
            for c in range(DC):
                dve.wait_ge(full_sem(f"r_o{c}"), filled(f"r_o{c}"))
                t = tile_of(f"r_o{c}")
                dve.tensor_tensor(M.gr[:, c, :], t[:, 0:T], M.gr[:, c, :], ALU.mult).then_inc(free_sem(f"r_o{c}"), 1)
                dve.wait_ge(free_sem(f"r_o{c}"), freed(f"r_o{c}"))
            for c in range(5):
                rotate_dve(dve, M.qp[:, c, :] if c < 4 else M.kp[:, 0, :], f"m_r{c}", c2("mcos"), c2("msin"),
                           M.t[:, 0, :], "m_rot0" if c == 4 else "m_rot")
            for f in range(2):
                dve.tensor_scalar(M.kp[:, 1 + f, :], M.kp[:, 0, :], C("cols")[:, 2 + f:3 + f], None,
                                            ALU.mult).then_inc(signal("m_rot"), 1)
                dve.wait_ge(sem("m_rot"), signalled("m_rot"))

            def outp(h, t):
                return dve.tensor_copy(A.o[:, h, :], t[:, 0:T])

            attention_dve(dve, "m", MH, float(192) ** -0.5, c2("mmask"), None, outp)
            for c in range(DC):
                dve.wait_ge(full_sem(f"m_out{c}"), filled(f"m_out{c}"))
                t = tile_of(f"m_out{c}")
                dve.tensor_tensor(M.gm[:, c, :], t[:, 0:T], M.gm[:, c, :], ALU.mult).then_inc(free_sem(f"m_out{c}"), 1)
                dve.wait_ge(free_sem(f"m_out{c}"), freed(f"m_out{c}"))
            dve.tensor_tensor(M.mg, M.gr, M.gm, ALU.add).then_inc(signal("merged"), 1)
            dve.wait_ge(sem("merged"), signalled("merged"))
            update_dve(dve, "mix", mod(112 + 16))

        def moe_dve(dve):
            parts_dve(dve, "e")
            dve.memset(E.g8, LOW).then_inc(signal("dve_step"), 1)
            dve.wait_ge(sem("dve_step"), signalled("dve_step"))
            for a in range(TT):
                dve.wait_ge(full_sem(f"e_l{a}"), filled(f"e_l{a}"))
                t = tile_of(f"e_l{a}")
                dve.tensor_tensor(E.l[:, a, :], t[:, 0:NG + NE], V("rb"), ALU.add).then_inc(free_sem(f"e_l{a}"), 1)
                dve.wait_ge(free_sem(f"e_l{a}"), freed(f"e_l{a}"))
            dve.tensor_copy(E.g8[:, :, 0:NG], E.l[:, :, 0:NG]).then_inc(signal("dve_step"), 1)
            dve.wait_ge(sem("dve_step"), signalled("dve_step"))
            i8 = E.i8.bitcast(U32)

            def top(src):
                for a in range(TT):
                    ins = dve.max(E.m8[:, a, :], src[:, a, :])
                ins.then_inc(signal("dve_step"), 1)
                dve.wait_ge(sem("dve_step"), signalled("dve_step"))
                for a in range(TT):
                    ins = dve.max_index(i8[:, a, :], E.m8[:, a, :], src[:, a, :])
                ins.then_inc(signal("dve_step"), 1)
                dve.wait_ge(sem("dve_step"), signalled("dve_step"))
                dve.tensor_copy(E.if8, i8).then_inc(signal("dve_step"), 1)
                dve.wait_ge(sem("dve_step"), signalled("dve_step"))

            def iota_b(k):
                return iota[:, 0:k].unsqueeze(1).broadcast_to([P, TT, k])

            def bc(ap, k):
                return ap.broadcast_to([P, TT, k])

            top(E.g8)
            dve.tensor_tensor(E.oh, bc(E.if8[:, :, 0:1], NG), iota_b(NG), ALU.is_equal).then_inc(signal("dve_step"), 1)
            dve.wait_ge(sem("dve_step"), signalled("dve_step"))
            dve.tensor_tensor(E.x8, E.g8, bc(E.m8[:, :, 0:1], 8), ALU.subtract).then_inc(signal("e_gx"), 1)
            dve.wait_ge(sem("e_gx"), signalled("e_gx"))
            t4 = E.tmp.rearrange("p a (g e) -> p a g e", g=NG)
            l4 = E.l[:, :, NG:NG + NE].rearrange("p a (g e) -> p a g e", g=NG)
            dve.tensor_tensor(t4, l4, E.oh.unsqueeze(3).broadcast_to([P, TT, NG, EG]), ALU.mult).then_inc(signal("dve_step"), 1)
            dve.wait_ge(sem("dve_step"), signalled("dve_step"))
            dve.tensor_reduce(E.g8, E.tmp.rearrange("p a (g e) -> p a e g", g=NG), AX.X, ALU.add).then_inc(signal("dve_step"), 1)
            dve.wait_ge(sem("dve_step"), signalled("dve_step"))
            top(E.g8)
            dve.tensor_tensor(E.w[:, :, 0:1], E.m8[:, :, 1:2], E.m8[:, :, 0:1], ALU.subtract).then_inc(signal("e_vx"), 1)
            dve.wait_ge(sem("e_vx"), signalled("e_vx"))
            dve.wait_ge(sem("e_gexp"), 1)
            dve.tensor_reduce(E.w[:, :, 1:2], E.x8[:, :, 0:NG], AX.X, ALU.add).then_inc(signal("dve_step"), 1)
            dve.wait_ge(sem("dve_step"), signalled("dve_step"))
            dve.wait_ge(sem("e_vexp"), 1)
            dve.scalar_tensor_tensor(E.w[:, :, 4:5], E.w[:, :, 0:1], 1.0, E.w[:, :, 1:2], ALU.add, ALU.mult).then_inc(signal("dve_step"), 1)
            dve.wait_ge(sem("dve_step"), signalled("dve_step"))
            dve.reciprocal(E.w[:, :, 2:3], E.w[:, :, 4:5]).then_inc(signal("dve_step"), 1)
            dve.wait_ge(sem("dve_step"), signalled("dve_step"))
            dve.tensor_tensor(E.w[:, :, 3:4], E.w[:, :, 0:1], E.w[:, :, 2:3], ALU.mult).then_inc(signal("dve_step"), 1)
            dve.wait_ge(sem("dve_step"), signalled("dve_step"))
            for k, dst in ((0, E.ew), (1, E.ew2)):
                dve.tensor_tensor(dst, bc(E.if8[:, :, k:k + 1], EG), iota_b(EG), ALU.is_equal).then_inc(signal("dve_step"), 1)
                dve.wait_ge(sem("dve_step"), signalled("dve_step"))
                dve.tensor_tensor(dst, dst, bc(E.w[:, :, 2 + k:3 + k], EG), ALU.mult).then_inc(signal("dve_step"), 1)
                dve.wait_ge(sem("dve_step"), signalled("dve_step"))
            dve.tensor_tensor(E.ew, E.ew, E.ew2, ALU.add).then_inc(signal("dve_step"), 1)
            dve.wait_ge(sem("dve_step"), signalled("dve_step"))
            dve.tensor_tensor(E.gate.rearrange("p a (g e) -> p a g e", g=NG),
                                        E.oh.unsqueeze(3).broadcast_to([P, TT, NG, EG]),
                                        E.ew.unsqueeze(2).broadcast_to([P, TT, NG, EG]), ALU.mult).then_inc(signal("e_gate"), 1)
            dve.wait_ge(sem("e_gate"), signalled("e_gate"))
            for e in range(NE // 2 - 4, NE // 2):
                dve.wait_ge(free_sem(f"e_b{e}"), freed(f"e_b{e}"))

            def lows(slots, step):
                for k in slots:
                    for j in range(2):
                        half = 2 * k + j
                        dve.wait_ge(sem("e_high"), step(half + 1))
                        w = w_parts[half % HALVES]
                        dve.tensor_tensor(w[:, 1, :], ring[moe_slot(k)[0]][:, j * 512:(j + 1) * 512],
                                          w[:, 0, :].bitcast(F32), ALU.subtract).then_inc(sem("e_low"), 1)

            def hidden(par, e, count):
                dve.wait_ge(sem("e_silu"), count)
                dve.tensor_tensor(E.hp[:, par, :], E.sa[:, par, :], bank[2 * par + 1][:, :], ALU.mult)\
                   .then_inc(sem("e_prod"), 1)
                dve.wait_ge(sem("e_prod"), count)
                dve.tensor_tensor(E.hid[:, par, :, :], E.hp[:, par, :].rearrange("p (f t) -> p f t", f=2),
                                  E.gb[:, e, :].broadcast_to([P, 2, T]), ALU.mult)\
                   .then_inc(sem("e_hid"), 1)

            def hidden_low(par, count):
                dve.wait_ge(sem("e_hhigh"), count)
                dve.tensor_tensor(a_parts[:, 1, :, :], E.hid[:, par, :, :], a_parts[:, 0, :, :].bitcast(F32),
                                  ALU.subtract).then_inc(sem("e_hlow"), 1)

            def expert(k, par, e, count, step):
                lows((k, k + 1), step)
                hidden(par, e, count)
                lows((k + 2, k + 3), step)
                hidden_low(par, count)
                lows((k + 4, k + 5), step)

            same = lambda n: n
            lows(range(4), same)
            expert(4, 0, slice(0, 1), 1, same)
            with dve.Fori(0, 7) as it:
                for j in range(4):
                    expert(10 + 6 * j, (1 + j) % 2, bass.ds(it * 4 + (1 + j), 1), it * 4 + (2 + j),
                           lambda n: it * 48 + n)
            for e in (30, 31):
                expert(6 * e - 2, (e - 1) % 2, slice(e - 1, e), e, same)
            hidden(1, slice(NE - 1, NE), NE)
            lows((6 * NE - 2, 6 * NE - 1), same)
            hidden_low(1, NE)
            update_dve(dve, "e_y", mod(112 + 40))

        def peer_pool(pool, l):
            n, base = f"p{l}", SO[f"peer{l}_u"][0]
            with pool.Fori(0, NK // 4) as it:
                for k in range(4):
                    for j in range(2):
                        half = 2 * k + j
                        pool.wait_ge(sem(f"{n}_high"), it * 8 + (half + 1))
                        w = w_parts[half % HALVES]
                        pool.tensor_tensor(w[:, 1, :], ring[(base + k) % RING][:, j * 512:(j + 1) * 512],
                                           w[:, 0, :].bitcast(F32), ALU.subtract).then_inc(sem(f"{n}_low"), 1)
            for a in range(TT):
                pool.wait_ge(free_sem(f"{n}_rt{a}"), freed(f"{n}_rt{a}"))
            pool.wait_ge(sem(f"{n}_gelu"), NK)
            with pool.Fori(0, T // TURN) as it:
                for k in range(TURN // 4):
                    pool.wait_ge(sem(f"{n}_hot_free"), it * TURN + (4 * k + 4))
                    pool.tensor_tensor(hot2[:, 4 * k:4 * k + 4, :], iota.unsqueeze(1).broadcast_to([P, 4, P]),
                                       route[:, 1, bass.ds(it * TURN + 4 * k, 4)].unsqueeze(2).broadcast_to([P, 4, P]),
                                       ALU.subtract).then_inc(sem(f"{n}_diff"), 1)
            pool.wait_ge(sem(f"{n}_hot_free"), TURN + T)
            pool.sem_inc(sem(f"{n}_part"), 2)
            prods = hT[:, 0:4, :].rearrange("p c t -> p (c t)"), mean[:, :, :].rearrange("p c t -> p (c t)")
            with pool.Fori(0, NK // 8) as it:
                for m in range(4):
                    prod = prods[m % 2]
                    pool.wait_ge(sem(f"{n}_prod"), it * 4 + (m + 1))
                    pool.tensor_tensor(prod[:, 0:512], prod[:, 0:512], prod[:, 512:1024],
                                       ALU.add).then_inc(sem(f"{n}_mod_step"), 1)
                    pool.wait_ge(sem(f"{n}_mod_step"), it * 8 + (2 * m + 1))
                    pool.tensor_tensor(prod[:, 0:256], prod[:, 0:256], prod[:, 256:512],
                                       ALU.add).then_inc(sem(f"{n}_mod_step"), 1)
                    pool.wait_ge(sem(f"{n}_mod_step"), it * 8 + (2 * m + 2))
                    pool.wait_ge(sem(f"{n}_half_free"), it * 16 + (HALVES + 2 * NK + 4 * m - 7))
                    pool.tensor_tensor(hT[:, 4 + m, 0:P], prod[:, 0:P], prod[:, P:2 * P],
                                       ALU.add).then_inc(sem(f"{n}_part"), 1)

        @block.gpsimd
        def _(pool):
            with pool.Fori(0, 40 // RING) as it:
                for s in range(RING):
                    pool.wait_ge(ring_free, it * RING + (RING + s + 1))
                    pool.tensor_tensor(mod_prod[s][:, 0:512], mod_prod[s][:, 0:512], mod_prod[s][:, 512:1024],
                                       ALU.add).then_inc(sem("mod_part"), 1)
            pool.wait_ge(sem("loaded"), 16 * N_LOADS)
            peer_pool(pool, 0)
            peer_pool(pool, 1)

        @block.vector
        def _(dve):
            dve.wait_ge(sem("loaded"), 16 * N_LOADS)
            mod_dve(dve)
            norm_dve(dve, "0a", gain[:, 0, :], mod(0))
            rope_dve(dve)
            gla_dve(dve)
            norm_dve(dve, "0b", gain[:, 1, :], mod(24))
            peer_dve(dve, 0)
            norm_dve(dve, "kv", gain[:, 4, :], mod(48))
            swa_dve(dve)
            norm_dve(dve, "1b", gain[:, 3, :], mod(88))
            peer_dve(dve, 1)
            norm_dve(dve, "mid", V("fing"), None, xT)
            norm_dve(dve, "2a", gain[:, 5, :], mod(112))
            mix_dve(dve)
            norm_dve(dve, "2b", gain[:, 6, :], mod(136))
            moe_dve(dve)
            norm_dve(dve, "out", V("fin2"), None, None)


def slots_out_features(w, tiles=None):
    k, m = w.shape
    return w.reshape(k // P, P, m // P, P).transpose(2, 1, 0, 3).reshape(m // P, P, k)


def slots_tokens(w):
    k, m = w.shape
    return w.reshape(k // 256, 2, P, m // 512, 512).transpose(3, 0, 2, 1, 4).reshape(-1, P, CH)


def pad(a):
    out = np.zeros((a.shape[0], P, CH), np.float32)
    out[:, :, :a.shape[2]] = a
    return out


def layout(x):
    S = {}
    mods = [x["mod_w"][0], x["kv_mod_w"], x["mod_w"][1], x["w_ada_2"][0]]
    mods = np.concatenate([slots_out_features(w) for w in mods] + [np.zeros((8, P, CH), np.float32)])
    S["mod"] = mods[:40]
    w = x["gla_w_in"][0]
    gl = np.zeros((D, P), np.float32)
    gl[:, :RANK] = w[:, 3072:3088]
    S["gla_gl"] = slots_out_features(gl)
    S["gla_q"], S["gla_k"] = slots_out_features(w[:, 0:512]), slots_out_features(w[:, 512:1024])
    S["gla_v"], S["gla_og"] = slots_tokens(w[:, 1024:2048]), slots_out_features(w[:, 2048:3072])
    S["gla_out"] = slots_out_features(x["gla_w_out"][0])
    for l in range(2):
        S[f"peer{l}_q"] = slots_out_features(x["peer_w_q"][l])
        S[f"peer{l}_u"] = x["peer_u"][l].reshape(NK, P, DC, P).transpose(0, 3, 2, 1).reshape(NK, P, CH)
        v = np.empty((NK // 2, 3, P, CH), np.float32)
        v[:, :2] = x["peer_v"][l].reshape(NK // 2, 2, P, CH)
        v[:, 2] = mods[40 + 64 * l:104 + 64 * l]
        S[f"peer{l}_v"] = v.reshape(-1, P, CH)
    w = x["kv_w"].reshape(D, 2, SKV, 1, SHD)
    w = np.broadcast_to(w, (D, 2, SKV, 2, SHD))
    S["kv_k"], S["kv_v"] = slots_out_features(w[:, 0].reshape(D, 512)), slots_tokens(w[:, 1].reshape(D, 512))
    S["swa_q"], S["swa_out"] = slots_out_features(x["swa_w_q"][0]), slots_out_features(x["swa_w_out"][0])
    w = x["w_in_2"][0]
    S["ret_q"], S["ret_k"] = slots_out_features(w[:, 0:1024]), slots_out_features(w[:, 1024:2048])
    S["ret_v"], S["ret_g"] = slots_tokens(w[:, 2048:3072]), slots_out_features(w[:, 3072:4096])
    S["mla_cq"], S["mla_ckv"] = slots_out_features(w[:, 4096:4480]), slots_out_features(w[:, 4480:4736])
    S["mla_kpe"] = slots_out_features(np.concatenate([w[:, 4736:4800]] * 2, 1))
    S["gate_r"], S["gate_m"] = slots_out_features(w[:, 4800:5824]), slots_out_features(w[:, 5824:6848])
    S["ret_o"], S["mla_o"] = slots_out_features(x["w_ret_o_2"][0]), slots_out_features(x["w_mla_o_2"][0])
    S["mix_out"] = slots_out_features(x["w_out_2"][0])
    w = x["w_uq_2"][0].reshape(QL, MH, 192)
    w = np.concatenate([w[:, :, :P].reshape(QL, -1), w[:, :, P:].reshape(QL, -1)], 1)
    S["mla_uq"] = pad(slots_out_features(w).reshape(6, 2, P, QL).transpose(0, 2, 1, 3).reshape(6, P, 2 * QL))
    w = x["w_ukv_2"][0].reshape(KVL, MH, 2, P)
    S["mla_uk"] = slots_out_features(w[:, :, 0].reshape(KVL, D)).reshape(2, 4, P, KVL).transpose(0, 2, 1, 3)\
        .reshape(2, P, CH)
    S["mla_uv"] = w[:, :, 1].reshape(2, P, 2, 512).transpose(2, 1, 0, 3).reshape(2, P, CH)
    r = np.zeros((D, P), np.float32)
    r[:, :NG], r[:, NG:NG + NE] = x["w_grp_2"][0], x["w_exp_2"][0]
    S["router"] = slots_out_features(r)
    w1 = x["w1_2"][0].reshape(NE, DC, P, 2, P).transpose(0, 3, 2, 1, 4).reshape(NE, 2, P, CH)
    w3 = x["w3_2"][0].reshape(NE, DC, P, 2, P).transpose(0, 3, 2, 1, 4).reshape(NE, 2, P, CH)
    w2 = x["w2_2"][0].reshape(NE, 2, P, CH)
    parts = [w1[0], w3[0]]
    for e in range(1, NE):
        parts += [w1[e], w3[e], w2[e - 1]]
    S["moe"] = np.concatenate(parts + [w2[NE - 1]])
    stream = np.empty((N_SLOTS, P, CH), np.float32)
    for name, n in STREAM:
        stream[SO[name][0]:SO[name][1]] = S.pop(name)

    def cols(*a):
        return np.concatenate([np.ascontiguousarray(v).reshape(-1, P).T for v in a], 1)

    rows = lambda v: np.broadcast_to(v.reshape(1, -1), (P, v.size))
    V = {"mod_b": cols(x["mod_b"][0], x["kv_mod_b"], x["mod_b"][1], x["b_ada_2"]), "ng0a": cols(x["norm_g"][0, 0]),
         "ng0b": cols(x["norm_g"][0, 1]), "ng1a": cols(x["norm_g"][1, 0]), "ng1b": cols(x["norm_g"][1, 1]),
         "kvg": cols(x["kv_norm_g"]), "fing": cols(x["final_norm_g"]), "n1": cols(x["norm1_2"]),
         "n2": cols(x["norm2_2"]), "fin2": cols(x["final_norm_2"]), "gla_b": cols(x["gla_b_g2"]),
         "gla_ng": cols(x["gla_norm_g"]), "qn": cols(x["q_norm_2"]), "kvn": cols(x["kv_norm_2"]),
         "c": cols(x["c"]), "c2": cols(x["c_2"]), "sinks": rows(x["swa_sinks"]),
         "rb": np.concatenate([rows(x["b_grp_2"]), rows(x["b_exp_2"])], 1)}
    return {
        "stream": stream,
        "vecs": np.ascontiguousarray(np.concatenate([V[n] for n, _ in VECS], 1)),
        "xin": np.ascontiguousarray(x["x"][0].T).reshape(DC, P, T),
        "pos": np.ascontiguousarray(np.broadcast_to(x["positions"].reshape(1, T), (P, T))),
        "wg2": np.ascontiguousarray(x["gla_w_g2"][0]),
        "subk": np.ascontiguousarray(x["peer_subkeys"].reshape(4, NK, P).transpose(2, 0, 1)),
        **shape_constants(),
    }


def kernel(**inputs):
    import concourse.bacc as bacc
    from concourse.bass_utils import run_bass_kernel_spmd

    arrays = layout({k: np.asarray(v) for k, v in inputs.items()})
    nc = bacc.Bacc("TRN2", target_bir_lowering=False, num_devices=1)
    args = [nc.dram_tensor(n, a.shape, mybir.dt.from_np(a.dtype), kind="ExternalInput").ap()
            for n, a in arrays.items()]
    out = nc.dram_tensor("out", (DC, P, T), F32, kind="ExternalOutput").ap()
    block_program(nc, *args, out)
    r = run_bass_kernel_spmd(nc, [arrays], core_ids=[0])
    y = r.results[0]["out"]
    return np.ascontiguousarray(y.reshape(1, D, T).transpose(0, 2, 1))
```
